# Optimizing a Trainium2 kernel written in Bass

```python
import math
import jax, jax.numpy as jnp
from jax import lax
import numpy as np

D_MODEL = 2048
BATCH = 1
SEQ = 256
DEPTH = 1

CHUNK = 64
Q_BLOCK = 128
EPS = 1e-6

GDN_HEADS = 6
GDN_DK = 128
GDN_DV = 128
GDN_CONV = 4
GDN_QK_W = GDN_HEADS * GDN_DK
GDN_V_W = GDN_HEADS * GDN_DV
ML_HEADS = 4
ML_DK = 128
ML_DV = 128
ML_QK_W = ML_HEADS * ML_DK
ML_V_W = ML_HEADS * ML_DV
SB_HEADS = 6
SB_DH = 128
SB_W = SB_HEADS * SB_DH
MEM_LEN = 256
XA_HEADS = 4
XA_DH = D_MODEL // XA_HEADS
D_FF = 5632
FFN_CONV = 3

IN_SIZES = (2 * GDN_QK_W + GDN_V_W,
            GDN_HEADS,
            GDN_HEADS,
            GDN_V_W,
            ML_QK_W, ML_QK_W, ML_V_W,
            ML_HEADS, ML_HEADS,
            ML_V_W,
            SB_W, SB_W, SB_W,
            3 * D_MODEL)
IN_WIDTH = sum(IN_SIZES)
BR_W = GDN_V_W + ML_V_W + SB_W

kernel_name = 'hybrid_gdn_mlstm_stickbreak_streaming_encoder'

def _split_cols(t, sizes):
    idx = np.cumsum(np.array(sizes))[:-1].tolist()
    return jnp.split(t, idx, axis=-1)

def rmsnorm(x, g):
    xf = x.astype(jnp.float32)
    y = xf * lax.rsqrt(jnp.mean(xf * xf, axis=-1, keepdims=True) + EPS)
    return (y * g.astype(jnp.float32)).astype(x.dtype)

def _l2norm(x):
    return x * lax.rsqrt(jnp.sum(x * x, axis=-1, keepdims=True) + EPS)

def causal_dwconv(x, w):
    K, C = w.shape
    return lax.conv_general_dilated(x, w.astype(x.dtype)[:, None, :], window_strides=(1,),
                                    padding=[(K - 1, 0)],
                                    dimension_numbers=('NWC', 'WIO', 'NWC'),
                                    feature_group_count=C)

def _to_chunks(t):
    B_, S_ = t.shape[:2]
    t = t.reshape((B_, S_ // CHUNK, CHUNK) + t.shape[2:])
    if t.ndim == 5:
        return t.transpose(1, 0, 3, 2, 4)
    return t.transpose(1, 0, 3, 2)

def _from_chunks(o):
    n, B_, H, C, d = o.shape
    return o.transpose(1, 0, 3, 2, 4).reshape(B_, n * C, H, d)

def gated_deltanet(q, k, v, g, beta):
    B_, S_, H, dk = q.shape
    dv = v.shape[-1]
    f32 = jnp.float32
    qc = _to_chunks(_l2norm(q.astype(f32)) * (dk ** -0.5))
    kc = _to_chunks(_l2norm(k.astype(f32)))
    vc = _to_chunks(v.astype(f32))
    gc = _to_chunks(g.astype(f32))
    bc = _to_chunks(beta.astype(f32))
    G = jnp.cumsum(gc, axis=-1)
    incl = jnp.tril(jnp.ones((CHUNK, CHUNK), dtype=bool))
    strict = jnp.tril(jnp.ones((CHUNK, CHUNK), dtype=bool), -1)
    decay = jnp.exp(jnp.where(incl, G[..., :, None] - G[..., None, :], -jnp.inf))
    kb = kc * bc[..., None]
    L = jnp.where(strict, jnp.einsum('nbhtd,nbhsd->nbhts', kb, kc) * decay, 0.0)
    eye = jnp.broadcast_to(jnp.eye(CHUNK, dtype=f32), L.shape)
    T = lax.linalg.triangular_solve(L, eye, left_side=True, lower=True, unit_diagonal=True)
    u = jnp.einsum('nbhts,nbhse->nbhte', T, vc * bc[..., None])
    w = jnp.einsum('nbhts,nbhsd->nbhtd', T, kb * jnp.exp(G)[..., None])
    a_intra = jnp.einsum('nbhtd,nbhsd->nbhts', qc, kc) * decay
    q_dec = qc * jnp.exp(G)[..., None]
    k_tail = kc * jnp.exp(G[..., -1:] - G)[..., None]
    g_last = jnp.exp(G[..., -1])

    def step(S, inp):
        u_i, w_i, a_i, qd_i, kt_i, gl_i = inp
        v_new = u_i - jnp.einsum('bhtd,bhde->bhte', w_i, S)
        o = jnp.einsum('bhtd,bhde->bhte', qd_i, S) + jnp.einsum('bhts,bhse->bhte', a_i, v_new)
        S = S * gl_i[..., None, None] + jnp.einsum('bhtd,bhte->bhde', kt_i, v_new)
        return S, o

    S0 = jnp.zeros((B_, H, dk, dv), f32)
    _, o = lax.scan(step, S0, (u, w, a_intra, q_dec, k_tail, g_last))
    return _from_chunks(o)

def mlstm(q, k, v, i_pre, f_pre):
    B_, S_, H, dk = q.shape
    dv = v.shape[-1]
    f32 = jnp.float32
    qc = _to_chunks(q.astype(f32) * (dk ** -0.5))
    kc = _to_chunks(k.astype(f32))
    vc = _to_chunks(v.astype(f32))
    ic = _to_chunks(i_pre.astype(f32))
    lfc = _to_chunks(jax.nn.log_sigmoid(f_pre.astype(f32)))
    b = jnp.cumsum(lfc, axis=-1)
    incl = jnp.tril(jnp.ones((CHUNK, CHUNK), dtype=bool))
    D = jnp.where(incl, b[..., :, None] - b[..., None, :] + ic[..., None, :], -jnp.inf)
    D_max = jnp.max(D, axis=-1)
    s_qk = jnp.einsum('nbhtd,nbhsd->nbhts', qc, kc)
    b_last = b[..., -1]
    a_end = b_last[..., None] - b + ic
    a_max = jnp.max(a_end, axis=-1)

    def step(carry, inp):
        C, nv, m = carry
        q_i, k_i, v_i, b_i, D_i, Dm_i, s_i, bl_i, ae_i, am_i = inp
        inter = b_i + m[..., None]
        m_t = jnp.maximum(inter, Dm_i)
        w_inter = jnp.exp(inter - m_t)
        W = jnp.exp(D_i - m_t[..., None]) * s_i
        num = (w_inter[..., None] * jnp.einsum('bhtd,bhde->bhte', q_i, C)
               + jnp.einsum('bhts,bhse->bhte', W, v_i))
        den = w_inter * jnp.einsum('bhtd,bhd->bht', q_i, nv) + jnp.sum(W, axis=-1)
        h = num / jnp.maximum(jnp.abs(den), jnp.exp(-m_t))[..., None]
        m_new = jnp.maximum(bl_i + m, am_i)
        w_old = jnp.exp(bl_i + m - m_new)
        w_s = jnp.exp(ae_i - m_new[..., None])
        C = w_old[..., None, None] * C + jnp.einsum('bhsd,bhse->bhde', k_i * w_s[..., None], v_i)
        nv = w_old[..., None] * nv + jnp.einsum('bhsd,bhs->bhd', k_i, w_s)
        return (C, nv, m_new), h

    init = (jnp.zeros((B_, H, dk, dv), f32), jnp.zeros((B_, H, dk), f32), jnp.zeros((B_, H), f32))
    _, h = lax.scan(step, init, (qc, kc, vc, b, D, D_max, s_qk, b_last, a_end, a_max))
    return _from_chunks(h)

def stick_breaking(q, k, v):
    B_, S_, H, dh = q.shape
    f32 = jnp.float32
    qh = (q.astype(f32) * (dh ** -0.5)).transpose(0, 2, 1, 3)
    kh = k.astype(f32).transpose(0, 2, 1, 3)
    vh = v.astype(f32).transpose(0, 2, 1, 3)
    outs = []
    for blk in range(S_ // Q_BLOCK):
        t0 = blk * Q_BLOCK
        t1 = t0 + Q_BLOCK
        logits = jnp.einsum('bhtd,bhsd->bhts', qh[:, :, t0:t1], kh[:, :, :t1])
        t_idx = t0 + jnp.arange(Q_BLOCK)
        s_idx = jnp.arange(t1)
        strict = s_idx[None, :] < t_idx[:, None]
        log_beta = jax.nn.log_sigmoid(logits)
        log_stay = jnp.where(strict, jax.nn.log_sigmoid(-logits), 0.0)
        log_surv = lax.cumsum(log_stay, axis=3, reverse=True) - log_stay
        A = jnp.where(strict, jnp.exp(log_beta + log_surv), 0.0)
        outs.append(jnp.einsum('bhts,bhsd->bhtd', A, vh[:, :, :t1]))
    o = jnp.concatenate(outs, axis=2)
    return o.transpose(0, 2, 1, 3)

def hybrid_mixer(h, w_in, conv_w, a_log, dt_bias, gdn_g, ml_bias, ml_g, w_br, w_out):
    B_, S_, _ = h.shape
    f32 = jnp.float32
    dt = h.dtype
    (qkv_a, a_pre, b_pre, z_a, q_b, k_b, v_b, i_b, f_b, o_b,
     q_c, k_c, v_c, gate_pre) = _split_cols(h @ w_in, IN_SIZES)

    def heads(t, n):
        return t.reshape(B_, S_, n, -1)

    qkv_a = jax.nn.silu(causal_dwconv(qkv_a, conv_w))
    q_a, k_a, v_a = _split_cols(qkv_a, (GDN_QK_W, GDN_QK_W, GDN_V_W))
    g_a = -jnp.exp(a_log.astype(f32)) * jax.nn.softplus(a_pre.astype(f32) + dt_bias.astype(f32))
    beta_a = jax.nn.sigmoid(b_pre.astype(f32))
    y_a = gated_deltanet(heads(q_a, GDN_HEADS), heads(k_a, GDN_HEADS), heads(v_a, GDN_HEADS), g_a, beta_a)
    y_a = rmsnorm(y_a, gdn_g) * jax.nn.silu(heads(z_a, GDN_HEADS).astype(f32))
    y_a = y_a.reshape(B_, S_, GDN_V_W).astype(dt)

    y_b = mlstm(heads(q_b, ML_HEADS), heads(k_b, ML_HEADS), heads(v_b, ML_HEADS),
                i_b + ml_bias[0], f_b + ml_bias[1])
    y_b = rmsnorm(y_b, ml_g) * jax.nn.sigmoid(heads(o_b, ML_HEADS).astype(f32))
    y_b = y_b.reshape(B_, S_, ML_V_W).astype(dt)

    y_c = stick_breaking(heads(q_c, SB_HEADS), heads(k_c, SB_HEADS), heads(v_c, SB_HEADS))
    y_c = y_c.reshape(B_, S_, SB_W).astype(dt)

    gate_a, gate_b, gate_c = jnp.split(jax.nn.sigmoid(gate_pre), 3, axis=-1)
    wb_a, wb_b, wb_c = jnp.split(w_br, [GDN_V_W, GDN_V_W + ML_V_W], axis=0)
    merged = gate_a * (y_a @ wb_a) + gate_b * (y_b @ wb_b) + gate_c * (y_c @ wb_c)
    return merged @ w_out

def memory_cross_attention(h, m, wq, wkv, wo, gq, gk):
    B_, S_, _ = h.shape
    M_ = m.shape[1]
    q = rmsnorm((h @ wq).reshape(B_, S_, XA_HEADS, XA_DH), gq)
    k, v = jnp.split(m @ wkv, 2, axis=-1)
    k = rmsnorm(k.reshape(B_, M_, XA_HEADS, XA_DH), gk)
    v = v.reshape(B_, M_, XA_HEADS, XA_DH)
    logits = jnp.einsum('bshd,bmhd->bhsm', q.astype(jnp.float32), k.astype(jnp.float32)) * (XA_DH ** -0.5)
    p = jax.nn.softmax(logits, axis=-1).astype(v.dtype)
    o = jnp.einsum('bhsm,bmhd->bshd', p, v).reshape(B_, S_, D_MODEL)
    return o @ wo

def conv_glu_ffn(h, w_up, w_conv, w_down):
    up = causal_dwconv(h @ w_up, w_conv)
    g, u = jnp.split(up, 2, axis=-1)
    return (jax.nn.silu(g) * u) @ w_down

def setup_inputs(seed: int = 0) -> dict:
    key = jax.random.key(seed)
    ks = jax.random.split(key, 26)
    f32 = jnp.float32

    def dense(k, fan_in, fan_out):
        return jax.random.normal(k, (DEPTH, fan_in, fan_out), f32) * (fan_in ** -0.5)

    def gain(k, n):
        return 1.0 + 0.02 * jax.random.normal(k, (DEPTH, n), f32)

    x = jax.random.normal(ks[0], (BATCH, SEQ, D_MODEL), f32)
    mem = jax.random.normal(ks[1], (BATCH, MEM_LEN, D_MODEL), f32)
    gdn_a_log = jnp.log(jax.random.uniform(ks[4], (DEPTH, GDN_HEADS), f32, 1.0, 16.0))
    dt0 = jnp.exp(jax.random.uniform(ks[5], (DEPTH, GDN_HEADS), f32, math.log(1e-3), math.log(1e-1)))
    gdn_dt_bias = dt0 + jnp.log(-jnp.expm1(-dt0))
    i_bias = 0.1 * jax.random.normal(ks[7], (DEPTH, ML_HEADS), f32)
    f_bias = jnp.linspace(3.0, 6.0, ML_HEADS, dtype=f32) + 0.1 * jax.random.normal(ks[8], (DEPTH, ML_HEADS), f32)
    ml_gate_bias = jnp.stack([i_bias, f_bias], axis=1)[..., None, None, :] if False else jnp.stack([i_bias, f_bias], axis=1)
    return {
        'x': x,
        'mem': mem,
        'norm_mix': gain(ks[2], D_MODEL),
        'w_in': dense(ks[3], D_MODEL, IN_WIDTH),
        'gdn_conv': jax.random.normal(ks[6], (DEPTH, GDN_CONV, 2 * GDN_QK_W + GDN_V_W), f32) * (GDN_CONV ** -0.5),
        'gdn_a_log': gdn_a_log,
        'gdn_dt_bias': gdn_dt_bias,
        'gdn_norm': gain(ks[9], GDN_DV),
        'ml_gate_bias': ml_gate_bias,
        'ml_norm': gain(ks[10], ML_DV),
        'w_br': dense(ks[11], BR_W, D_MODEL),
        'w_out': dense(ks[12], D_MODEL, D_MODEL),
        'norm_xa': gain(ks[13], D_MODEL),
        'norm_mem': gain(ks[14], D_MODEL),
        'xa_wq': dense(ks[15], D_MODEL, D_MODEL),
        'xa_wkv': dense(ks[16], D_MODEL, 2 * D_MODEL),
        'xa_wo': dense(ks[17], D_MODEL, D_MODEL),
        'xa_qnorm': gain(ks[18], XA_DH),
        'xa_knorm': gain(ks[19], XA_DH),
        'norm_ffn': gain(ks[20], D_MODEL),
        'ffn_up': dense(ks[21], D_MODEL, 2 * D_FF),
        'ffn_conv': jax.random.normal(ks[22], (DEPTH, FFN_CONV, 2 * D_FF), f32) * (FFN_CONV ** -0.5),
        'ffn_down': dense(ks[23], D_FF, D_MODEL),
    }

def reference(x, mem, norm_mix, w_in, gdn_conv, gdn_a_log, gdn_dt_bias, gdn_norm, ml_gate_bias,
              ml_norm, w_br, w_out, norm_xa, norm_mem, xa_wq, xa_wkv, xa_wo, xa_qnorm, xa_knorm,
              norm_ffn, ffn_up, ffn_conv, ffn_down):
    for l in range(DEPTH):
        x = x + hybrid_mixer(rmsnorm(x, norm_mix[l]), w_in[l], gdn_conv[l], gdn_a_log[l],
                             gdn_dt_bias[l], gdn_norm[l], ml_gate_bias[l], ml_norm[l],
                             w_br[l], w_out[l])
        x = x + memory_cross_attention(rmsnorm(x, norm_xa[l]), rmsnorm(mem, norm_mem[l]),
                                       xa_wq[l], xa_wkv[l], xa_wo[l], xa_qnorm[l], xa_knorm[l])
        x = x + conv_glu_ffn(rmsnorm(x, norm_ffn[l]), ffn_up[l], ffn_conv[l], ffn_down[l])
    return x


_drawn_inputs = setup_inputs


def setup_inputs(seed=0):
    import zlib

    import numpy as np

    out = dict(_drawn_inputs(seed))
    spreads = {}
    factors = {'norm_mix': 4.906,
     'gdn_norm': 8.0,
     'ml_norm': 28.668,
     'norm_xa': 8.0,
     'norm_mem': 8.0,
     'xa_qnorm': 8.0,
     'xa_knorm': 8.0,
     'norm_ffn': 12.612}
    for name, (base, spread) in spreads.items():
        noise = np.random.default_rng([zlib.crc32(name.encode()), seed]).standard_normal(out[name].shape)
        drawn = base * np.exp(spread * noise) if base else spread * noise
        out[name] = __import__('jax').numpy.asarray(drawn.astype(out[name].dtype))
    for name, factor in factors.items():
        out[name] = (out[name] * factor).astype(out[name].dtype)
    return out
```

```python
import math
from contextlib import ExitStack

import numpy as np
import concourse.bass as bass
from concourse import mybir

P = 128
SEQ, D = 256, 2048
TT = SEQ // P
KC = D // P
GH, MH, SH = 6, 4, 6
DK = 128
XH = 4
XD = D // XH
XC = XD // P
FF = 5632
FC = FF // P
CW = 256
GDN_TAPS, FFN_TAPS = 4, 3
EPS = 1e-6
BIG = 1e30

C_A = 0
C_AB = C_A + 3 * GH * DK
C_Z = C_AB + 2 * GH
C_QKB = C_Z + GH * DK
C_VB = C_QKB + 2 * MH * DK
C_IF = C_VB + MH * DK
C_O = C_IF + 2 * MH
C_QKC = C_O + MH * DK
C_VC = C_QKC + 2 * SH * DK
C_G = C_VC + SH * DK

FM, TM_, BR, DOWN = "feature-major", "token-major", "branches", "down"
DG = 11
NDG = FC // DG
STREAM = [
    ("A", "w_in", C_A, 9, FM), ("Z", "w_in", C_Z, 3, FM),
    ("BQK", "w_in", C_QKB, 4, FM), ("BV", "w_in", C_VB, 2, TM_), ("BO", "w_in", C_O, 2, FM),
    ("CQK", "w_in", C_QKC, 6, FM), ("CV", "w_in", C_VC, 3, TM_), ("G", "w_in", C_G, 24, FM),
    ("BR", "w_br", 0, 8, BR), ("WO", "w_out", 0, 8, FM),
    ("K", "xa_wkv", 0, 8, FM), ("V", "xa_wkv", D, 8, TM_), ("Q", "xa_wq", 0, 8, FM),
    ("XO", "xa_wo", 0, 8, FM), ("UP", "ffn_up", 0, 2 * FC // 2, FM), ("DN", "ffn_down", 0, 8 * NDG, DOWN),
]
FIRST, COUNT = {}, {}
_u = 0
for _n, _w, _c, _k, _kind in STREAM:
    FIRST[_n], COUNT[_n] = _u, _k
    _u += _k
UNITS = _u
EVAC = {n: "act" for n in ("A", "Z", "BQK", "BV", "BO", "CQK", "CV", "G", "K", "V", "Q")}
EVAC.update({n: "dve" for n in ("BR", "WO", "XO", "UP", "DN")})


def slot_of(name, k):
    return (FIRST[name] + k) % 2, (FIRST[name] + k) // 2


def last_unit(name):
    return FIRST[name] + COUNT[name] - 1


def evacuated(name, i):
    engine, n = EVAC[name], 0
    for m, _, _, k, kind in STREAM:
        per = NDG if kind == DOWN else 1
        if m == name:
            return engine, n + i // per + 1
        if EVAC[m] == engine:
            n += k // per
    raise ValueError(name)


def phase_of(u):
    for n, _, _, k, _ in STREAM:
        if FIRST[n] <= u < FIRST[n] + k:
            return n
    raise ValueError(u)


def shape_masks():
    r, c = np.arange(P)[:, None], np.arange(P)[None, :]
    ident = (r == c)
    levels = [((r >> (l + 1)) == (c >> (l + 1))) & ((r >> l) % 2 == 1) & ((c >> l) % 2 == 0) for l in range(7)]
    upper = r <= c
    later = r >= c
    t = np.arange(SEQ)[None, :]
    strict = np.concatenate([r < t, r < c], 1)
    incl = np.concatenate([r <= t, r <= c], 1)
    return np.concatenate([ident, upper, later] + levels + [np.where(strict, 0, -BIG), np.where(incl, 0, BIG)],
                          1).astype(np.float32)


def build_program(nc, T, out):
    f32, f32r = mybir.dt.float32, mybir.dt.float32r
    ALU, ACT, AX = mybir.AluOpType, mybir.ActivationFunctionType, mybir.AxisListType
    ctx = ExitStack()
    with ctx:
        def sb(name, shape, dt=f32, stack=ctx):
            return stack.enter_context(nc.sbuf_tensor(name, shape, dt))

        def sem(name):
            return ctx.enter_context(nc.semaphore(name))

        raw = sb("raw", [P, 2, KC * CW])
        w_hi = sb("w_hi", [P, 2, KC * P], f32r)
        w_lo = sb("w_lo", [P, 2, KC * P], f32r)
        e_scope = ExitStack()
        x_back = sb("x_back", [P, KC, SEQ], f32, e_scope)
        o_tm = sb("o_tm", [P, TT, D], f32, e_scope)
        e_scope.close()
        x_hl = sb("x_hl", [P, 2, KC, SEQ], f32r)
        tmp = sb("tmp", [P, 2, 1024])
        ident = sb("ident", [P, P])
        upper = sb("upper", [P, P])
        later = sb("later", [P, P])
        ones = sb("ones", [P, P])
        rstd = sb("rstd", [P, SEQ])
        vec1 = sb("vec1", [P, 74])
        vec2 = sb("vec2", [P, GDN_TAPS, 18])
        vec3 = sb("vec3", [P, FFN_TAPS, 2 * FC])
        cols = sb("cols", [P, TT, P])
        colm = sb("colm", [P, TT, MH])
        small = sb("small", [P, 128])
        r_scope = ExitStack()
        xT = sb("xT", [P, KC, SEQ], f32, r_scope)
        yT = xT

        a_scope = ExitStack()
        A = lambda name, shape, dt=f32: sb(name, shape, dt, a_scope)
        proj = A("proj", [P, 24, SEQ])
        conv = A("conv", [P, 18, SEQ])
        lev = A("lev", [P, 7, P])
        rt = A("rt", [P, SEQ])
        rt2 = A("rt2", [MH, SEQ])
        g_row = A("g_row", [GH, SEQ])
        m_row = A("m_row", [MH, SEQ])
        s_scope = ExitStack()
        slab = sb("slab", [P, 5, 12, P], f32, s_scope)
        s_scope.close()
        w_scope = ExitStack()
        gw = sb("gw", [P, KC, P], f32, w_scope)
        gw_hi = sb("gw_hi", [P, KC, P], f32r, w_scope)
        gw_lo = sb("gw_lo", [P, KC, P], f32r, w_scope)
        vecs = sb("vecs", [P, 5, P], f32, w_scope)
        w_scope.close()
        a_scope.close()
        b_scope = ExitStack()
        gates = sb("gates", [P, 3 * KC, SEQ], f32, b_scope)
        m_hl = sb("m_hl", [P, 2, KC, SEQ], f32r, b_scope)
        b_scope.close()
        c_scope = ExitStack()
        mem_hl = sb("mem_hl", [P, 2, KC, SEQ], f32r, c_scope)
        kT = sb("kT", [P, KC, SEQ], f32, c_scope)
        v_tm = sb("v_tm", [P, TT, D], f32, c_scope)
        qT = sb("qT", [P, KC, SEQ], f32, c_scope)
        c_scope.close()
        c2_scope = ExitStack()
        prob = sb("prob", [P, TT, XH, SEQ], f32, c2_scope)
        probT = sb("probT", [P, TT, XH, SEQ], f32, c2_scope)
        c2_scope.close()
        r_scope.close()
        d_scope = ExitStack()
        act_hl = sb("act_hl", [P, 2, FC, SEQ], f32r, d_scope)
        d_scope.close()

        bank = [ctx.enter_context(nc.psum_tensor(f"bank{i}", [P, 512], f32)) for i in range(8)]

        x_tm = proj[:, 0:16, :].rearrange("p (a c) s -> p a (c s)", a=TT)
        mem_tm = gates[:, 16:32, :].rearrange("p (a c) s -> p a (c s)", a=TT)
        memT = gates[:, 32:48, :]
        tm = proj[:, 0:18, :].rearrange("p (a s) (b d) -> p a (s b) d", a=TT, d=P)
        zs = proj[:, 18:24, :]
        qk_b, o_b, qk_c = proj[:, 0:8, :], proj[:, 8:12, :], proj[:, 12:24, :]
        convf = conv[:, :, :].rearrange("p a b -> p (a b)")
        v_b = convf[:, 0:TT * MH * 129].rearrange("p (a h d) -> p a h d", a=TT, h=MH)
        num = convf[:, 1032:2064].rearrange("p (a h d) -> p a h d", a=TT, h=MH)
        v_c = convf[:, 2064:3600].rearrange("p (a n) -> p a n", a=TT)
        slabf = slab[:, :, :, :].rearrange("p a b c -> p (a b c)")
        S_L, S_C, S_Z, S_T, S_U = (slab[:, i, :, :] for i in range(5))
        ml_x = slabf[:, 0:1536].rearrange("p (h n) -> p h n", h=MH)
        sb_z = slabf[:, 1536:3840].rearrange("p (h n) -> p h n", h=SH)
        sb_s = slabf[:, 3840:6144].rearrange("p (h n) -> p h n", h=SH)
        neg_mask, pos_mask = slabf[:, 6144:6528], slabf[:, 6528:6912]
        x_spill = nc.dram_tensor("x_spill", [P, KC * SEQ], f32).ap()

        ss = small[:, 0:24]
        eg, tail, beg = small[:, 24:36], small[:, 36:48], small[:, 48:54]
        nalog, dtb = small[0:GH, 54:55], small[0:GH, 55:56]
        ib, fb = small[0:MH, 56:57], small[0:MH, 57:58]
        den, emn = small[:, 60:68], small[:, 68:76]
        xss, xmx, xsum = small[:, 76:84], small[:, 84:92], small[:, 92:100]
        gqk = small[:, 100:104]

        g_mix, g_xa, g_mem, g_ffn = (vec1[:, 16 * i:16 * i + 16] for i in range(4))
        gq, gk = vec1[:, 64:68], vec1[:, 68:72]
        g_gdn, g_ml = vec1[:, 72:73], vec1[:, 73:74]

        raw_full = [sem("raw_full0"), sem("raw_full1")]
        hi_ready = sem("hi_ready")
        lo_ready = sem("lo_ready")
        half_used = sem("half_used")
        act_evac, dve_evac = sem("act_evac"), sem("dve_evac")
        evac = {"act": act_evac, "dve": dve_evac}
        x_in, mem_in, const_in, lev_in, mask_in = (sem(n) for n in ("x_in", "mem_in", "const_in", "lev_in", "mask_in"))
        vec_in, gw_zero, gw_in, spill, back, stored = (sem(n) for n in ("vec_in", "gw_zero", "gw_in", "spill", "back", "stored"))
        tin_t, tin_e = sem("tin_t"), sem("tin_e")
        vec_t, vec_e = sem("vec_t"), sem("vec_e")
        n_sq, n_ss, n_stat, n_rt, n_n, n_hi, n_lo = (sem("norm_" + n) for n in ("sq", "ss", "stat", "rt", "n", "hi", "lo"))
        set_up = sem("set_up")
        gw_h, gw_l, row_mm, row_v, row_a, row_t, col_e, col_a = (sem(n) for n in (
            "gw_h", "gw_l", "row_mm", "row_v", "row_a", "row_t", "col_e", "col_a"))
        cv, cs, tm_t, tm_ea, tm_ed, l2_v, l2_a, qk_t, qk_e, kv_v, qd_t, qd_e = (sem(n) for n in (
            "conv_v", "conv_silu", "tm_t", "tm_ea", "tm_ed", "l2_v", "l2_a", "qk_t", "qk_e", "kv_v", "qd_t", "qd_e"))
        dec_t, dec_v, dec_a, kk_t, l_v, z_t, z_e, d_t, d_e, c_v = (sem("gdn_" + n) for n in (
            "dec_t", "dec_v", "dec_a", "kk_t", "l_v", "z_t", "z_e", "d_t", "d_e", "c_v"))
        u_t, u_e, w_t, w_e, s_t, s_e, a_t, a_v, a_a, vn_t, vn_e, o_t, o_e, yn_v, yn_a, y_t, y_e = (sem("gdn_" + n) for n in (
            "u_t", "u_e", "w_t", "w_e", "st_t", "st_e", "at_t", "at_v", "at_a", "vn_t", "vn_e", "o_t", "o_e", "yn_v", "yn_a",
            "y_t", "y_e"))
        ml_s, ml_v, ml_a, ml_n, ml_ne, ml_h, ml_ha, ml_t, ml_y = (sem("ml_" + n) for n in (
            "s", "v", "a", "n", "ne", "h", "ha", "t", "y"))
        ml_w = sem("ml_w")
        sb_t, sb_zv, sb_a, sb_sp, sb_r, sb_x, sb_e, sb_o, sb_y = (sem("sb_" + n) for n in (
            "t", "zv", "a", "sp", "r", "x", "e", "o", "y"))
        y_hi, y_lo, br_c, br_m, m_hi, m_lo = (sem(n) for n in ("y_hi", "y_lo", "br_c", "br_m", "m_hi", "m_lo"))
        xk_s, xk_t, xk_v, xk_a, xq_s, xq_t, xq_v, xq_a = (sem(n) for n in (
            "xk_s", "xk_t", "xk_v", "xk_a", "xq_s", "xq_t", "xq_v", "xq_a"))
        xl_t, xl_v, xl_a, xp_v, xp_t, xp_e, xo_t, xo_h, xo_l = (sem(n) for n in (
            "xl_t", "xl_v", "xl_a", "xp_v", "xp_t", "xp_e", "xo_t", "xo_h", "xo_l"))
        f_c, f_g, f_s, f_p, f_h, f_l = (sem("ffn_" + n) for n in ("c", "g", "s", "p", "h", "l"))
        ot_t, ot_e, dn_e = sem("ot_t"), sem("ot_e"), sem("dn_e")

        block = ctx.enter_context(nc.Block())

        @block.sync
        def _(sp):
            W = {n: T[n][0].rearrange("(k p) n -> p k n", p=P) for n in ("w_in", "w_br", "w_out", "xa_wq", "xa_wkv", "xa_wo", "ffn_up")}
            down = T["ffn_down"][0].rearrange("(g k p) n -> g p k n", p=P, k=DG)

            def load(par, half, src, kc, first=False):
                if not first:
                    sp.wait_ge(lo_ready, half * 4 + (2 * par - 2))
                sp.dma_start(raw[:, par, 0:kc * CW].rearrange("p (k n) -> p k n", n=CW), src).then_inc(raw_full[par], 16)

            def stream(name, between=None):
                u0, n = FIRST[name], COUNT[name]
                _, w, c0, _, kind = next(s for s in STREAM if s[0] == name)
                if name == "UP":
                    with sp.Fori(0, n // 2) as i:
                        for j in range(2):
                            par, h0 = slot_of(name, j)
                            load(par, i + h0, W[w][:, :, bass.ds(i * CW + j * FF, CW)], KC)
                    return
                if name == "DN":
                    with sp.Fori(0, n // NDG) as i:
                        for g in range(NDG):
                            par, h0 = slot_of(name, g)
                            load(par, i * (NDG // 2) + h0, down[g][:, :, bass.ds(i * CW, CW)], DG)
                    return
                i = 0
                while i < n:
                    u = u0 + i
                    pairs = (n - i) // 2
                    if u % 2 == 0 and u >= 2 and pairs > 1:
                        with sp.Fori(0, pairs) as r:
                            for j in range(2):
                                load(j, r + u // 2, W[w][:, :, bass.ds(r * (2 * CW) + (c0 + (i + j) * CW), CW)], KC)
                        i += 2 * pairs
                    else:
                        load(u % 2, u // 2, W[w][:, :, c0 + i * CW:c0 + (i + 1) * CW], KC, first=u < 2)
                        i += 1

            sp.dma_start(x_tm, T["x"][0].rearrange("(a p) d -> p a d", p=P)).then_inc(x_in, 16)
            c = T["shape_masks"]
            sp.dma_start(ident[:, :], c[:, 0:P]).then_inc(const_in, 16)
            sp.dma_start(upper[:, :], c[:, P:2 * P]).then_inc(const_in, 16)
            sp.dma_start(later[:, :], c[:, 2 * P:3 * P]).then_inc(const_in, 16)
            row = 0
            for name, k in (("norm_mix", 16), ("norm_xa", 16), ("norm_mem", 16), ("norm_ffn", 16), ("xa_qnorm", 4),
                            ("xa_knorm", 4), ("gdn_norm", 1), ("ml_norm", 1)):
                sp.dma_start(vecs[row:row + k, 0, :], T[name].rearrange("o (c p) -> (o c) p", p=P)).then_inc(vec_in, 16)
                row += k
            sp.dma_start(vecs[0:72, 1, :], T["gdn_conv"][0].rearrange("t (c p) -> (t c) p", p=P)).then_inc(vec_in, 16)
            sp.dma_start(vecs[0:2 * FC, 2:5, :], T["ffn_conv"][0].rearrange("t (c p) -> c t p", p=P)).then_inc(vec_in, 16)
            sp.dma_start(nalog, T["gdn_a_log"].rearrange("o h -> h o")).then_inc(vec_in, 16)
            sp.dma_start(dtb, T["gdn_dt_bias"].rearrange("o h -> h o")).then_inc(vec_in, 16)
            sp.dma_start(ib, T["ml_gate_bias"][0, 0:1, :].rearrange("o h -> h o")).then_inc(vec_in, 16)
            sp.dma_start(fb, T["ml_gate_bias"][0, 1:2, :].rearrange("o h -> h o")).then_inc(vec_in, 16)
            sp.wait_ge(gw_zero, 1)
            for at, c0, k in ((0, C_AB, GH), (32, C_AB + GH, GH), (64, C_IF, MH), (96, C_IF + MH, MH)):
                sp.dma_start(gw[:, :, at:at + k], W["w_in"][:, :, c0:c0 + k]).then_inc(gw_in, 16)
            sp.dma_start(lev[:, :, :], c[:, 3 * P:10 * P].rearrange("p (l n) -> p l n", l=7)).then_inc(lev_in, 16)
            for name, _, _, _, _ in STREAM:
                stream(name)

        @block.gpsimd
        def _(pool):
            pool.memset(gw[:, :, :], 0.0).then_inc(gw_zero, 1)
            pool.wait_ge(tin_e, 8)
            pool.dma_start(x_spill, xT[:, :, :].rearrange("p c s -> p (c s)")).then_inc(spill, 16)
            pool.wait_ge(y_t, 3)
            c = T["shape_masks"]
            pool.dma_start(neg_mask, c[:, 10 * P:10 * P + 384]).then_inc(mask_in, 16)
            pool.dma_start(pos_mask, c[:, 10 * P + 384:10 * P + 768]).then_inc(mask_in, 16)
            pool.wait_ge(y_lo, 4)
            pool.wait_ge(spill, 16)
            pool.dma_start(xT[:, :, :].rearrange("p c s -> p (c s)"), x_spill).then_inc(back, 16)
            pool.wait_ge(dve_evac, evacuated("BR", 7)[1])
            pool.dma_start(mem_tm, T["mem"][0].rearrange("(a p) d -> p a d", p=P)).then_inc(mem_in, 16)
            pool.wait_ge(dve_evac, evacuated("XO", 7)[1])
            pool.wait_ge(back, 16)
            pool.dma_start(x_spill, xT[:, :, :].rearrange("p c s -> p (c s)")).then_inc(spill, 16)
            pool.wait_ge(half_used, 2 * last_unit("UP") + 2)
            pool.wait_ge(spill, 32)
            pool.dma_start(x_back[:, :, :].rearrange("p c s -> p (c s)"), x_spill).then_inc(back, 16)
            for c in range(D // CW):
                pool.wait_ge(ot_e, c + 1)
                pool.dma_start(out[0].rearrange("(a p) d -> p a d", p=P)[:, :, c * CW:(c + 1) * CW],
                               o_tm[:, :, c * CW:(c + 1) * CW]).then_inc(stored, 16)
            pool.wait_ge(stored, 16 * (D // CW))

        def each_unit(eng, name, fn, start=0, stop=None):
            u0, n = FIRST[name], COUNT[name] if stop is None else stop
            i = start
            while i < n:
                u, pairs = u0 + i, (n - i) // 2
                if u % 2 == 0 and pairs > 1:
                    with eng.Fori(0, pairs) as r:
                        for j in range(2):
                            fn(r * 2 + (i + j), j, r + u // 2)
                    i += 2 * pairs
                else:
                    fn(i, u % 2, u // 2)
                    i += 1

        kind_of = {n: k for n, _, _, _, k in STREAM}

        def halves(tile, kind, half, slot):
            if kind == TM_:
                return tile[:, slot, half * (KC // 2) * CW:(half + 1) * (KC // 2) * CW]
            k = DG if kind == DOWN else KC
            return tile[:, slot, 0:k * CW].rearrange("p (k n) -> p k n", n=CW)[:, :, half * P:(half + 1) * P]

        def split_out(tile, kind, half):
            if kind == TM_:
                return tile[:, half, :]
            k = DG if kind == DOWN else KC
            return tile[:, half, 0:k * P].rearrange("p (k n) -> p k n", n=P)

        def mb(i):
            return bank[4 + i % 4]

        @block.scalar
        def _(act):
            def copy(out_, in_, func=ACT.Copy, **kw):
                return nc.scalar.activation(out_, in_, func, **kw)

            def hi(name, i, par, hp):
                act.wait_ge(raw_full[par], hp * 16 + 16)
                for half in range(2):
                    if not (isinstance(hp, int) and 2 * hp + par == 0):
                        act.wait_ge(half_used, hp * 4 + (2 * par + half - 1))
                    copy(split_out(w_hi, kind_of[name], half), halves(raw, kind_of[name], half, par)).then_inc(hi_ready, 1)

            def first(name):
                hi(name, 0, FIRST[name] % 2, FIRST[name] // 2)

            def evac_unit(name, i, par, hp):
                act.wait_ge(half_used, hp * 4 + (2 * par + 2))
                b = bank[par]
                strips = lambda t: t[:, bass.ds(i * 2, 2), :].rearrange("p c s -> p (c s)")
                if name == "BV":
                    for a in range(TT):
                        last = copy(v_b[:, a, 2 * i:2 * i + 2, 0:DK],
                                    bank[par + 2 * a][:, :].rearrange("p (x h d) -> p x h d", x=2, h=2)[:, 0])
                elif name == "CV":
                    for a in range(TT):
                        last = copy(v_c[:, a, i * CW:(i + 1) * CW], bank[par + 2 * a][:, 0:CW])
                elif name == "V":
                    for a in range(TT):
                        last = copy(v_tm[:, a, bass.ds(i * CW, CW)], bank[par + 2 * a][:, 0:CW])
                else:
                    to, func = {"A": (proj[:, 0:18, :], ACT.Copy), "Z": (zs, ACT.Silu), "BQK": (qk_b, ACT.Copy),
                                "BO": (o_b, ACT.Sigmoid), "CQK": (qk_c, ACT.Copy), "G": (gates, ACT.Sigmoid),
                                "K": (kT, ACT.Copy), "Q": (qT, ACT.Copy)}[name]
                    last = copy(strips(to), b[:, :], func)
                last.then_inc(act_evac, 1)

            def evac_last(name):
                u = last_unit(name)
                evac_unit(name, COUNT[name] - 1, u % 2, u // 2)

            def rest(name, start=1, stop=None):
                def unit(i, par, hp):
                    hi(name, i, par, hp)
                    if EVAC[name] == "act":
                        evac_unit(name, i - 1, 1 - par, hp if par else hp - 1)
                each_unit(act, name, unit, start, stop)

            def transposed(k, to):
                for g in range(8):
                    act.wait_ge(tin_t, 8 * k + g + 1)
                    copy(to[:, 4 * (g % 4):4 * (g % 4) + 4, (g // 4) * P:(g // 4 + 1) * P],
                         mb(g)[:, :].rearrange("p (c s) -> p c s", c=4)).then_inc(tin_e, 1)

            def norm(k, src, gain, dst, own=0):
                if k < 2:
                    act.wait_ge(tin_e, 8 * k + 8)
                else:
                    act.wait_ge(dve_evac, evacuated("WO" if k == 2 else "XO", 7)[1])
                if k == 1:
                    act.wait_ge(m_lo, COUNT["BR"])
                elif k:
                    act.wait_ge(n_lo, 4 * k)
                for c in range(4):
                    if c >= 2:
                        act.wait_ge(n_ss, 4 * k + c - 1)
                    copy(tmp[:, c % 2, :], src[:, 4 * c:4 * c + 4, :].rearrange("p c s -> p (c s)"), ACT.Square).then_inc(n_sq, 1)
                act.wait_ge(n_stat, 2 * k + 1)
                copy(rstd[:, :], rstd[:, :], ACT.Sqrt).then_inc(n_rt, 1)
                for c in range(4):
                    act.wait_ge(n_n, 4 * k + c + 1)
                    for j in range(4):
                        last = copy(dst[:, 0, 4 * c + j, :], tmp[:, c % 2, j * SEQ:(j + 1) * SEQ], scale=gain[:, 4 * c + j:4 * c + j + 1])
                    last.then_inc(n_hi, 1)

            transposed(0, xT)
            first("A")
            act.wait_ge(set_up, 2)
            norm(0, xT, g_mix, x_hl)
            act.wait_ge(gw_in, 64)
            copy(gw_hi[:, :, :], gw[:, :, :]).then_inc(gw_h, 1)
            rest("A")
            first("Z")
            evac_last("A")
            rest("Z")
            first("BQK")
            evac_last("Z")

            ra, rb, ri, rf, t0, t1 = (tmp[0:GH if j < 2 or j == 4 else MH, j // 4, (j % 4) * SEQ:(j % 4 + 1) * SEQ] for j in range(6))
            act.wait_ge(row_v, 4)
            copy(rb, rb, ACT.Sigmoid).then_inc(row_a, 1)
            nc.scalar.preload_act_table_set("natural_log_exp_and_others")
            copy(t0, ra, ACT.Abs).then_inc(row_a, 1)
            copy(t1, rf, ACT.Abs).then_inc(row_a, 1)
            act.wait_ge(row_a, 3)
            copy(t0, t0, ACT.Exp, scale=-1.0).then_inc(row_a, 1)
            copy(t1, t1, ACT.Exp, scale=-1.0).then_inc(row_a, 1)
            copy(nalog, nalog, ACT.Exp).then_inc(row_a, 1)
            act.wait_ge(row_a, 6)
            copy(t0, t0, ACT.Ln, bias=1.0).then_inc(row_a, 1)
            copy(t1, t1, ACT.Ln, bias=1.0).then_inc(row_a, 1)
            act.wait_ge(col_e, 2)
            copy(eg.rearrange("p (a h) -> p a h", a=TT), cols[:, :, 32:32 + GH], ACT.Exp).then_inc(col_a, 1)
            copy(tail.rearrange("p (a h) -> p a h", a=TT), cols[:, :, 64:64 + GH], ACT.Exp).then_inc(col_a, 1)
            copy(emn.rearrange("p (a h) -> p a h", a=TT), colm[:, :, :], ACT.Exp, scale=-1.0).then_inc(col_a, 1)

            nc.scalar.preload_act_table_set("silu_and_others")
            for j in range(3):
                act.wait_ge(cv, 24 * (j + 1))
                copy(conv[:, 6 * j:6 * j + 6, :], conv[:, 6 * j:6 * j + 6, :], ACT.Silu).then_inc(cs, 1)
            for g in range(0, 9, 2):
                act.wait_ge(tm_t, g + 1)
                copy(tm[:, :, 2 * g:2 * g + 2, :].rearrange("p a c d -> p c a d"),
                     mb(g)[:, :].rearrange("p (c a d) -> p c a d", c=2, a=TT)).then_inc(tm_ea, 1)
            act.wait_ge(l2_v, 3)
            copy(ss, ss, ACT.Sqrt).then_inc(l2_a, 1)
            nc.scalar.preload_act_table_set("natural_log_exp_and_others")
            for g in range(6):
                act.wait_ge(qk_t, g + 1)
                copy(conv[:, 2 * g:2 * g + 2, :].rearrange("p c s -> p (c s)"), mb(g)[:, :]).then_inc(qk_e, 1)
            act.wait_ge(dec_v, 12)
            copy(S_L, S_L, ACT.Exp, scale=-1.0).then_inc(dec_a, 1)
            for l in range(7):
                for g in range(3):
                    act.wait_ge(z_t, 3 * l + g + 1)
                    if l and g == 0:
                        act.wait_ge(d_t, 6 * l)
                    copy(S_Z[:, 4 * g:4 * g + 4, :].rearrange("p c s -> p (c s)"), bank[4 + g % 2][:, :]).then_inc(z_e, 1)
            for g in range(2):
                act.wait_ge(w_t, g + 1)
                k = 4 if g == 0 else 2
                nc.scalar.mul(S_Z[:, 4 * g:4 * g + k, :].rearrange("p c s -> p (c s)"), bank[6 + g][:, 0:k * P], -1.0).then_inc(w_e, 1)
            for g in range(2):
                act.wait_ge(s_t, g + 1)
                k = 4 if g == 0 else 2
                copy(S_Z[:, 6 + 4 * g:6 + 4 * g + k, :].rearrange("p c s -> p (c s)"), bank[4 + g][:, 0:k * P]).then_inc(s_e, 1)
            for g in range(2):
                act.wait_ge(qd_t, g + 1)
                k = 4 if g == 0 else 2
                copy(tm[:, 0, 4 * g:4 * g + k, :], bank[6 + g][:, 0:k * P].rearrange("p (c d) -> p c d", d=P)).then_inc(qd_e, 1)
            act.wait_ge(a_v, 12)
            copy(S_L, S_L, ACT.Exp).then_inc(a_a, 1)
            for g in range(3):
                act.wait_ge(o_t, g + 1)
                copy(S_T[:, 4 * g:4 * g + 4, :].rearrange("p c s -> p (c s)"), mb(g)[:, :]).then_inc(o_e, 1)
            act.wait_ge(yn_v, 3)
            copy(ss[:, 0:12], ss[:, 0:12], ACT.Sqrt).then_inc(yn_a, 1)

            rest("BQK")
            first("BV")
            evac_last("BQK")
            rest("BV")
            first("BO")
            evac_last("BV")
            rest("BO")
            first("CQK")
            evac_last("BO")
            act.wait_ge(y_e, 3)
            rest("CQK")
            first("CV")
            evac_last("CQK")
            rest("CV")
            first("G")
            evac_last("CV")

            nc.scalar.preload_act_table_set("natural_log_exp_and_others")
            for h in range(MH):
                act.wait_ge(ml_v, 2 * h + 2)
                copy(ml_x[:, h, :], ml_x[:, h, :], ACT.Exp, scale=-1.0).then_inc(ml_a, 1)
            for h in range(MH):
                act.wait_ge(ml_n, h + 1)
                copy(num[:, :, h, :], bank[6 + h % 2][:, 0:258].rearrange("p (a d) -> p a d", a=TT)).then_inc(ml_ne, 1)
            act.wait_ge(ml_h, 7)
            copy(ss[:, 0:8], ss[:, 0:8], ACT.Sqrt).then_inc(ml_ha, 1)

            nc.scalar.preload_act_table_set("natural_log_exp_and_others")
            for h in range(SH):
                act.wait_ge(sb_zv, h + 1)
                copy(sb_s[:, h, :], sb_z[:, h, :], ACT.Abs).then_inc(sb_a, 1)
                act.wait_ge(sb_a, 3 * h + 1)
                copy(sb_s[:, h, :], sb_s[:, h, :], ACT.Exp, scale=-1.0).then_inc(sb_a, 1)
                act.wait_ge(sb_a, 3 * h + 2)
                copy(sb_s[:, h, :], sb_s[:, h, :], ACT.Ln, bias=1.0).then_inc(sb_a, 1)
            for h in range(SH):
                act.wait_ge(sb_x, h + 1)
                copy(sb_z[:, h, :], sb_z[:, h, :], ACT.Exp).then_inc(sb_e, 1)
            for h in range(SH):
                act.wait_ge(sb_o, h + 1)
                copy(yT[:, GH + MH + h, :], bank[6 + h % 2][:, 0:SEQ]).then_inc(sb_y, 1)

            act.wait_ge(ml_y, 2)
            rest("G")
            first("BR")
            evac_last("G")
            act.wait_ge(sb_y, SH)
            for c in range(4):
                copy(x_hl[:, 0, 4 * c:4 * c + 4, :], yT[:, 4 * c:4 * c + 4, :]).then_inc(y_hi, 1)

            def merged_hi(i, par):
                act.wait_ge(br_m, i + 1)
                copy(m_hl[:, 0, bass.ds(i * 2, 2), :].rearrange("p c s -> p (c s)"), tmp[:, par, 0:512]).then_inc(m_hi, 1)

            def br_unit(i, par, hp):
                hi("BR", i, par, hp)
                merged_hi(i - 1, 1 - par)
            each_unit(act, "BR", br_unit, 1)
            first("WO")
            merged_hi(COUNT["BR"] - 1, last_unit("BR") % 2)
            rest("WO", 1, 5)
            transposed(1, memT)
            rest("WO", 5)
            first("K")
            norm(1, memT, g_mem, mem_hl)
            rest("K", 1, 2)
            norm(2, xT, g_xa, x_hl)
            rest("K", 2)
            first("V")
            evac_last("K")
            rest("V", 1, 2)
            act.wait_ge(n_lo, 12)
            act.wait_ge(act_evac, evacuated("K", 7)[1])
            for h in range(XH):
                if h >= 2:
                    act.wait_ge(xk_t, h - 1)
                copy(tmp[:, h % 2, :], kT[:, 4 * h:4 * h + 4, :].rearrange("p c s -> p (c s)"), ACT.Square).then_inc(xk_s, 1)
            for h in range(XH):
                act.wait_ge(xk_v, 3 * h + 1)
                copy(rstd[:, :], rstd[:, :], ACT.Sqrt).then_inc(xk_a, 1)
            rest("V", 2)
            first("Q")
            evac_last("V")
            rest("Q")
            first("XO")
            evac_last("Q")
            act.wait_ge(act_evac, evacuated("Q", 7)[1])
            for h in range(XH):
                if h >= 2:
                    act.wait_ge(xq_t, h - 1)
                copy(tmp[:, h % 2, :], qT[:, 4 * h:4 * h + 4, :].rearrange("p c s -> p (c s)"), ACT.Square).then_inc(xq_s, 1)
            act.wait_ge(xq_v, 1)
            copy(xss, xss, ACT.Sqrt).then_inc(xq_a, 1)
            nc.scalar.preload_act_table_set("natural_log_exp_and_others")
            for j in range(2 * XH):
                h, a = j // 2, j % 2
                act.wait_ge(xl_v, 2 * j + 2)
                copy(prob[:, a, h, :], bank[4 + j % 2][:, 0:SEQ], ACT.Exp, bias=xmx[:, j:j + 1], scale=xss[:, j:j + 1],
                     accum_out=xsum[:, j:j + 1]).then_inc(xl_a, 1)
            for g in range(4):
                act.wait_ge(xp_t, g + 1)
                copy(probT[:, :, g, :], bank[6 + g % 2][:, :].rearrange("p (m s) -> p m s", m=TT)).then_inc(xp_e, 1)
            for c in range(8):
                act.wait_ge(xo_t, c + 1)
                copy(x_hl[:, 0, 2 * c:2 * c + 2, :].rearrange("p c s -> p (c s)"), mb(c)[:, :]).then_inc(xo_h, 1)
            rest("XO")
            first("UP")
            norm(3, xT, g_ffn, x_hl)
            nc.scalar.preload_act_table_set("silu_and_others")

            def silu_gate(j):
                act.wait_ge(dve_evac, j * 2 + evacuated("UP", 0)[1])
                copy(tmp[:, 0, 0:512], tmp[:, 0, 0:512], ACT.Silu).then_inc(f_s, 1)

            def product_hi(j):
                act.wait_ge(f_p, j + 1)
                copy(act_hl[:, 0, bass.ds(j * 2, 2), :].rearrange("p c s -> p (c s)"), tmp[:, 1, 512:1024]).then_inc(f_h, 1)

            (p0, h0), (p1, h1) = slot_of("UP", 0), slot_of("UP", 1)
            hi("UP", 1, p1, h1)
            silu_gate(0)
            act.wait_ge(spill, 32)
            with act.Fori(1, FC // 2) as j:
                hi("UP", 2 * j, p0, j + h0)
                hi("UP", 2 * j + 1, p1, j + h1)
                product_hi(j - 1)
                silu_gate(j)
            first("DN")
            product_hi(FC // 2 - 1)

            for g in range(1, NDG):
                hi("DN", g, *slot_of("DN", g))
            with act.Fori(1, D // CW) as c:
                for g in range(NDG):
                    par, h0 = slot_of("DN", g)
                    hi("DN", g, par, c * (NDG // 2) + h0)
                act.wait_ge(ot_t, c)
                copy(o_tm[:, :, bass.ds((c - 1) * CW, CW)].rearrange("p a (x d) -> p a x d", x=2),
                     bank[6][:, :].rearrange("p (a x d) -> p a x d", a=TT, x=2)).then_inc(ot_e, 1)
            act.wait_ge(ot_t, D // CW)
            copy(o_tm[:, :, D - CW:D].rearrange("p a (x d) -> p a x d", x=2),
                 bank[6][:, :].rearrange("p (a x d) -> p a x d", a=TT, x=2)).then_inc(ot_e, 1)

        class Count:

            def __init__(self, eng, sem_):
                self.eng, self.sem, self.n = eng, sem_, 0

            def __call__(self, ins):
                ins.then_inc(self.sem, 1)
                self.n += 1

            def settle(self, back=0):
                self.eng.wait_ge(self.sem, self.n - back)

        @block.vector
        def _(dve):
            v = nc.vector
            tt = v.tensor_tensor
            bc = lambda t, shape: t.to_broadcast(shape)

            def lo(name, i, par, hp):
                for half in range(2):
                    dve.wait_ge(hi_ready, hp * 4 + (2 * par + half + 1))
                    kind = kind_of[name]
                    tt(split_out(w_lo, kind, half), halves(raw, kind, half, par),
                       split_out(w_hi, kind, half).bitcast(f32), ALU.subtract).then_inc(lo_ready, 1)

            def first(name):
                lo(name, 0, FIRST[name] % 2, FIRST[name] // 2)

            def add_residual(name, i, par, hp):
                dve.wait_ge(half_used, hp * 4 + (2 * par + 2))
                x2 = xT[:, bass.ds(i * 2, 2), :].rearrange("p c s -> p (c s)")
                tt(x2, bank[par][:, :], x2, ALU.add).then_inc(dve_evac, 1)

            def rest(name, start=1, stop=None):
                def unit(i, par, hp):
                    lo(name, i, par, hp)
                    if name in ("WO", "XO"):
                        add_residual(name, i - 1, 1 - par, hp if par else hp - 1)
                each_unit(dve, name, unit, start, stop)

            def norm(k, src, gain, dst):
                dve.wait_ge(n_ss, 4 * k + 4)
                v.tensor_scalar(rstd[:, :], bank[7][:, 0:SEQ], 1.0 / D, EPS, ALU.mult, ALU.add).then_inc(n_stat, 1)
                dve.wait_ge(n_rt, k + 1)
                v.reciprocal(rstd[:, :], rstd[:, :]).then_inc(n_stat, 1)
                dve.wait_ge(n_stat, 2 * k + 2)

                def normed(c):
                    if c >= 2:
                        dve.wait_ge(n_lo, 4 * k + c - 1)
                    tt(tmp[:, c % 2, :].rearrange("p (c s) -> p c s", c=4), src[:, 4 * c:4 * c + 4, :],
                       bc(rstd[:, :].unsqueeze(1), [P, 4, SEQ]), ALU.mult).then_inc(n_n, 1)

                def lower(c):
                    dve.wait_ge(n_hi, 4 * k + c + 1)
                    for j in range(4):
                        last = v.scalar_tensor_tensor(dst[:, 1, 4 * c + j, :], tmp[:, c % 2, j * SEQ:(j + 1) * SEQ],
                                                      gain[:, 4 * c + j:4 * c + j + 1], dst[:, 0, 4 * c + j, :].bitcast(f32),
                                                      ALU.mult, ALU.subtract)
                    last.then_inc(n_lo, 1)

                for c in range(4):
                    normed(c)
                    if c:
                        lower(c - 1)
                lower(3)

            v.memset(ones[:, :], 1.0).then_inc(set_up, 1)
            dve.wait_ge(vec_t, 1)
            v.tensor_copy(vec1[:, :], bank[4][:, 0:74])
            v.tensor_copy(vec2[:, :, :].rearrange("p t c -> p (t c)"), bank[4][:, 74:146])
            v.tensor_copy(vec3[:, :, :].rearrange("p t c -> p (t c)"), bank[4][:, 146:410]).then_inc(set_up, 1)
            first("A")
            dve.wait_ge(set_up, 2)
            norm(0, xT, g_mix, x_hl)
            dve.wait_ge(gw_h, 1)
            tt(gw_lo[:, :, :], gw[:, :, :], gw_hi[:, :, :].bitcast(f32), ALU.subtract).then_inc(gw_l, 1)
            rest("A")
            first("Z")
            rest("Z")
            first("BQK")

            ra, rb, ri, rf, t0, t1, rg, rl = (tmp[0:GH if j in (0, 1, 4, 6) else MH, j // 4, (j % 4) * SEQ:(j % 4 + 1) * SEQ]
                                              for j in range(8))
            rv = Count(dve, row_v)
            dve.wait_ge(row_mm, 1)
            dve.wait_ge(n_lo, 4)
            rv(v.tensor_scalar(ra, bank[4][0:GH, 0:SEQ], dtb, None, ALU.add))
            rv(v.tensor_copy(rb, bank[4][32:32 + GH, 0:SEQ]))
            rv(v.tensor_scalar(ri, bank[4][64:64 + MH, 0:SEQ], ib, None, ALU.add))
            rv(v.tensor_scalar(rf, bank[4][96:96 + MH, 0:SEQ], fb, None, ALU.add))
            rv(v.memset(rt[:, :], 0.0))
            dve.wait_ge(row_a, 8)
            rv.settle()
            rv(v.scalar_tensor_tensor(rg, ra, 0.0, t0, ALU.max, ALU.add))
            rv(v.scalar_tensor_tensor(rl, rf, 0.0, t1, ALU.min, ALU.subtract))
            rv.settle()
            rv(v.tensor_scalar(rg, rg, nalog, -1.0, ALU.mult, ALU.mult))
            rv.settle()
            for a in range(TT):
                sl = slice(a * P, a * P + P)
                rv(v.tensor_tensor_scan(g_row[:, sl], ones[0:GH, :], rg[:, sl], 0.0, ALU.mult, ALU.add))
            rv(v.tensor_tensor_scan(t1[:, 0:P], ones[0:MH, :], rl[:, 0:P], 0.0, ALU.mult, ALU.add))
            rv.settle()
            rv(v.tensor_tensor_scan(t1[:, P:SEQ], ones[0:MH, :], rl[:, P:SEQ], t1[:, P - 1:P], ALU.mult, ALU.add))
            rv.settle()
            rv(tt(ri, ri, t1, ALU.subtract))
            rv.settle()
            rv(v.tensor_tensor_scan(m_row[:, :], ri, ri, 0.0, ALU.max, ALU.max))
            rv.settle()
            rv(tt(rt2[:, :], t1, m_row[:, :], ALU.add))
            rv(v.tensor_copy(rt[0:GH, :], rb))
            rv(v.tensor_copy(rt[32:32 + GH, :], g_row[:, :]))
            for a in range(TT):
                sl = slice(a * P, a * P + P)
                rv(v.tensor_scalar(rt[64:64 + GH, sl], g_row[:, sl], g_row[:, a * P + P - 1:a * P + P], -1.0, ALU.subtract, ALU.mult))
            rv(v.tensor_copy(rt[96:96 + MH, :], ri))
            assert rv.n == ROW_V
            dve.wait_ge(row_t, 1)
            v.tensor_copy(cols[:, :, :].rearrange("p a n -> p (a n)"), bank[5][:, 0:SEQ]).then_inc(col_e, 1)
            v.tensor_copy(colm[:, :, :].rearrange("p a n -> p (a n)"), bank[5][:, SEQ:SEQ + TT * MH]).then_inc(col_e, 1)
            dve.wait_ge(col_a, 1)
            dve.wait_ge(col_e, 2)
            tt(beg, eg[:, GH:2 * GH], cols[:, 1, 0:GH], ALU.mult).then_inc(col_e, 1)

            dve.wait_ge(act_evac, evacuated("A", 8)[1])
            c_ = Count(dve, cv)
            for j in range(3):
                for tap in range(GDN_TAPS - 1, -1, -1):
                    for c in range(6 * j, 6 * j + 6):
                        d = GDN_TAPS - 1 - tap
                        if d:
                            c_.settle(5)
                            c_(v.scalar_tensor_tensor(conv[:, c, d:], proj[:, c, 0:SEQ - d], vec2[:, tap, c:c + 1], conv[:, c, d:],
                                                      ALU.mult, ALU.add))
                        else:
                            c_(v.tensor_scalar(conv[:, c, :], proj[:, c, :], vec2[:, tap, c:c + 1], None, ALU.mult))
            c_.settle()
            for g in range(1, 9, 2):
                dve.wait_ge(tm_t, g + 1)
                v.tensor_copy(tm[:, :, 2 * g:2 * g + 2, :].rearrange("p a c d -> p c a d"),
                              mb(g)[:, :].rearrange("p (c a d) -> p c a d", c=2, a=TT)).then_inc(tm_ed, 1)
            dve.wait_ge(tm_ea, 5)
            dve.wait_ge(tm_ed, 4)
            l2 = Count(dve, l2_v)
            dve.wait_ge(gw_l, 1)
            sq = slabf[:, 0:24 * P].rearrange("p (a c d) -> p a c d", a=TT, d=P)
            ssv = ss.rearrange("p (a c) -> p a c", a=TT)
            l2(tt(sq, tm[:, :, 0:12, :], tm[:, :, 0:12, :], ALU.mult))
            l2.settle()
            l2(v.tensor_reduce(ssv, sq, AX.X, ALU.add))
            l2.settle()
            l2(v.tensor_scalar(ss, ss, EPS, None, ALU.add))
            dve.wait_ge(l2_a, 1)
            l2(v.reciprocal(ss, ss))
            l2.settle()
            l2(v.tensor_scalar(ssv[:, :, 0:GH], ssv[:, :, 0:GH], DK ** -0.5, None, ALU.mult))
            l2.settle()
            l2(tt(tm[:, :, 0:12, :], tm[:, :, 0:12, :], bc(ssv.unsqueeze(3), [P, TT, 12, P]), ALU.mult))
            for j in range(3):
                dve.wait_ge(dec_t, j + 1)
                for x in range(2):
                    for a in range(TT):
                        h = 2 * j + x
                        v.tensor_scalar(S_L[:, a * GH + h, :], bank[4 + j][:, x * SEQ + a * P:x * SEQ + a * P + P],
                                        cols[:, a, 32 + h:33 + h], 0.0, ALU.subtract, ALU.max).then_inc(dec_v, 1)
            bshape = [P, 12, P]
            cc = Count(dve, c_v)
            cc(v.tensor_copy(S_T, bc(ident[:, :].unsqueeze(1), bshape)))
            cc(v.tensor_copy(S_U, bc(ident[:, :].unsqueeze(1), bshape)))
            dve.wait_ge(qk_t, 6)
            kv = Count(dve, kv_v)
            hs = [P, GH, P]
            kv(tt(tm[:, :, 12:18, :], tm[:, :, 12:18, :], bc(cols[:, :, 0:GH].unsqueeze(3), [P, TT, GH, P]), ALU.mult))
            kv(tt(tm[:, 0, 6:12, :], tm[:, 0, 6:12, :], bc(tail[:, 0:GH].unsqueeze(2), hs), ALU.mult))
            dve.wait_ge(col_e, 3)
            kv(tt(tm[:, 1, 6:12, :], tm[:, 1, 6:12, :], bc(beg.unsqueeze(2), hs), ALU.mult))
            kv(tt(tm[:, 1, 0:6, :], tm[:, 1, 0:6, :], bc(eg[:, GH:2 * GH].unsqueeze(2), hs), ALU.mult))
            dve.wait_ge(dec_a, 1)
            for n in range(12):
                a, h = n // GH, n % GH
                dve.wait_ge(kk_t, n // 4 + 1)
                b = bank[(7, 4, 5)[n // 4]]
                v.scalar_tensor_tensor(S_L[:, n, :], b[:, n % 4 * P:n % 4 * P + P], cols[:, a, h:h + 1], S_L[:, n, :],
                                       ALU.mult, ALU.mult).then_inc(l_v, 1)
            dve.wait_ge(lev_in, 16)
            dve.wait_ge(l_v, 12)
            cc(tt(S_C, S_L, bc(lev[:, 0, :].unsqueeze(1), bshape), ALU.mult))
            for l in range(7):
                if l < 6:
                    dve.wait_ge(z_t, 3 * l + 3)
                    cc(tt(S_C, S_L, bc(lev[:, l + 1, :].unsqueeze(1), bshape), ALU.mult))
                for g in range(3):
                    dve.wait_ge(d_t, 6 * l + 2 * g + 2)
                    for S_X, b in ((S_T, bank[6]), (S_U, bank[7])):
                        t = S_X[:, 4 * g:4 * g + 4, :].rearrange("p c s -> p (c s)")
                        v.scalar_tensor_tensor(t, b[:, :], -1.0, t, ALU.mult, ALU.add).then_inc(d_e, 1)
            for g in range(2):
                dve.wait_ge(u_t, g + 1)
                k = 4 if g == 0 else 2
                v.tensor_copy(S_C[:, 4 * g:4 * g + k, :].rearrange("p c s -> p (c s)"), bank[4 + g][:, 0:k * P]).then_inc(u_e, 1)
            av = Count(dve, a_v)
            cc.settle()
            for j in range(3):
                dve.wait_ge(a_t, j + 1)
                for x in range(2):
                    for a in range(TT):
                        h = 2 * j + x
                        av(v.tensor_scalar(S_L[:, a * GH + h, :], bank[4 + j][:, x * SEQ + a * P:x * SEQ + a * P + P],
                                           cols[:, a, 32 + h:33 + h], 0.0, ALU.subtract, ALU.min))
            dve.wait_ge(a_a, 1)
            av(tt(S_L, S_L, bc(upper[:, :].unsqueeze(1), bshape), ALU.mult))
            av.settle()
            for g in range(3):
                dve.wait_ge(a_t, 4 + g)
                t = S_L[:, 4 * g:4 * g + 4, :].rearrange("p c s -> p (c s)")
                av(tt(t, bank[(7, 4, 5)[g]][:, :], t, ALU.mult))
            for g in range(2):
                dve.wait_ge(vn_t, g + 1)
                k = 4 if g == 0 else 2
                v.tensor_copy(S_C[:, 6 + 4 * g:6 + 4 * g + k, :].rearrange("p c s -> p (c s)"),
                              bank[6 + g][:, 0:k * P]).then_inc(vn_e, 1)
            dve.wait_ge(o_e, 3)
            yn = Count(dve, yn_v)
            yn(tt(S_L, S_T, S_T, ALU.mult))
            yn.settle()
            yn(v.tensor_reduce(ss[:, 0:12], S_L, AX.X, ALU.add))
            yn.settle()
            yn(v.tensor_scalar(ss[:, 0:12], ss[:, 0:12], 1.0 / DK, EPS, ALU.mult, ALU.add))
            dve.wait_ge(yn_a, 1)
            yn(v.reciprocal(ss[:, 0:12], ss[:, 0:12]))
            yn.settle()
            yn(tt(S_T, S_T, bc(ss[:, 0:12].unsqueeze(2), bshape), ALU.mult))
            dve.wait_ge(spill, 16)
            dve.wait_ge(act_evac, evacuated("Z", 2)[1])
            for j in range(3):
                dve.wait_ge(y_t, j + 1)
                v.scalar_tensor_tensor(yT[:, 2 * j:2 * j + 2, :].rearrange("p c s -> p (c s)"), bank[4 + j][:, :], g_gdn,
                                       zs[:, 2 * j:2 * j + 2, :].rearrange("p c s -> p (c s)"), ALU.mult, ALU.mult).then_inc(y_e, 1)
            v.memset(v_b[:, :, :, DK:DK + 1], 1.0).then_inc(set_up, 1)

            rest("BQK")
            for name in ("BV", "BO", "CQK", "CV"):
                first(name)
                rest(name)
            first("G")

            dve.wait_ge(mask_in, 32)
            for h in range(MH):
                dve.wait_ge(ml_s, h + 1)
                v.scalar_tensor_tensor(ml_x[:, h, 0:SEQ], bank[4][:, 0:SEQ], cols[:, 0, 96 + h:97 + h], pos_mask[:, 0:SEQ],
                                       ALU.subtract, ALU.add).then_inc(ml_v, 1)
                v.scalar_tensor_tensor(ml_x[:, h, SEQ:384], bank[4][:, P:SEQ], cols[:, 1, 96 + h:97 + h], pos_mask[:, SEQ:384],
                                       ALU.subtract, ALU.add).then_inc(ml_v, 1)
                dve.wait_ge(ml_a, h + 1)
                v.scalar_tensor_tensor(ml_x[:, h, :], bank[5][:, 0:384], DK ** -0.5, ml_x[:, h, :], ALU.mult, ALU.mult).then_inc(ml_w, 1)
            dve.wait_ge(ml_ne, MH)
            mh = Count(dve, ml_h)
            den3 = den.rearrange("p (a h) -> p a h", a=TT)
            mh(v.scalar_tensor_tensor(den3, num[:, :, :, DK], -1.0, num[:, :, :, DK], ALU.mult, ALU.max))
            mh.settle()
            mh(tt(den, den, emn, ALU.max))
            mh.settle()
            mh(v.reciprocal(den, den))
            mh.settle()
            hv = num[:, :, :, 0:DK]
            nshape = [P, TT, MH, DK]
            mh(tt(hv, hv, bc(den3.unsqueeze(3), nshape), ALU.mult))
            mh.settle()
            sq = slabf[:, 0:8 * DK].rearrange("p (a h d) -> p a h d", a=TT, h=MH)
            mh(tt(sq, hv, hv, ALU.mult))
            mh.settle()
            s3 = ss[:, 0:8].rearrange("p (a h) -> p a h", a=TT)
            mh(v.tensor_reduce(s3, sq, AX.X, ALU.add))
            mh.settle()
            mh(v.tensor_scalar(ss[:, 0:8], ss[:, 0:8], 1.0 / DK, EPS, ALU.mult, ALU.add))
            dve.wait_ge(ml_ha, 1)
            mh(v.reciprocal(ss[:, 0:8], ss[:, 0:8]))
            mh.settle()
            mh(tt(hv, hv, bc(s3.unsqueeze(3), nshape), ALU.mult))
            for j in range(2):
                dve.wait_ge(ml_t, j + 1)
                v.scalar_tensor_tensor(yT[:, GH + 2 * j:GH + 2 * j + 2, :].rearrange("p c s -> p (c s)"), bank[4 + j][:, :], g_ml,
                                       o_b[:, 2 * j:2 * j + 2, :].rearrange("p c s -> p (c s)"), ALU.mult, ALU.mult).then_inc(ml_y, 1)

            for h in range(SH):
                dve.wait_ge(sb_t, h + 1)
                v.scalar_tensor_tensor(sb_z[:, h, :], mb(h)[:, 0:384], DK ** -0.5, neg_mask, ALU.mult, ALU.add).then_inc(sb_zv, 1)
            for h in range(SH):
                dve.wait_ge(sb_a, 3 * h + 3)
                v.scalar_tensor_tensor(sb_s[:, h, :], sb_z[:, h, :], 0.0, sb_s[:, h, :], ALU.max, ALU.add).then_inc(sb_sp, 1)
            for h in range(SH):
                dve.wait_ge(sb_r, h + 1)
                tt(sb_z[:, h, :], sb_z[:, h, :], bank[4 + h % 2][:, 0:384], ALU.subtract).then_inc(sb_x, 1)

            rest("G")
            first("BR")
            for c in range(4):
                dve.wait_ge(y_hi, c + 1)
                tt(x_hl[:, 1, 4 * c:4 * c + 4, :], yT[:, 4 * c:4 * c + 4, :], x_hl[:, 0, 4 * c:4 * c + 4, :].bitcast(f32),
                   ALU.subtract).then_inc(y_lo, 1)
            dve.wait_ge(act_evac, evacuated("G", 23)[1])

            def merge(i, par, hp):
                dve.wait_ge(half_used, hp * 4 + (2 * par + 2))
                if not isinstance(i, int) or i >= 2:
                    dve.wait_ge(m_lo, i - 1)
                m0, m1 = tmp[:, par, 0:512], tmp[:, par, 512:1024]
                gate = lambda j: gates[:, bass.ds(i * 2 + j * KC, 2), :].rearrange("p c s -> p (c s)")
                tt(m0, bank[par][:, :], gate(0), ALU.mult)
                tt(m1, bank[2 + par][:, :], gate(1), ALU.mult).then_inc(br_c, 1)
                dve.wait_ge(br_c, i * 2 + 1)
                tt(m0, m0, m1, ALU.add).then_inc(br_c, 1)
                dve.wait_ge(br_c, i * 2 + 2)
                tt(m1, bank[4 + par][:, :], gate(2), ALU.mult).then_inc(dve_evac, 1)
                dve.wait_ge(dve_evac, i + 1)
                tt(m0, m0, m1, ALU.add).then_inc(br_m, 1)

            def merged_lo(i, par):
                dve.wait_ge(m_hi, i + 1)
                two = lambda j: m_hl[:, j, bass.ds(i * 2, 2), :].rearrange("p c s -> p (c s)")
                tt(two(1), tmp[:, par, 0:512], two(0).bitcast(f32), ALU.subtract).then_inc(m_lo, 1)

            def br_unit(i, par, hp):
                lo("BR", i, par, hp)
                if not isinstance(i, int) or i >= 2:
                    merged_lo(i - 2, par)
                merge(i - 1, 1 - par, hp if par else hp - 1)
            each_unit(dve, "BR", br_unit, 1, 2)
            each_unit(dve, "BR", br_unit, 2)
            first("WO")
            u = last_unit("BR")
            merged_lo(COUNT["BR"] - 2, 1 - u % 2)
            merge(COUNT["BR"] - 1, u % 2, u // 2)
            merged_lo(COUNT["BR"] - 1, u % 2)
            dve.wait_ge(back, 16)
            rest("WO", 1)
            first("K")
            u = last_unit("WO")
            add_residual("WO", 7, u % 2, u // 2)
            norm(1, memT, g_mem, mem_hl)
            rest("K", 1, 2)
            norm(2, xT, g_xa, x_hl)
            rest("K", 2)
            first("V")
            rest("V", 1, 2)
            tt(gqk, gq, gk, ALU.mult).then_inc(set_up, 1)
            dve.wait_ge(set_up, 4)
            for h in range(XH):
                dve.wait_ge(xk_t, h + 1)
                if h:
                    dve.wait_ge(xk_v, 3 * h)
                v.tensor_scalar(rstd[:, :], bank[6 + h % 2][:, 0:SEQ], 1.0 / XD, EPS, ALU.mult, ALU.add).then_inc(xk_v, 1)
                dve.wait_ge(xk_a, h + 1)
                v.reciprocal(rstd[:, :], rstd[:, :]).then_inc(xk_v, 1)
                dve.wait_ge(xk_v, 3 * h + 2)
                for c in range(XC):
                    last = v.scalar_tensor_tensor(kT[:, 4 * h + c, :], kT[:, 4 * h + c, :], gqk[:, c:c + 1], rstd[:, :], ALU.mult, ALU.mult)
                last.then_inc(xk_v, 1)
            rest("V", 2)
            first("Q")
            rest("Q")
            first("XO")
            dve.wait_ge(xq_t, XH)
            v.tensor_scalar(xss, bank[6][:, 0:8], 1.0 / XD, EPS, ALU.mult, ALU.add).then_inc(xq_v, 1)
            dve.wait_ge(xq_a, 1)
            v.reciprocal(xss, xss).then_inc(xq_v, 1)
            dve.wait_ge(xq_v, 2)
            v.tensor_scalar(xss, xss, XD ** -0.5, None, ALU.mult).then_inc(xq_v, 1)
            dve.wait_ge(xq_v, 3)

            def scale_prob(j):
                h, a = j // 2, j % 2
                dve.wait_ge(xl_a, j + 1)
                v.reciprocal(xsum[:, j:j + 1], xsum[:, j:j + 1]).then_inc(xp_v, 1)
                dve.wait_ge(xp_v, 2 * j + 1)
                v.tensor_scalar(prob[:, a, h, :], prob[:, a, h, :], xsum[:, j:j + 1], None, ALU.mult).then_inc(xp_v, 1)

            for j in range(2 * XH):
                dve.wait_ge(xl_t, j + 1)
                v.reduce_max(xmx[:, j:j + 1], bank[4 + j % 2][:, 0:SEQ], AX.X).then_inc(xl_v, 1)
                dve.wait_ge(xl_v, 2 * j + 1)
                v.scalar_tensor_tensor(xmx[:, j:j + 1], xmx[:, j:j + 1], -1.0, xss[:, j:j + 1], ALU.mult, ALU.mult).then_inc(xl_v, 1)
                if j:
                    scale_prob(j - 1)
            scale_prob(2 * XH - 1)
            for c in range(8):
                dve.wait_ge(xo_h, c + 1)
                tt(x_hl[:, 1, 2 * c:2 * c + 2, :].rearrange("p c s -> p (c s)"), mb(c)[:, :],
                   x_hl[:, 0, 2 * c:2 * c + 2, :].rearrange("p c s -> p (c s)").bitcast(f32), ALU.subtract).then_inc(xo_l, 1)
            rest("XO")
            first("UP")
            u = last_unit("XO")
            add_residual("XO", 7, u % 2, u // 2)
            norm(3, xT, g_ffn, x_hl)

            def taps(j, up, done):
                par, h0 = slot_of("UP", up)
                dve.wait_ge(half_used, j * 4 + (4 * h0 + 2 * par + 2))
                if not isinstance(j, int) or j:
                    dve.wait_ge(f_p, j)
                n = 0
                for d in range(FFN_TAPS):
                    for x in range(2):
                        o = tmp[:, 0, (2 * up + x) * SEQ + d:(2 * up + x + 1) * SEQ]
                        b = bank[par][:, x * SEQ:(x + 1) * SEQ - d]
                        w = vec3[:, FFN_TAPS - 1 - d, bass.ds(j * 2 + (up * FC + x), 1)]
                        if d:
                            dve.wait_ge(done, j * 5 + (n - 1))
                            ins = v.scalar_tensor_tensor(o, b, w, o, ALU.mult, ALU.add)
                        else:
                            ins = v.tensor_scalar(o, b, w, None, ALU.mult)
                        n += 1
                        ins.then_inc(done if n < 6 else dve_evac, 1)

            def product(j):
                dve.wait_ge(f_s, j + 1)
                if not isinstance(j, int) or j:
                    dve.wait_ge(f_l, j)
                dve.wait_ge(dve_evac, j * 2 + (evacuated("UP", 1)[1]))
                tt(tmp[:, 1, 512:1024], tmp[:, 0, 0:512], tmp[:, 0, 512:1024], ALU.mult).then_inc(f_p, 1)

            def product_lo(j):
                dve.wait_ge(f_h, j + 1)
                two = lambda k: act_hl[:, k, bass.ds(j * 2, 2), :].rearrange("p c s -> p (c s)")
                tt(two(1), tmp[:, 1, 512:1024], two(0).bitcast(f32), ALU.subtract).then_inc(f_l, 1)

            (p0, h0), (p1, h1) = slot_of("UP", 0), slot_of("UP", 1)
            lo("UP", 1, p1, h1)
            taps(0, 0, f_c)
            with dve.Fori(1, FC // 2) as j:
                lo("UP", 2 * j, p0, j + h0)
                taps(j - 1, 1, f_g)
                product(j - 1)
                lo("UP", 2 * j + 1, p1, j + h1)
                taps(j, 0, f_c)
                product_lo(j - 1)
            first("DN")
            taps(FC // 2 - 1, 1, f_g)
            product(FC // 2 - 1)
            product_lo(FC // 2 - 1)

            for g in range(1, NDG):
                lo("DN", g, *slot_of("DN", g))
            dve.wait_ge(back, 32)
            dve.wait_ge(f_l, FC // 2)

            def finish(c, par):
                dve.wait_ge(half_used, c * (2 * NDG) + (2 * FIRST["DN"] + 2 * NDG))
                if not isinstance(c, int) or c >= 2:
                    dve.wait_ge(ot_t, c - 1)
                for x in range(2):
                    last = tt(tmp[:, par, x * SEQ:(x + 1) * SEQ], bank[par + 2 * x][:, 0:SEQ],
                              x_back[:, bass.ds(c * 2 + x, 1), :].rearrange("p c s -> p (c s)"), ALU.add)
                last.then_inc(dve_evac, 1)

            def down_pair(c, par):
                for g in range(NDG):
                    p, h0 = slot_of("DN", g)
                    lo("DN", g, p, c * (NDG // 2) + h0)
                    if g == 0:
                        finish(c - 1, 1 - par)

            down_pair(1, 1)
            down_pair(2, 0)
            down_pair(3, 1)
            with dve.Fori(2, 4) as r:
                down_pair(r * 2, 0)
                down_pair(r * 2 + 1, 1)
            finish(7, 1)

        @block.tensor
        def _(pe):
            mm = nc.tensor.matmul

            def three(o, w, x, start, stop):
                mm(o, w[0], x[0], start=start, stop=False)
                mm(o, w[0], x[1], start=False, stop=False)
                return mm(o, w[1], x[0], start=False, stop=stop)

            def wait_bank(name, i):
                if isinstance(i, int) and i < 2:
                    u = FIRST[name] + i - 2
                    if u < 0:
                        return
                    before = phase_of(u)
                    e, n = evacuated(before, u - FIRST[before])
                    pe.wait_ge(evac[e], n)
                else:
                    e, n = evacuated(name, 0)
                    pe.wait_ge(evac[e], i + (n - 2))

            def project(name, acts, start=0, stop=None):
                kind = kind_of[name]

                def unit(i, par, hp):
                    wait_bank(name, i)
                    for half in range(2):
                        pe.wait_ge(lo_ready, hp * 4 + (2 * par + half + 1))
                        if kind == TM_:
                            for k in range(KC // 2):
                                kk = half * (KC // 2) + k
                                w = [t[:, half, k * CW:(k + 1) * CW] for t in (w_hi, w_lo)]
                                for a in range(TT):
                                    x = [acts[:, j, kk, a * P:(a + 1) * P] for j in range(2)]
                                    last = three(bank[par + 2 * a][:, 0:CW], x, w, kk == 0, kk == KC - 1)
                        else:
                            cuts = (0, GH, GH + MH, KC) if kind == BR else (0, KC)
                            for k in range(KC):
                                g = sum(k >= c for c in cuts) - 1
                                w = [t[:, half, k * P:(k + 1) * P] for t in (w_hi, w_lo)]
                                last = three(bank[par + 2 * g][:, half * SEQ:(half + 1) * SEQ], w, [acts[:, j, k, :] for j in range(2)],
                                             k == cuts[g], k + 1 == cuts[g + 1])
                        last.then_inc(half_used, 1)
                stop = COUNT[name] if stop is None else stop
                if start < 2:
                    each_unit(pe, name, unit, start, min(2, stop))
                each_unit(pe, name, unit, max(2, start), stop)

            def transposes(k, src):
                for g in range(8):
                    if g >= 4:
                        pe.wait_ge(tin_e, 8 * k + g - 3)
                    for c in range(4):
                        cc = 4 * (g % 4) + c
                        last = nc.tensor.transpose(mb(g)[:, c * P:(c + 1) * P], src[:, g // 4, cc * P:(cc + 1) * P], ident[:, :])
                    last.then_inc(tin_t, 1)

            def sum_squares(k):
                for c in range(4):
                    pe.wait_ge(n_sq, 4 * k + c + 1)
                    for j in range(4):
                        last = mm(bank[7][:, 0:SEQ], ones[:, :], tmp[:, c % 2, j * SEQ:(j + 1) * SEQ], start=c + j == 0, stop=c + j == 6)
                    last.then_inc(n_ss, 1)

            pe.wait_ge(x_in, 16)
            pe.wait_ge(const_in, 48)
            transposes(0, x_tm)
            pe.wait_ge(vec_in, 16 * 14)
            pe.wait_ge(tin_e, 8)
            at = 0
            for i, k in ((0, 74), (1, 72), (2, 88), (3, 88), (4, 88)):
                last = nc.tensor.transpose(bank[4][:, at:at + k], vecs[0:k, i, :], ident[0:k, 0:k])
                at += k
            last.then_inc(vec_t, 1)
            pe.wait_ge(set_up, 1)
            sum_squares(0)
            pe.wait_ge(n_lo, 4)
            pe.wait_ge(gw_l, 1)
            pe.wait_ge(set_up, 2)
            for k in range(KC):
                last = three(bank[4][:, 0:SEQ], [t[:, k, :] for t in (gw_hi, gw_lo)], [x_hl[:, j, k, :] for j in range(2)],
                             k == 0, k == KC - 1)
            last.then_inc(row_mm, 1)
            project("A", x_hl)
            project("Z", x_hl)
            pe.wait_ge(row_v, ROW_V)
            for a in range(TT):
                nc.tensor.transpose(bank[5][:, a * P:(a + 1) * P], rt[:, a * P:(a + 1) * P], ident[:, :])
                last = nc.tensor.transpose(bank[5][:, SEQ + a * MH:SEQ + (a + 1) * MH], rt2[:, a * P:(a + 1) * P], ident[0:MH, 0:MH])
            last.then_inc(row_t, 1)

            pe.wait_ge(col_e, 2)
            for g in range(9):
                pe.wait_ge(cs, (2 * g + 1) // 6 + 1)
                if g >= 4:
                    pe.wait_ge(tm_ed if g % 2 else tm_ea, (g - 4) // 2 + 1)
                for c in range(2):
                    for a in range(TT):
                        last = nc.tensor.transpose(mb(g)[:, (2 * c + a) * P:(2 * c + a + 1) * P],
                                                   conv[:, 2 * g + c, a * P:(a + 1) * P], ident[:, :])
                last.then_inc(tm_t, 1)
            pe.wait_ge(l2_v, 6)
            pe.wait_ge(tm_ea, 5)
            for g in range(6):
                if g >= 4:
                    pe.wait_ge(qk_e, g - 3)
                for c in range(2):
                    for a in range(TT):
                        last = nc.tensor.transpose(mb(g)[:, (2 * c + a) * P:(2 * c + a + 1) * P], tm[:, a, 2 * g + c, :], ident[:, :])
                last.then_inc(qk_t, 1)

            def spread(b, h, row):
                n = row.shape[0]
                return mm(b, ident[0:n, h:h + 1].to_broadcast([n, P]), row, start=True, stop=True)

            pe.wait_ge(qk_e, 6)
            for j in range(3):
                for x in range(2):
                    last = spread(bank[4 + j][:, x * SEQ:(x + 1) * SEQ], 2 * j + x, g_row[:, :])
                last.then_inc(dec_t, 1)

            def chunk_pairs(sem_, lhs, rhs, waits):
                for g in range(3):
                    pe.wait_ge(*waits[g])
                    for n in range(4 * g, 4 * g + 4):
                        a, h = n // GH, n % GH
                        last = mm(bank[(7, 4, 5)[g]][:, n % 4 * P:n % 4 * P + P], conv[:, lhs + h, a * P:(a + 1) * P],
                                  conv[:, rhs + h, a * P:(a + 1) * P], start=True, stop=True)
                    last.then_inc(sem_, 1)

            chunk_pairs(kk_t, GH, GH, ((qk_e, 6), (dec_v, 4), (dec_v, 8)))

            def group(o, lhs, rhs, ns):
                for i, n in enumerate(ns):
                    last = mm(o[:, i * P:(i + 1) * P], lhs(n), rhs(n), start=True, stop=True)
                return last

            for l in range(7):
                def zs_of(g):
                    if l:
                        pe.wait_ge(d_e, 6 * (l - 1) + 2 * g + 2)
                    pe.wait_ge(c_v, 3 + l)
                    if l or g == 2:
                        pe.wait_ge(z_e, 3 * l + (1 if g == 2 else 0))
                    elif g == 0:
                        pe.wait_ge(l_v, 12)
                    group(bank[4 + g % 2], lambda n: S_C[:, n, :], lambda n: S_U[:, n, :], range(4 * g, 4 * g + 4)).then_inc(z_t, 1)

                def ds_of(g):
                    pe.wait_ge(z_e, 3 * l + g + 1)
                    if l or g:
                        pe.wait_ge(d_e, 6 * l + 2 * g)
                    ns = range(4 * g, 4 * g + 4)
                    group(bank[6], lambda n: S_Z[:, n, :], lambda n: S_T[:, n, :], ns).then_inc(d_t, 1)
                    group(bank[7], lambda n: S_T[:, n, :], lambda n: S_Z[:, n, :], ns).then_inc(d_t, 1)

                zs_of(0)
                zs_of(1)
                ds_of(0)
                zs_of(2)
                ds_of(1)
                ds_of(2)

            two_groups = ((0, range(0, 4)), (1, range(4, 6)))
            pe.wait_ge(d_e, 42)
            pe.wait_ge(kv_v, 4)
            for g, hs in two_groups:
                group(bank[4 + g], lambda h: S_U[:, h, :], lambda h: tm[:, 0, 12 + h, :], hs).then_inc(u_t, 1)
            for g, hs in two_groups:
                group(bank[6 + g], lambda h: tm[:, 1, 6 + h, :], lambda h: S_U[:, 6 + h, :], hs).then_inc(w_t, 1)
            pe.wait_ge(u_e, 2)
            for g, hs in two_groups:
                group(bank[4 + g], lambda h: tm[:, 0, 6 + h, :], lambda h: S_C[:, h, :], hs).then_inc(s_t, 1)
            for g, hs in two_groups:
                pe.wait_ge(w_e, g + 1)
                for i, h in enumerate(hs):
                    last = nc.tensor.transpose(bank[6 + g][:, i * P:(i + 1) * P], tm[:, 1, h, :], ident[:, :])
                last.then_inc(qd_t, 1)
            for j in range(3):
                pe.wait_ge(*((s_e, 1), (s_e, 2), (qd_e, 1))[j])
                for x in range(2):
                    last = spread(bank[4 + j][:, x * SEQ:(x + 1) * SEQ], 2 * j + x, g_row[:, :])
                last.then_inc(a_t, 1)
            chunk_pairs(a_t, GH, 0, ((qd_e, 2), (a_v, 4), (a_v, 8)))
            for g, hs in two_groups:
                pe.wait_ge(a_v, 12 if g == 0 else 14)
                for i, h in enumerate(hs):
                    o = bank[6 + g][:, i * P:(i + 1) * P]
                    mm(o, S_U[:, 6 + h, :], tm[:, 1, 12 + h, :], start=True, stop=False)
                    last = mm(o, S_Z[:, h, :], S_Z[:, 6 + h, :], start=False, stop=True)
                last.then_inc(vn_t, 1)
            pe.wait_ge(a_v, 16)
            pe.wait_ge(vn_e, 2)
            for g in range(3):
                for n in range(4 * g, 4 * g + 4):
                    o = mb(g)[:, n % 4 * P:n % 4 * P + P]
                    if n >= GH:
                        mm(o, tm[:, 0, n - GH, :], S_Z[:, n, :], start=True, stop=False)
                    last = mm(o, S_L[:, n, :], S_C[:, n, :], start=n < GH, stop=True)
                last.then_inc(o_t, 1)

            def to_features(j, src, sem_):
                for x in range(2):
                    for a in range(TT):
                        last = nc.tensor.transpose(bank[4 + j][:, x * SEQ + a * P:x * SEQ + (a + 1) * P], src(2 * j + x, a), ident[:, :])
                last.then_inc(sem_, 1)

            pe.wait_ge(yn_v, 5)
            for j in range(3):
                to_features(j, lambda h, a: S_T[:, a * GH + h, :], y_t)

            for name in ("BQK", "BV", "BO", "CQK", "CV"):
                project(name, x_hl)

            pe.wait_ge(act_evac, evacuated("CV", 2)[1])
            pe.wait_ge(set_up, 3)

            def scores(b, k, q):
                mm(b[:, 0:SEQ], k[:, 0:P], q, start=True, stop=True)
                return mm(b[:, SEQ:384], k[:, P:SEQ], q[:, P:SEQ], start=True, stop=True)

            def ml_scores(h):
                if h:
                    pe.wait_ge(ml_w, h)
                spread(bank[4][:, 0:SEQ], h, m_row[:, :])
                scores(bank[5], qk_b[:, MH + h, :], qk_b[:, h, :]).then_inc(ml_s, 1)

            pe.wait_ge(y_e, 3)
            ml_scores(0)
            for h in range(MH):
                if h + 1 < MH:
                    ml_scores(h + 1)
                pe.wait_ge(ml_w, h + 1)
                if h >= 2:
                    pe.wait_ge(ml_ne, h - 1)
                b = bank[6 + h % 2]
                mm(b[:, 0:129], ml_x[:, h, 0:P], v_b[:, 0, h, :], start=True, stop=True)
                mm(b[:, 129:258], ml_x[:, h, P:SEQ], v_b[:, 0, h, :], start=True, stop=False)
                mm(b[:, 129:258], ml_x[:, h, SEQ:384], v_b[:, 1, h, :], start=False, stop=True).then_inc(ml_n, 1)
            pe.wait_ge(ml_h, 9)
            for j in range(2):
                to_features(j, lambda h, a: num[:, a, h, 0:DK], ml_t)

            for h in range(SH):
                if h < 2:
                    pe.wait_ge(ml_y, h + 1)
                elif h >= 4:
                    pe.wait_ge(sb_zv, h - 3)
                scores(mb(h), qk_c[:, SH + h, :], qk_c[:, h, :]).then_inc(sb_t, 1)
            pe.wait_ge(sb_zv, SH)
            for h in range(SH):
                pe.wait_ge(sb_sp, h + 1)
                if h >= 2:
                    pe.wait_ge(sb_x, h - 1)
                b = bank[4 + h % 2]
                mm(b[:, 0:SEQ], later[:, :], sb_s[:, h, 0:SEQ], start=True, stop=False)
                mm(b[:, P:SEQ], ones[:, :], sb_s[:, h, SEQ:384], start=False, stop=True)
                mm(b[:, SEQ:384], later[:, :], sb_s[:, h, SEQ:384], start=True, stop=True).then_inc(sb_r, 1)
            for h in range(SH):
                pe.wait_ge(sb_e, h + 1)
                if h >= 2:
                    pe.wait_ge(sb_y, h - 1)
                b = bank[6 + h % 2]
                mm(b[:, 0:SEQ], v_c[:, 0, h * DK:(h + 1) * DK], sb_z[:, h, 0:SEQ], start=True, stop=False)
                mm(b[:, P:SEQ], v_c[:, 1, h * DK:(h + 1) * DK], sb_z[:, h, SEQ:384], start=False, stop=True).then_inc(sb_o, 1)

            project("G", x_hl)
            pe.wait_ge(y_lo, 4)
            project("BR", x_hl)
            pe.wait_ge(m_lo, COUNT["BR"])
            project("WO", m_hl, 0, 5)
            pe.wait_ge(mem_in, 16)
            transposes(1, mem_tm)
            project("WO", m_hl, 5)
            pe.wait_ge(tin_e, 16)
            sum_squares(1)
            pe.wait_ge(n_lo, 8)
            project("K", mem_hl, 0, 2)
            sum_squares(2)
            project("K", mem_hl, 2)
            project("V", mem_hl, 0, 2)
            for h in range(XH):
                pe.wait_ge(xk_s, h + 1)
                if h >= 2:
                    pe.wait_ge(xk_v, 3 * (h - 2) + 1)
                for c in range(XC):
                    last = mm(bank[6 + h % 2][:, 0:SEQ], ones[:, :], tmp[:, h % 2, c * SEQ:(c + 1) * SEQ], start=c == 0, stop=c == XC - 1)
                last.then_inc(xk_t, 1)
            project("V", mem_hl, 2)
            pe.wait_ge(n_lo, 12)
            project("Q", x_hl)
            pe.wait_ge(xk_v, 3 * XH)
            for h in range(XH):
                pe.wait_ge(xq_s, h + 1)
                for a in range(TT):
                    for c in range(XC):
                        last = mm(bank[6][:, 2 * h + a:2 * h + a + 1], tmp[:, h % 2, c * SEQ + a * P:c * SEQ + (a + 1) * P],
                                  ones[:, 0:1], start=c == 0, stop=c == XC - 1)
                last.then_inc(xq_t, 1)

            def prob_transposes(h):
                pe.wait_ge(xp_v, 4 * h + 4)
                if h >= 2:
                    pe.wait_ge(xp_e, h - 1)
                elif h == 0:
                    pe.wait_ge(xq_v, 1)
                for m in range(TT):
                    for a in range(TT):
                        last = nc.tensor.transpose(bank[6 + h % 2][:, m * SEQ + a * P:m * SEQ + (a + 1) * P],
                                                   prob[:, a, h, m * P:(m + 1) * P], ident[:, :])
                last.then_inc(xp_t, 1)

            for j in range(2 * XH):
                h, a = j // 2, j % 2
                if j >= 2:
                    pe.wait_ge(xl_a, j - 1)
                for c in range(XC):
                    last = mm(bank[4 + j % 2][:, 0:SEQ], qT[:, 4 * h + c, a * P:(a + 1) * P], kT[:, 4 * h + c, :], start=c == 0, stop=c == XC - 1)
                last.then_inc(xl_t, 1)
                if j in (3, 5, 7):
                    prob_transposes((j - 3) // 2)
            prob_transposes(XH - 1)
            for c in range(8):
                h = c // 2
                pe.wait_ge(xp_e, max(h + 1, 4 if c == 3 else 3 if c == 2 else 0))
                if c < 2:
                    pe.wait_ge(xl_a, 2 * XH)
                if c >= 4:
                    pe.wait_ge(xo_l, c - 3)
                for x in range(2):
                    f = 2 * c + x
                    for m in range(TT):
                        last = mm(mb(c)[:, x * SEQ:(x + 1) * SEQ], v_tm[:, m, f * P:(f + 1) * P], probT[:, m, h, :],
                                  start=m == 0, stop=m == TT - 1)
                last.then_inc(xo_t, 1)
            pe.wait_ge(xo_l, 8)
            project("XO", x_hl)
            sum_squares(3)
            pe.wait_ge(n_lo, 16)
            project("UP", x_hl)
            pe.wait_ge(f_l, FC // 2)
            def down_pair(c, par):
                if isinstance(c, int) and c < 2:
                    pe.wait_ge(dve_evac, evacuated("UP", COUNT["UP"] - 1)[1])
                else:
                    pe.wait_ge(dve_evac, c + (evacuated("DN", 0)[1] - 2))
                for g in range(NDG):
                    for half in range(2):
                        pe.wait_ge(lo_ready, c * (2 * NDG) + (2 * FIRST["DN"] + 2 * g + half + 1))
                        for k in range(DG):
                            w = [t[:, half, k * P:(k + 1) * P] for t in (w_hi, w_lo)]
                            x = [act_hl[:, j, g * DG + k, :] for j in range(2)]
                            last = three(bank[par + 2 * half][:, 0:SEQ], w, x, g + k == 0, g * DG + k == FC - 1)
                        last.then_inc(half_used, 1)
                    if g == 1 and not (isinstance(c, int) and c == 0):
                        finished(c - 1, 1 - par)

            def finished(c, par):
                pe.wait_ge(dve_evac, c + evacuated("DN", 0)[1])
                if not isinstance(c, int) or c >= 1:
                    pe.wait_ge(ot_e, c)
                for a in range(TT):
                    for x in range(2):
                        last = nc.tensor.transpose(bank[6][:, (2 * a + x) * P:(2 * a + x + 1) * P],
                                                   tmp[:, par, x * SEQ + a * P:x * SEQ + (a + 1) * P], ident[:, :])
                last.then_inc(ot_t, 1)

            down_pair(0, 0)
            down_pair(1, 1)
            with pe.Fori(1, 4) as r:
                down_pair(r * 2, 0)
                down_pair(r * 2 + 1, 1)
            finished(7, 1)


ROW_V = 20

INPUTS = ['x', 'mem', 'norm_mix', 'w_in', 'gdn_conv', 'gdn_a_log', 'gdn_dt_bias', 'gdn_norm', 'ml_gate_bias', 'ml_norm', 'w_br',
          'w_out', 'norm_xa', 'norm_mem', 'xa_wq', 'xa_wkv', 'xa_wo', 'xa_qnorm', 'xa_knorm', 'norm_ffn', 'ffn_up', 'ffn_conv',
          'ffn_down']


def kernel(**inputs):
    import concourse.bacc as bacc
    from concourse.bass_utils import run_bass_kernel_spmd

    nc = bacc.Bacc("TRN2", target_bir_lowering=False, num_devices=1)
    arrays = {f"in_{n}": np.ascontiguousarray(inputs[n]) for n in INPUTS}
    arrays["in_shape_masks"] = shape_masks()
    T = {n[3:]: nc.dram_tensor(n, a.shape, mybir.dt.from_np(a.dtype), kind="ExternalInput").ap() for n, a in arrays.items()}
    out = nc.dram_tensor("out", (1, SEQ, D), mybir.dt.float32, kind="ExternalOutput").ap()
    build_program(nc, T, out)
    result = run_bass_kernel_spmd(nc, [arrays], core_ids=[0])
    return result.results[0]["out"]
```

```python
import math
from contextlib import ExitStack

import numpy as np
import concourse.bass as bass
from concourse import mybir

P = 128
SEQ, D = 256, 2048
TT = SEQ // P
KC = D // P
GH, MH, SH = 6, 4, 6
DK = 128
XH = 4
XD = D // XH
XC = XD // P
FF = 5632
FC = FF // P
CW = 256
GDN_TAPS, FFN_TAPS = 4, 3
EPS = 1e-6
BIG = 1e30

C_A = 0
C_AB = C_A + 3 * GH * DK
C_Z = C_AB + 2 * GH
C_QKB = C_Z + GH * DK
C_VB = C_QKB + 2 * MH * DK
C_IF = C_VB + MH * DK
C_O = C_IF + 2 * MH
C_QKC = C_O + MH * DK
C_VC = C_QKC + 2 * SH * DK
C_G = C_VC + SH * DK

FM, TM_, BR, DOWN = "feature-major", "token-major", "branches", "down"
DG = 11
NDG = FC // DG
GA_UNITS, GB_UNITS = 14, 3
STREAM = [
    ("A", "w_in", C_A, 9, FM), ("Z", "w_in", C_Z, 3, FM), ("GA", "w_in", C_G, GA_UNITS, FM),
    ("BQK", "w_in", C_QKB, 4, FM), ("BV", "w_in", C_VB, 2, TM_), ("BO", "w_in", C_O, 2, FM),
    ("CQK", "w_in", C_QKC, 6, FM), ("CV", "w_in", C_VC, 3, TM_), 
    ("GB", "w_in", C_G + GA_UNITS * CW, GB_UNITS, FM),
    ("GC", "w_in", C_G + (GA_UNITS + GB_UNITS) * CW, 3 * D // CW - GA_UNITS - GB_UNITS, FM),
    ("BR", "w_br", 0, 8, BR), ("WO", "w_out", 0, 8, FM),
    ("K", "xa_wkv", 0, 8, FM), ("Q", "xa_wq", 0, 8, FM), ("V", "xa_wkv", D, 8, TM_),
    ("XO", "xa_wo", 0, 8, FM), ("UP", "ffn_up", 0, 2 * FC // 2, FM), ("DN", "ffn_down", 0, 8 * NDG, DOWN),
]
FIRST, COUNT = {}, {}
_u = 0
for _n, _w, _c, _k, _kind in STREAM:
    FIRST[_n], COUNT[_n] = _u, _k
    _u += _k
UNITS = _u
EVAC = {n: "act" for n in ("A", "Z", "BQK", "BV", "BO", "CQK", "CV", "GA", "GB", "GC", "K", "V", "Q")}
EVAC.update({n: "dve" for n in ("BR", "WO", "XO", "UP", "DN")})


def slot_of(name, k):
    return (FIRST[name] + k) % 2, (FIRST[name] + k) // 2


def last_unit(name):
    return FIRST[name] + COUNT[name] - 1


def evacuated(name, i):
    engine, n = EVAC[name], 0
    for m, _, _, k, kind in STREAM:
        per = NDG if kind == DOWN else 1
        if m == name:
            return engine, n + i // per + 1
        if EVAC[m] == engine:
            n += k // per
    raise ValueError(name)


def half_of(m):
    u, half = divmod(m, 2)
    name = phase_of(u)
    return name, u - FIRST[name], u % 2, u // 2, half


def first_half(name, i=0):
    return 2 * (FIRST[name] + i)


def phase_of(u):
    for n, _, _, k, _ in STREAM:
        if FIRST[n] <= u < FIRST[n] + k:
            return n
    raise ValueError(u)


def shape_masks():
    r, c = np.arange(P)[:, None], np.arange(P)[None, :]
    ident = (r == c)
    levels = [((r >> (l + 1)) == (c >> (l + 1))) & ((r >> l) % 2 == 1) & ((c >> l) % 2 == 0) for l in range(7)]
    upper = r <= c
    later = r >= c
    t = np.arange(SEQ)[None, :]
    strict = np.concatenate([r < t, r < c], 1)
    incl = np.concatenate([r <= t, r <= c], 1)
    return np.concatenate([ident, upper, later] + levels + [np.where(strict, 0, -BIG), np.where(incl, 0, BIG)],
                          1).astype(np.float32)


def build_program(nc, T, out):
    f32, f32r = mybir.dt.float32, mybir.dt.float32r
    ALU, ACT, AX = mybir.AluOpType, mybir.ActivationFunctionType, mybir.AxisListType
    ctx = ExitStack()
    with ctx:
        def sb(name, shape, dt=f32, stack=ctx):
            return stack.enter_context(nc.sbuf_tensor(name, shape, dt))

        def sem(name):
            return ctx.enter_context(nc.semaphore(name))

        raw = sb("raw", [P, 2, KC * CW])
        w_hi = sb("w_hi", [P, 2, KC * P], f32r)
        w_lo = sb("w_lo", [P, 2, KC * P], f32r)
        e_scope = ExitStack()
        x_back = sb("x_back", [P, KC, SEQ], f32, e_scope)
        o_tm = sb("o_tm", [P, TT, D], f32, e_scope)
        e_scope.close()
        p_scope = ExitStack()
        prob = sb("prob", [P, TT, XH, SEQ], f32, p_scope)
        p_scope.close()
        x_hl = sb("x_hl", [P, 2, KC, SEQ], f32r)
        tmp = sb("tmp", [P, 2, 1024])
        ident = sb("ident", [P, P])
        upper = sb("upper", [P, P])
        later = sb("later", [P, P])
        ones = sb("ones", [P, P])
        rstd = sb("rstd", [P, SEQ])
        vec1 = sb("vec1", [P, 74])
        vec2 = sb("vec2", [P, GDN_TAPS, 18])
        vec3 = sb("vec3", [P, FFN_TAPS, 2 * FC])
        cols = sb("cols", [P, TT, P])
        colm = sb("colm", [P, TT, MH])
        small = sb("small", [P, 128])
        r_scope = ExitStack()
        xT = sb("xT", [P, KC, SEQ], f32, r_scope)
        yT = xT

        a_scope = ExitStack()
        A = lambda name, shape, dt=f32: sb(name, shape, dt, a_scope)
        proj = A("proj", [P, 24, SEQ])
        conv = A("conv", [P, 18, SEQ])
        lev = A("lev", [P, 7, P])
        rt = A("rt", [P, SEQ])
        rt2 = A("rt2", [MH, SEQ])
        g_row = A("g_row", [GH, SEQ])
        m_row = A("m_row", [MH, SEQ])
        s_scope = ExitStack()
        slab = sb("slab", [P, 5, 12, P], f32, s_scope)
        s_scope.close()
        w_scope = ExitStack()
        gw = sb("gw", [P, KC, P], f32, w_scope)
        gw_hi = sb("gw_hi", [P, KC, P], f32r, w_scope)
        gw_lo = sb("gw_lo", [P, KC, P], f32r, w_scope)
        vecs = sb("vecs", [P, 5, P], f32, w_scope)
        w_scope.close()
        a_scope.close()
        b_scope = ExitStack()
        gates = sb("gates", [P, 3 * KC, SEQ], f32, b_scope)
        m_hl = sb("m_hl", [P, 2, KC, SEQ], f32r, b_scope)
        b_scope.close()
        c_scope = ExitStack()
        mem_hl = sb("mem_hl", [P, 2, KC, SEQ], f32r, c_scope)
        kT = sb("kT", [P, KC, SEQ], f32, c_scope)
        v_tm = sb("v_tm", [P, TT, D], f32, c_scope)
        qT = sb("qT", [P, KC, SEQ], f32, c_scope)
        c_scope.close()
        r_scope.close()
        d_scope = ExitStack()
        act_hl = sb("act_hl", [P, 2, FC, SEQ], f32r, d_scope)
        d_scope.close()

        bank = [ctx.enter_context(nc.psum_tensor(f"bank{i}", [P, 512], f32)) for i in range(8)]

        x_tm = proj[:, 0:16, :].rearrange("p (a c) s -> p a (c s)", a=TT)
        mem_tm = gates[:, 16:32, :].rearrange("p (a c) s -> p a (c s)", a=TT)
        memT = gates[:, 32:48, :]
        tm = proj[:, 0:18, :].rearrange("p (a s) (b d) -> p a (s b) d", a=TT, d=P)
        zs = proj[:, 18:24, :]
        qk_b, o_b, qk_c = proj[:, 0:8, :], proj[:, 8:12, :], proj[:, 12:24, :]
        convf = conv[:, :, :].rearrange("p a b -> p (a b)")
        v_b = convf[:, 0:TT * MH * 129].rearrange("p (a h d) -> p a h d", a=TT, h=MH)
        num = convf[:, 1032:2064].rearrange("p (a h d) -> p a h d", a=TT, h=MH)
        v_c = convf[:, 2064:3600].rearrange("p (a n) -> p a n", a=TT)
        slabf = slab[:, :, :, :].rearrange("p a b c -> p (a b c)")
        S_L, S_C, S_Z, S_T, S_U = (slab[:, i, :, :] for i in range(5))
        ml_x = slabf[:, 0:1536].rearrange("p (h n) -> p h n", h=MH)
        sb_z = slabf[:, 1536:3840].rearrange("p (h n) -> p h n", h=SH)
        sb_s = slabf[:, 3840:6144].rearrange("p (h n) -> p h n", h=SH)
        neg_mask, pos_mask = slabf[:, 6144:6528], slabf[:, 6528:6912]
        probT = kT[:, :, :].rearrange("p (h m) s -> p m h s", h=XH)
        x_spill = nc.dram_tensor("x_spill", [P, KC * SEQ], f32).ap()
        g_spill = nc.dram_tensor("g_spill", [P, (GA_UNITS + GB_UNITS) * 2 * SEQ], f32).ap()

        ss = small[:, 0:24]
        eg, tail, beg = small[:, 24:36], small[:, 36:48], small[:, 48:54]
        nalog, dtb = small[0:GH, 54:55], small[0:GH, 55:56]
        ib, fb = small[0:MH, 56:57], small[0:MH, 57:58]
        den, emn = small[:, 60:68], small[:, 68:76]
        xss, xmx, xsum = small[:, 76:84], small[:, 84:92], small[:, 92:100]
        gqk = small[:, 100:104]

        g_mix, g_xa, g_mem, g_ffn = (vec1[:, 16 * i:16 * i + 16] for i in range(4))
        gq, gk = vec1[:, 64:68], vec1[:, 68:72]
        g_gdn, g_ml = vec1[:, 72:73], vec1[:, 73:74]

        raw_full = [sem("raw_full0"), sem("raw_full1")]
        hi_ready = sem("hi_ready")
        lo_ready = sem("lo_ready")
        half_used = sem("half_used")
        act_evac, dve_evac = sem("act_evac"), sem("dve_evac")
        evac = {"act": act_evac, "dve": dve_evac}
        x_in, mem_in, const_in, lev_in, mask_in = (sem(n) for n in ("x_in", "mem_in", "const_in", "lev_in", "mask_in"))
        vec_in, gw_zero, gw_in, spill, back, stored = (sem(n) for n in ("vec_in", "gw_zero", "gw_in", "spill", "back", "stored"))
        g_out = [sem("g_out0"), sem("g_out1")]
        g_back = sem("g_back")
        tin_t, tin_e = sem("tin_t"), sem("tin_e")
        vec_t, vec_e = sem("vec_t"), sem("vec_e")
        n_sq, n_ss, n_stat, n_rt, n_n, n_hi, n_lo = (sem("norm_" + n) for n in ("sq", "ss", "stat", "rt", "n", "hi", "lo"))
        x_sq, x_ss = sem("residual_sq"), sem("residual_ss")
        set_up = sem("set_up")
        gw_h, gw_l, row_mm, row_v, row_a, row_t, col_e, col_a = (sem(n) for n in (
            "gw_h", "gw_l", "row_mm", "row_v", "row_a", "row_t", "col_e", "col_a"))
        cv, cs, tm_t, tm_ea, tm_ed, l2_v, l2_a, qk_t, qk_e, kv_v, qd_t, qd_e = (sem(n) for n in (
            "conv_v", "conv_silu", "tm_t", "tm_ea", "tm_ed", "l2_v", "l2_a", "qk_t", "qk_e", "kv_v", "qd_t", "qd_e"))
        dec_t, dec_v, dec_a, kk_t, l_v, z_t, z_e, d_t, d_e, c_v = (sem("gdn_" + n) for n in (
            "dec_t", "dec_v", "dec_a", "kk_t", "l_v", "z_t", "z_e", "d_t", "d_e", "c_v"))
        u_t, u_e, w_t, w_e, s_t, s_e, a_t, a_v, a_a, vn_t, vn_e, o_t, o_e, yn_v, yn_a, y_t, y_e = (sem("gdn_" + n) for n in (
            "u_t", "u_e", "w_t", "w_e", "st_t", "st_e", "at_t", "at_v", "at_a", "vn_t", "vn_e", "o_t", "o_e", "yn_v", "yn_a",
            "y_t", "y_e"))
        ml_s, ml_v, ml_a, ml_n, ml_ne, ml_h, ml_ha, ml_t, ml_y = (sem("ml_" + n) for n in (
            "s", "v", "a", "n", "ne", "h", "ha", "t", "y"))
        ml_w = sem("ml_w")
        sb_t, sb_zv, sb_a, sb_sp, sb_r, sb_x, sb_e, sb_o, sb_y = (sem("sb_" + n) for n in (
            "t", "zv", "a", "sp", "r", "x", "e", "o", "y"))
        y_hi, y_lo, br_c, br_m, m_hi, m_lo = (sem(n) for n in ("y_hi", "y_lo", "br_c", "br_m", "m_hi", "m_lo"))
        xk_s, xk_t, xk_v, xk_a, xq_s, xq_t, xq_v, xq_a = (sem(n) for n in (
            "xk_s", "xk_t", "xk_v", "xk_a", "xq_s", "xq_t", "xq_v", "xq_a"))
        xl_t, xl_v, xl_a, xp_v, xp_t, xp_e, xo_t, xo_h, xo_l = (sem(n) for n in (
            "xl_t", "xl_v", "xl_a", "xp_v", "xp_t", "xp_e", "xo_t", "xo_h", "xo_l"))
        f_c, f_g, f_s, f_p, f_h, f_l = (sem("ffn_" + n) for n in ("c", "g", "s", "p", "h", "l"))
        ot_t, ot_e, dn_e = sem("ot_t"), sem("ot_e"), sem("dn_e")

        block = ctx.enter_context(nc.Block())

        @block.sync
        def _(sp):
            W = {n: T[n][0].rearrange("(k p) n -> p k n", p=P) for n in ("w_in", "w_br", "w_out", "xa_wq", "xa_wkv", "xa_wo", "ffn_up")}
            down = T["ffn_down"][0].rearrange("(g k p) n -> g p k n", p=P, k=DG)

            def load(par, half, src, kc, first=False):
                if not first:
                    sp.wait_ge(lo_ready, half * 4 + (2 * par - 2))
                sp.dma_start(raw[:, par, 0:kc * CW].rearrange("p (k n) -> p k n", n=CW), src).then_inc(raw_full[par], 16)

            def stream(name, between=None):
                u0, n = FIRST[name], COUNT[name]
                _, w, c0, _, kind = next(s for s in STREAM if s[0] == name)
                if name == "UP":
                    with sp.Fori(0, n // 2) as i:
                        for j in range(2):
                            par, h0 = slot_of(name, j)
                            load(par, i + h0, W[w][:, :, bass.ds(i * CW + j * FF, CW)], KC)
                    return
                if name == "DN":
                    with sp.Fori(0, n // NDG) as i:
                        for g in range(NDG):
                            par, h0 = slot_of(name, g)
                            load(par, i * (NDG // 2) + h0, down[g][:, :, bass.ds(i * CW, CW)], DG)
                    return
                i = 0
                while i < n:
                    u = u0 + i
                    pairs = (n - i) // 2
                    if u % 2 == 0 and u >= 2 and pairs > 1:
                        with sp.Fori(0, pairs) as r:
                            for j in range(2):
                                load(j, r + u // 2, W[w][:, :, bass.ds(r * (2 * CW) + (c0 + (i + j) * CW), CW)], KC)
                        i += 2 * pairs
                    else:
                        load(u % 2, u // 2, W[w][:, :, c0 + i * CW:c0 + (i + 1) * CW], KC, first=u < 2)
                        i += 1

            sp.dma_start(x_tm, T["x"][0].rearrange("(a p) d -> p a d", p=P)).then_inc(x_in, 16)
            c = T["shape_masks"]
            sp.dma_start(ident[:, :], c[:, 0:P]).then_inc(const_in, 16)
            sp.dma_start(upper[:, :], c[:, P:2 * P]).then_inc(const_in, 16)
            sp.dma_start(later[:, :], c[:, 2 * P:3 * P]).then_inc(const_in, 16)
            row = 0
            for name, k in (("norm_mix", 16), ("norm_xa", 16), ("norm_mem", 16), ("norm_ffn", 16), ("xa_qnorm", 4),
                            ("xa_knorm", 4), ("gdn_norm", 1), ("ml_norm", 1)):
                sp.dma_start(vecs[row:row + k, 0, :], T[name].rearrange("o (c p) -> (o c) p", p=P)).then_inc(vec_in, 16)
                row += k
            sp.dma_start(vecs[0:72, 1, :], T["gdn_conv"][0].rearrange("t (c p) -> (t c) p", p=P)).then_inc(vec_in, 16)
            sp.dma_start(vecs[0:2 * FC, 2:5, :], T["ffn_conv"][0].rearrange("t (c p) -> c t p", p=P)).then_inc(vec_in, 16)
            sp.dma_start(nalog, T["gdn_a_log"].rearrange("o h -> h o")).then_inc(vec_in, 16)
            sp.dma_start(dtb, T["gdn_dt_bias"].rearrange("o h -> h o")).then_inc(vec_in, 16)
            sp.dma_start(ib, T["ml_gate_bias"][0, 0:1, :].rearrange("o h -> h o")).then_inc(vec_in, 16)
            sp.dma_start(fb, T["ml_gate_bias"][0, 1:2, :].rearrange("o h -> h o")).then_inc(vec_in, 16)
            sp.wait_ge(gw_zero, 1)
            for at, c0, k in ((0, C_AB, GH), (32, C_AB + GH, GH), (64, C_IF, MH), (96, C_IF + MH, MH)):
                sp.dma_start(gw[:, :, at:at + k], W["w_in"][:, :, c0:c0 + k]).then_inc(gw_in, 16)
            sp.dma_start(lev[:, :, :], c[:, 3 * P:10 * P].rearrange("p (l n) -> p l n", l=7)).then_inc(lev_in, 16)
            for name, _, _, _, _ in STREAM:
                stream(name)

        @block.gpsimd
        def _(pool):
            pool.memset(gw[:, :, :], 0.0).then_inc(gw_zero, 1)
            pool.wait_ge(tin_e, 8)
            pool.dma_start(x_spill, xT[:, :, :].rearrange("p c s -> p (c s)")).then_inc(spill, 16)

            def store_gates(i):
                name, k = ("GA", i) if i < GA_UNITS else ("GB", i - GA_UNITS)
                pool.wait_ge(act_evac, evacuated(name, k)[1])
                pool.dma_start(g_spill[:, i * 2 * SEQ:(i + 1) * 2 * SEQ], tmp[:, i % 2, 0:512]).then_inc(g_out[i % 2], 16)

            for i in range(GA_UNITS - 1):
                store_gates(i)
            pool.wait_ge(y_t, 3)
            c = T["shape_masks"]
            pool.dma_start(neg_mask, c[:, 10 * P:10 * P + 384]).then_inc(mask_in, 16)
            pool.dma_start(pos_mask, c[:, 10 * P + 384:10 * P + 768]).then_inc(mask_in, 16)
            for i in range(GA_UNITS - 1, GA_UNITS + GB_UNITS):
                store_gates(i)
            for par in range(2):
                pool.wait_ge(g_out[par], 16 * ((GA_UNITS + GB_UNITS + 1 - par) // 2))
            pool.wait_ge(ml_y, 2)
            pool.wait_ge(sb_y, SH)
            pool.dma_start(gates[:, 0:2 * (GA_UNITS + GB_UNITS), :].rearrange("p c s -> p (c s)"), g_spill).then_inc(g_back, 16)
            pool.wait_ge(y_lo, 4)
            pool.wait_ge(spill, 16)
            pool.dma_start(xT[:, :, :].rearrange("p c s -> p (c s)"), x_spill).then_inc(back, 16)
            pool.wait_ge(dve_evac, evacuated("BR", 7)[1])
            pool.dma_start(mem_tm, T["mem"][0].rearrange("(a p) d -> p a d", p=P)).then_inc(mem_in, 16)
            pool.wait_ge(dve_evac, evacuated("XO", 7)[1])
            pool.wait_ge(back, 16)
            pool.dma_start(x_spill, xT[:, :, :].rearrange("p c s -> p (c s)")).then_inc(spill, 16)
            pool.wait_ge(half_used, 2 * last_unit("UP") + 2)
            pool.wait_ge(spill, 32)
            pool.dma_start(x_back[:, :, :].rearrange("p c s -> p (c s)"), x_spill).then_inc(back, 16)
            for c in range(D // CW):
                pool.wait_ge(ot_e, c + 1)
                pool.dma_start(out[0].rearrange("(a p) d -> p a d", p=P)[:, :, c * CW:(c + 1) * CW],
                               o_tm[:, :, c * CW:(c + 1) * CW]).then_inc(stored, 16)
            pool.wait_ge(stored, 16 * (D // CW))

        def each_unit(eng, name, fn, start=0, stop=None):
            u0, n = FIRST[name], COUNT[name] if stop is None else stop
            i = start
            while i < n:
                u, pairs = u0 + i, (n - i) // 2
                if u % 2 == 0 and pairs > 1:
                    with eng.Fori(0, pairs) as r:
                        for j in range(2):
                            fn(r * 2 + (i + j), j, r + u // 2)
                    i += 2 * pairs
                else:
                    fn(i, u % 2, u // 2)
                    i += 1

        kind_of = {n: k for n, _, _, _, k in STREAM}

        def halves(tile, kind, half, slot):
            if kind == TM_:
                return tile[:, slot, half * (KC // 2) * CW:(half + 1) * (KC // 2) * CW]
            k = DG if kind == DOWN else KC
            return tile[:, slot, 0:k * CW].rearrange("p (k n) -> p k n", n=CW)[:, :, half * P:(half + 1) * P]

        def split_out(tile, kind, half):
            if kind == TM_:
                return tile[:, half, :]
            k = DG if kind == DOWN else KC
            return tile[:, half, 0:k * P].rearrange("p (k n) -> p k n", n=P)

        def mb(i):
            return bank[4 + i % 4]

        def mb6(i):
            return bank[2 + i % 6]

        @block.scalar
        def _(act):
            def copy(out_, in_, func=ACT.Copy, **kw):
                return nc.scalar.activation(out_, in_, func, **kw)

            def hi_half(name, i, par, hp, half):
                act.wait_ge(raw_full[par], hp * 16 + 16)
                if not (isinstance(hp, int) and 2 * hp + par == 0):
                    act.wait_ge(half_used, hp * 4 + (2 * par + half - 1))
                copy(split_out(w_hi, kind_of[name], half), halves(raw, kind_of[name], half, par)).then_inc(hi_ready, 1)

            def hi(name, i, par, hp):
                for half in range(2):
                    hi_half(name, i, par, hp, half)

            def first(name):
                hi(name, 0, FIRST[name] % 2, FIRST[name] // 2)

            def beside(m):
                hi_half(*half_of(m + 1))
                name, i, par, hp, _ = half_of(m - 2 if m >= 2 else 0)
                if m >= 2 and m % 2 == 0 and EVAC[name] == "act":
                    evac_unit(name, i, par, hp)

            def evac_unit(name, i, par, hp):
                act.wait_ge(half_used, hp * 4 + (2 * par + 2))
                b = bank[par]
                strips = lambda t: t[:, bass.ds(i * 2, 2), :].rearrange("p c s -> p (c s)")
                if name == "BV":
                    for a in range(TT):
                        last = copy(v_b[:, a, 2 * i:2 * i + 2, 0:DK],
                                    bank[par + 2 * a][:, :].rearrange("p (x h d) -> p x h d", x=2, h=2)[:, 0])
                elif name == "CV":
                    for a in range(TT):
                        last = copy(v_c[:, a, i * CW:(i + 1) * CW], bank[par + 2 * a][:, 0:CW])
                elif name == "V":
                    for a in range(TT):
                        last = copy(v_tm[:, a, bass.ds(i * CW, CW)], bank[par + 2 * a][:, 0:CW])
                elif name in ("GA", "GB"):
                    k = i + (GA_UNITS if name == "GB" else 0)
                    if k < 2:
                        act.wait_ge(row_v, ROW_V)
                    else:
                        act.wait_ge(g_out[k % 2], 16 * (k // 2))
                    last = copy(tmp[:, k % 2, 0:512], b[:, :], ACT.Sigmoid)
                elif name == "GC":
                    last = copy(gates[:, bass.ds(i * 2 + 2 * (GA_UNITS + GB_UNITS), 2), :].rearrange("p c s -> p (c s)"), b[:, :], ACT.Sigmoid)
                else:
                    to, func = {"A": (proj[:, 0:18, :], ACT.Copy), "Z": (zs, ACT.Silu), "BQK": (qk_b, ACT.Copy),
                                "BO": (o_b, ACT.Sigmoid), "CQK": (qk_c, ACT.Copy),
                                "K": (kT, ACT.Copy), "Q": (qT, ACT.Copy)}[name]
                    last = copy(strips(to), b[:, :], func)
                last.then_inc(act_evac, 1)

            def evac_last(name):
                u = last_unit(name)
                evac_unit(name, COUNT[name] - 1, u % 2, u // 2)

            def rest(name, start=1, stop=None):
                def unit(i, par, hp):
                    hi(name, i, par, hp)
                    if EVAC[name] == "act":
                        evac_unit(name, i - 1, 1 - par, hp if par else hp - 1)
                each_unit(act, name, unit, start, stop)

            def transposed(k, to, gs):
                for g in gs:
                    act.wait_ge(tin_t, 8 * k + g + 1)
                    copy(to[:, 4 * (g % 4):4 * (g % 4) + 4, (g // 4) * P:(g // 4 + 1) * P],
                         mb(g)[:, :].rearrange("p (c s) -> p c s", c=4)).then_inc(tin_e, 1)

            def squares(k, src, c):
                if c >= 2:
                    act.wait_ge(n_ss, 4 * k + c - 1)
                copy(tmp[:, c % 2, :], src[:, 4 * c:4 * c + 4, :].rearrange("p c s -> p (c s)"), ACT.Square).then_inc(n_sq, 1)

            def root(k):
                act.wait_ge(n_stat, 2 * k + 1)
                copy(rstd[:, :], rstd[:, :], ACT.Sqrt).then_inc(n_rt, 1)

            def upper_part(k, gain, dst, c):
                act.wait_ge(n_n, 4 * k + c + 1)
                for j in range(4):
                    last = copy(dst[:, 0, 4 * c + j, :], tmp[:, c % 2, j * SEQ:(j + 1) * SEQ], scale=gain[:, 4 * c + j:4 * c + j + 1])
                last.then_inc(n_hi, 1)

            def norm_beside(k, m, src, gain, dst):
                beside(m)
                if k == 1:
                    act.wait_ge(m_lo, COUNT["BR"])
                    act.wait_ge(tin_e, 16)
                else:
                    act.wait_ge(n_lo, 4 * k)
                    act.wait_ge(dve_evac, evacuated("WO", 7)[1])
                squares(k, src, 0)
                squares(k, src, 1)
                beside(m + 1)
                squares(k, src, 2)
                squares(k, src, 3)
                beside(m + 2)
                root(k)
                beside(m + 3)
                upper_part(k, gain, dst, 0)
                upper_part(k, gain, dst, 1)
                beside(m + 4)
                upper_part(k, gain, dst, 2)
                upper_part(k, gain, dst, 3)

            transposed(0, xT, range(8))
            first("A")
            act.wait_ge(set_up, 2)
            act.wait_ge(tin_e, 8)
            for c in range(4):
                squares(0, xT, c)
            root(0)
            for c in range(4):
                upper_part(0, g_mix, x_hl, c)
            beside(1)
            act.wait_ge(gw_in, 64)
            copy(gw_hi[:, :, :], gw[:, :, :]).then_inc(gw_h, 1)
            for m in range(2, 7):
                beside(m)

            ra, rb, ri, rf, t0, t1 = (tmp[0:GH if j < 2 or j == 4 else MH, j // 4, (j % 4) * SEQ:(j % 4 + 1) * SEQ] for j in range(6))
            act.wait_ge(row_v, 4)
            copy(rb, rb, ACT.Sigmoid).then_inc(row_a, 1)
            nc.scalar.preload_act_table_set("natural_log_exp_and_others")
            copy(t0, ra, ACT.Abs).then_inc(row_a, 1)
            copy(t1, rf, ACT.Abs).then_inc(row_a, 1)
            act.wait_ge(row_a, 3)
            copy(t0, t0, ACT.Exp, scale=-1.0).then_inc(row_a, 1)
            copy(t1, t1, ACT.Exp, scale=-1.0).then_inc(row_a, 1)
            copy(nalog, nalog, ACT.Exp).then_inc(row_a, 1)
            beside(7)
            act.wait_ge(row_a, 6)
            copy(t0, t0, ACT.Ln, bias=1.0).then_inc(row_a, 1)
            copy(t1, t1, ACT.Ln, bias=1.0).then_inc(row_a, 1)
            for m in range(8, 15):
                beside(m)

            def conv_silu(j):
                act.wait_ge(cv, 24 * (j + 1))
                copy(conv[:, 6 * j:6 * j + 6, :], conv[:, 6 * j:6 * j + 6, :], ACT.Silu).then_inc(cs, 1)

            act.wait_ge(col_e, 2)
            copy(eg.rearrange("p (a h) -> p a h", a=TT), cols[:, :, 32:32 + GH], ACT.Exp).then_inc(col_a, 1)
            copy(tail.rearrange("p (a h) -> p a h", a=TT), cols[:, :, 64:64 + GH], ACT.Exp).then_inc(col_a, 1)
            copy(emn.rearrange("p (a h) -> p a h", a=TT), colm[:, :, :], ACT.Exp, scale=-1.0).then_inc(col_a, 1)
            nc.scalar.preload_act_table_set("silu_and_others")
            for m in (15, 16, 17):
                beside(m)
            conv_silu(0)
            for m in (18, 19, 20):
                beside(m)
            conv_silu(1)
            for m in (21, 22, 23):
                beside(m)
            conv_silu(2)

            def tm_even(g):
                act.wait_ge(tm_t, g + 1)
                copy(tm[:, :, 2 * g:2 * g + 2, :].rearrange("p a c d -> p c a d"),
                     mb6(g)[:, :].rearrange("p (c a d) -> p c a d", c=2, a=TT)).then_inc(tm_ea, 1)

            m = first_half("GA")
            beside(m)
            tm_even(0)
            tm_even(2)
            beside(m + 1)
            tm_even(4)
            beside(m + 2)
            tm_even(6)
            tm_even(8)
            beside(m + 3)
            act.wait_ge(l2_v, 3)
            copy(ss, ss, ACT.Sqrt).then_inc(l2_a, 1)
            act.wait_ge(dec_v, 12)
            copy(S_L, S_L, ACT.Exp, scale=-1.0).then_inc(dec_a, 1)
            beside(m + 4)
            for g in range(6):
                act.wait_ge(qk_t, g + 1)
                copy(conv[:, 2 * g:2 * g + 2, :].rearrange("p c s -> p (c s)"), mb6(g)[:, :]).then_inc(qk_e, 1)
            beside(m + 5)
            beside(m + 6)
            m += 7
            for l in range(7):
                beside(m)
                for g in range(3):
                    act.wait_ge(z_t, 3 * l + g + 1)
                    if l and g == 0:
                        act.wait_ge(d_t, 6 * l)
                    copy(S_Z[:, 4 * g:4 * g + 4, :].rearrange("p c s -> p (c s)"), bank[5 + g][:, :]).then_inc(z_e, 1)
                beside(m + 1)
                m += 2
            beside(m)
            for g, k in ((0, 4), (1, 2)):
                act.wait_ge(w_t, g + 1)
                nc.scalar.mul(S_Z[:, 4 * g:4 * g + k, :].rearrange("p c s -> p (c s)"), bank[4 + g][:, 0:k * P], -1.0).then_inc(w_e, 1)
            beside(m + 1)
            for g, k in ((0, 4), (1, 2)):
                act.wait_ge(s_t, g + 1)
                copy(S_Z[:, 6 + 4 * g:6 + 4 * g + k, :].rearrange("p c s -> p (c s)"), bank[6 + g][:, 0:k * P]).then_inc(s_e, 1)
            for g, k in ((0, 4), (1, 2)):
                act.wait_ge(qd_t, g + 1)
                copy(tm[:, 0, 4 * g:4 * g + k, :], bank[2 + g][:, 0:k * P].rearrange("p (c d) -> p c d", d=P)).then_inc(qd_e, 1)
            beside(m + 2)
            beside(m + 3)
            act.wait_ge(a_v, 12)
            copy(S_L, S_L, ACT.Exp).then_inc(a_a, 1)
            beside(m + 4)
            for g in range(3):
                act.wait_ge(o_t, g + 1)
                copy(S_T[:, 4 * g:4 * g + 4, :].rearrange("p c s -> p (c s)"), bank[(6, 7, 2)[g]][:, :]).then_inc(o_e, 1)
            beside(m + 5)
            act.wait_ge(yn_v, 3)
            copy(ss[:, 0:12], ss[:, 0:12], ACT.Sqrt).then_inc(yn_a, 1)
            beside(m + 6)
            assert m + 7 == first_half("BQK")

            beside(first_half("BQK"))
            rest("BQK")
            first("BV")
            evac_last("BQK")
            rest("BV")
            first("BO")
            evac_last("BV")
            rest("BO")

            def ml_exp(h):
                act.wait_ge(ml_v, 2 * h + 2)
                copy(ml_x[:, h, :], ml_x[:, h, :], ACT.Exp, scale=-1.0).then_inc(ml_a, 1)

            def ml_num(h):
                act.wait_ge(ml_n, h + 1)
                copy(num[:, :, h, :], bank[(4, 5, 6, 7)[h]][:, 0:258].rearrange("p (a d) -> p a d", a=TT)).then_inc(ml_ne, 1)

            m = first_half("CQK")
            hi_half(*half_of(m))
            beside(m)
            ml_exp(0)
            ml_exp(1)
            act.wait_ge(y_e, 3)
            beside(m + 1)
            beside(m + 2)
            ml_num(0)
            ml_num(1)
            ml_exp(2)
            beside(m + 3)
            beside(m + 4)
            ml_exp(3)
            beside(m + 5)
            ml_num(2)
            ml_num(3)
            beside(m + 6)
            act.wait_ge(ml_h, 7)
            copy(ss[:, 0:8], ss[:, 0:8], ACT.Sqrt).then_inc(ml_ha, 1)
            for j in range(7, 13):
                beside(m + j)
            rest("CV")

            def sb_soft(h):
                act.wait_ge(sb_zv, h + 1)
                copy(sb_s[:, h, :], sb_z[:, h, :], ACT.Abs).then_inc(sb_a, 1)
                act.wait_ge(sb_a, 3 * h + 1)
                copy(sb_s[:, h, :], sb_s[:, h, :], ACT.Exp, scale=-1.0).then_inc(sb_a, 1)
                act.wait_ge(sb_a, 3 * h + 2)
                copy(sb_s[:, h, :], sb_s[:, h, :], ACT.Ln, bias=1.0).then_inc(sb_a, 1)

            m = first_half("GB")
            hi_half(*half_of(m))
            for j in range(3):
                beside(m + j)
                nc.scalar.preload_act_table_set("natural_log_exp_and_others")
                sb_soft(2 * j)
                sb_soft(2 * j + 1)
            beside(m + 3)
            for h in range(SH):
                act.wait_ge(sb_x, h + 1)
                copy(sb_z[:, h, :], sb_z[:, h, :], ACT.Exp).then_inc(sb_e, 1)
            beside(m + 4)
            beside(m + 5)
            for h in range(SH):
                act.wait_ge(sb_o, h + 1)
                copy(yT[:, GH + MH + h, :], mb6(h + 2)[:, 0:SEQ]).then_inc(sb_y, 1)
            beside(m + 6)

            act.wait_ge(ml_y, 2)
            act.wait_ge(sb_y, SH)
            rest("GC")
            hi_half(*half_of(first_half("BR")))
            act.wait_ge(half_used, first_half("BR"))
            for c in range(4):
                copy(x_hl[:, 0, 4 * c:4 * c + 4, :], yT[:, 4 * c:4 * c + 4, :]).then_inc(y_hi, 1)
            beside(first_half("BR"))

            def merged_hi(i, par):
                act.wait_ge(br_m, i + 1)
                copy(m_hl[:, 0, bass.ds(i * 2, 2), :].rearrange("p c s -> p (c s)"), tmp[:, par, 0:512]).then_inc(m_hi, 1)

            def br_unit(i, par, hp):
                hi("BR", i, par, hp)
                merged_hi(i - 1, 1 - par)
            each_unit(act, "BR", br_unit, 1)
            first("WO")
            merged_hi(COUNT["BR"] - 1, last_unit("BR") % 2)
            rest("WO", 1, 4)
            m = first_half("WO", 4)
            hi_half(*half_of(m))
            beside(m)
            transposed(1, memT, range(4))
            beside(m + 1)
            transposed(1, memT, range(4, 8))
            norm_beside(1, m + 2, memT, g_mem, mem_hl)
            beside(m + 7)
            m = first_half("K")
            beside(m)
            norm_beside(2, m + 1, xT, g_xa, x_hl)
            beside(m + 6)
            rest("K", 4)
            m = first_half("Q")
            hi_half(*half_of(m))
            for j in range(XH + 1):
                beside(m + j)
                if j == 0:
                    act.wait_ge(n_lo, 12)
                    act.wait_ge(act_evac, evacuated("K", 7)[1])
                if j < XH:
                    if j >= 2:
                        act.wait_ge(xk_t, j - 1)
                    copy(tmp[:, j % 2, :], kT[:, 4 * j:4 * j + 4, :].rearrange("p c s -> p (c s)"), ACT.Square).then_inc(xk_s, 1)
                if j:
                    act.wait_ge(xk_v, 3 * j - 2)
                    copy(rstd[:, :], rstd[:, :], ACT.Sqrt).then_inc(xk_a, 1)
            beside(m + 5)
            beside(m + 6)
            rest("Q", 4)
            def query_squares(h):
                if h >= 2:
                    act.wait_ge(xq_t, h - 1)
                copy(tmp[:, h % 2, :], qT[:, 4 * h:4 * h + 4, :].rearrange("p c s -> p (c s)"), ACT.Square).then_inc(xq_s, 1)

            def output_hi(c):
                act.wait_ge(xo_t, c + 1)
                copy(x_hl[:, 0, 2 * c:2 * c + 2, :].rearrange("p c s -> p (c s)"), mb(c)[:, :]).then_inc(xo_h, 1)

            m = first_half("V")
            hi_half(*half_of(m))
            beside(m)
            act.wait_ge(act_evac, evacuated("Q", 7)[1])
            act.wait_ge(xk_t, XH)
            query_squares(0)
            query_squares(1)
            beside(m + 1)
            query_squares(2)
            query_squares(3)
            beside(m + 2)
            act.wait_ge(xq_v, 1)
            copy(xss, xss, ACT.Sqrt).then_inc(xq_a, 1)
            nc.scalar.preload_act_table_set("natural_log_exp_and_others")
            for p in range(XH):
                beside(m + 3 + p)
                for a in range(TT):
                    j = 2 * p + a
                    act.wait_ge(xl_v, 2 * j + 2)
                    copy(prob[:, a, p, :], mb(j)[:, 0:SEQ], ACT.Exp, bias=xmx[:, j:j + 1], scale=xss[:, j:j + 1],
                         accum_out=xsum[:, j:j + 1]).then_inc(xl_a, 1)
            for p in range(2):
                beside(m + 7 + p)
                for h in (2 * p, 2 * p + 1):
                    act.wait_ge(xp_t, h + 1)
                    copy(probT[:, 0:TT, h, :], mb(h)[:, :].rearrange("p (m s) -> p m s", m=TT)).then_inc(xp_e, 1)
            for j, cs_ in ((9, (0, 1)), (10, (2, 3)), (11, (4,)), (12, ()), (13, (5,)), (14, ()), (15, (6,)), (16, (7,))):
                beside(m + j)
                for c in cs_:
                    output_hi(c)

            def residual_squares(i, par):
                act.wait_ge(dve_evac, i + evacuated("XO", 0)[1])
                if not isinstance(i, int) or i >= 2:
                    act.wait_ge(x_ss, i - 1)
                copy(tmp[:, par, 0:512], xT[:, bass.ds(i * 2, 2), :].rearrange("p c s -> p (c s)"), ACT.Square).then_inc(x_sq, 1)

            def xo_unit(i, par, hp):
                hi("XO", i, par, hp)
                residual_squares(i - 1, 1 - par)
            each_unit(act, "XO", xo_unit, 1, 3)
            each_unit(act, "XO", xo_unit, 3)
            hi_half(*half_of(first_half("UP")))
            residual_squares(COUNT["XO"] - 1, last_unit("XO") % 2)
            root(3)
            hi_half(*half_of(first_half("UP") + 1))
            for c in range(4):
                upper_part(3, g_ffn, x_hl, c)
            nc.scalar.preload_act_table_set("silu_and_others")

            def silu_gate(j):
                act.wait_ge(dve_evac, j * 2 + evacuated("UP", 0)[1])
                copy(tmp[:, 0, 0:512], tmp[:, 0, 0:512], ACT.Silu).then_inc(f_s, 1)

            def product_hi(j):
                act.wait_ge(f_p, j + 1)
                copy(act_hl[:, 0, bass.ds(j * 2, 2), :].rearrange("p c s -> p (c s)"), tmp[:, 1, 512:1024]).then_inc(f_h, 1)

            (p0, h0), (p1, h1) = slot_of("UP", 0), slot_of("UP", 1)
            hi("UP", 1, p1, h1)
            silu_gate(0)
            act.wait_ge(spill, 32)
            with act.Fori(1, FC // 2) as j:
                hi("UP", 2 * j, p0, j + h0)
                hi("UP", 2 * j + 1, p1, j + h1)
                product_hi(j - 1)
                silu_gate(j)
            first("DN")
            product_hi(FC // 2 - 1)

            for g in range(1, NDG):
                hi("DN", g, *slot_of("DN", g))
            with act.Fori(1, D // CW) as c:
                for g in range(NDG):
                    par, h0 = slot_of("DN", g)
                    hi("DN", g, par, c * (NDG // 2) + h0)
                act.wait_ge(ot_t, c)
                copy(o_tm[:, :, bass.ds((c - 1) * CW, CW)].rearrange("p a (x d) -> p a x d", x=2),
                     bank[6][:, :].rearrange("p (a x d) -> p a x d", a=TT, x=2)).then_inc(ot_e, 1)
            act.wait_ge(ot_t, D // CW)
            copy(o_tm[:, :, D - CW:D].rearrange("p a (x d) -> p a x d", x=2),
                 bank[6][:, :].rearrange("p (a x d) -> p a x d", a=TT, x=2)).then_inc(ot_e, 1)

        class Count:

            def __init__(self, eng, sem_):
                self.eng, self.sem, self.n = eng, sem_, 0

            def __call__(self, ins):
                ins.then_inc(self.sem, 1)
                self.n += 1

            def settle(self, back=0):
                self.eng.wait_ge(self.sem, self.n - back)

        @block.vector
        def _(dve):
            v = nc.vector
            tt = v.tensor_tensor
            bc = lambda t, shape: t.to_broadcast(shape)

            def lo_half(name, i, par, hp, half):
                dve.wait_ge(hi_ready, hp * 4 + (2 * par + half + 1))
                kind = kind_of[name]
                tt(split_out(w_lo, kind, half), halves(raw, kind, half, par),
                   split_out(w_hi, kind, half).bitcast(f32), ALU.subtract).then_inc(lo_ready, 1)

            def lo(name, i, par, hp):
                for half in range(2):
                    lo_half(name, i, par, hp, half)

            def first(name):
                lo(name, 0, FIRST[name] % 2, FIRST[name] // 2)

            def add_residual(name, i, par, hp):
                dve.wait_ge(half_used, hp * 4 + (2 * par + 2))
                x2 = xT[:, bass.ds(i * 2, 2), :].rearrange("p c s -> p (c s)")
                tt(x2, bank[par][:, :], x2, ALU.add).then_inc(dve_evac, 1)

            def beside(m):
                lo_half(*half_of(m + 1))
                name, i, par, hp, _ = half_of(m - 2 if m >= 2 else 0)
                if m >= 2 and m % 2 == 0 and name in ("WO", "XO"):
                    add_residual(name, i, par, hp)

            def rest(name, start=1, stop=None):
                def unit(i, par, hp):
                    lo(name, i, par, hp)
                    if name in ("WO", "XO"):
                        add_residual(name, i - 1, 1 - par, hp if par else hp - 1)
                each_unit(dve, name, unit, start, stop)

            def mean(k):
                dve.wait_ge(*((n_ss, 4 * k + 4) if k < 3 else (x_ss, COUNT["XO"])))
                v.tensor_scalar(rstd[:, :], bank[7][:, 0:SEQ], 1.0 / D, EPS, ALU.mult, ALU.add).then_inc(n_stat, 1)

            def inverse(k):
                dve.wait_ge(n_rt, k + 1)
                v.reciprocal(rstd[:, :], rstd[:, :]).then_inc(n_stat, 1)
                dve.wait_ge(n_stat, 2 * k + 2)

            def normed(k, src, c):
                if c >= 2:
                    dve.wait_ge(n_lo, 4 * k + c - 1)
                tt(tmp[:, c % 2, :].rearrange("p (c s) -> p c s", c=4), src[:, 4 * c:4 * c + 4, :],
                   bc(rstd[:, :].unsqueeze(1), [P, 4, SEQ]), ALU.mult).then_inc(n_n, 1)

            def lower_part(k, gain, dst, c):
                dve.wait_ge(n_hi, 4 * k + c + 1)
                for j in range(4):
                    last = v.scalar_tensor_tensor(dst[:, 1, 4 * c + j, :], tmp[:, c % 2, j * SEQ:(j + 1) * SEQ],
                                                  gain[:, 4 * c + j:4 * c + j + 1], dst[:, 0, 4 * c + j, :].bitcast(f32),
                                                  ALU.mult, ALU.subtract)
                last.then_inc(n_lo, 1)

            def norm(k, src, gain, dst):
                mean(k)
                inverse(k)
                for c in range(4):
                    normed(k, src, c)
                    if c:
                        lower_part(k, gain, dst, c - 1)
                lower_part(k, gain, dst, 3)

            def norm_beside(k, m, src, gain, dst):
                beside(m)
                beside(m + 1)
                mean(k)
                beside(m + 2)
                inverse(k)
                normed(k, src, 0)
                normed(k, src, 1)
                beside(m + 3)
                lower_part(k, gain, dst, 0)
                lower_part(k, gain, dst, 1)
                normed(k, src, 2)
                normed(k, src, 3)
                beside(m + 4)
                lower_part(k, gain, dst, 2)
                lower_part(k, gain, dst, 3)

            v.memset(ones[:, :], 1.0).then_inc(set_up, 1)
            dve.wait_ge(vec_t, 1)
            v.tensor_copy(vec1[:, :], bank[4][:, 0:74])
            v.tensor_copy(vec2[:, :, :].rearrange("p t c -> p (t c)"), bank[4][:, 74:146])
            v.tensor_copy(vec3[:, :, :].rearrange("p t c -> p (t c)"), bank[4][:, 146:410]).then_inc(set_up, 1)
            first("A")
            dve.wait_ge(set_up, 2)
            norm(0, xT, g_mix, x_hl)
            beside(1)
            dve.wait_ge(gw_h, 1)
            tt(gw_lo[:, :, :], gw[:, :, :], gw_hi[:, :, :].bitcast(f32), ALU.subtract).then_inc(gw_l, 1)
            for m in range(2, 6):
                beside(m)

            ra, rb, ri, rf, t0, t1, rg, rl = (tmp[0:GH if j in (0, 1, 4, 6) else MH, j // 4, (j % 4) * SEQ:(j % 4 + 1) * SEQ]
                                              for j in range(8))
            rv = Count(dve, row_v)
            dve.wait_ge(row_mm, 1)
            dve.wait_ge(n_lo, 4)
            rv(v.tensor_scalar(ra, bank[4][0:GH, 0:SEQ], dtb, None, ALU.add))
            rv(v.tensor_copy(rb, bank[4][32:32 + GH, 0:SEQ]))
            rv(v.tensor_scalar(ri, bank[4][64:64 + MH, 0:SEQ], ib, None, ALU.add))
            rv(v.tensor_scalar(rf, bank[4][96:96 + MH, 0:SEQ], fb, None, ALU.add))
            rv(v.memset(rt[:, :], 0.0))
            for m in range(6, 9):
                beside(m)
            dve.wait_ge(row_a, 8)
            rv.settle()
            rv(v.scalar_tensor_tensor(rg, ra, 0.0, t0, ALU.max, ALU.add))
            rv(v.scalar_tensor_tensor(rl, rf, 0.0, t1, ALU.min, ALU.subtract))
            rv.settle()
            rv(v.tensor_scalar(rg, rg, nalog, -1.0, ALU.mult, ALU.mult))
            rv.settle()
            for a in range(TT):
                sl = slice(a * P, a * P + P)
                rv(v.tensor_tensor_scan(g_row[:, sl], ones[0:GH, :], rg[:, sl], 0.0, ALU.mult, ALU.add))
            rv(v.tensor_tensor_scan(t1[:, 0:P], ones[0:MH, :], rl[:, 0:P], 0.0, ALU.mult, ALU.add))
            rv.settle()
            rv(v.tensor_tensor_scan(t1[:, P:SEQ], ones[0:MH, :], rl[:, P:SEQ], t1[:, P - 1:P], ALU.mult, ALU.add))
            rv.settle()
            beside(9)
            rv(tt(ri, ri, t1, ALU.subtract))
            rv.settle()
            rv(v.tensor_tensor_scan(m_row[:, :], ri, ri, 0.0, ALU.max, ALU.max))
            rv.settle()
            rv(tt(rt2[:, :], t1, m_row[:, :], ALU.add))
            rv(v.tensor_copy(rt[0:GH, :], rb))
            rv(v.tensor_copy(rt[32:32 + GH, :], g_row[:, :]))
            for a in range(TT):
                sl = slice(a * P, a * P + P)
                rv(v.tensor_scalar(rt[64:64 + GH, sl], g_row[:, sl], g_row[:, a * P + P - 1:a * P + P], -1.0, ALU.subtract, ALU.mult))
            rv(v.tensor_copy(rt[96:96 + MH, :], ri))
            assert rv.n == ROW_V
            beside(10)

            c_ = Count(dve, cv)

            def tap_of(j, d):
                tap = GDN_TAPS - 1 - d
                if d == 0:
                    dve.wait_ge(act_evac, evacuated("A", 3 * j + 2)[1])
                for c in range(6 * j, 6 * j + 6):
                    if d:
                        c_.settle(5)
                        c_(v.scalar_tensor_tensor(conv[:, c, d:], proj[:, c, 0:SEQ - d], vec2[:, tap, c:c + 1], conv[:, c, d:],
                                                  ALU.mult, ALU.add))
                    else:
                        c_(v.tensor_scalar(conv[:, c, :], proj[:, c, :], vec2[:, tap, c:c + 1], None, ALU.mult))

            for d in range(3):
                tap_of(0, d)
                beside(11 + d)
            dve.wait_ge(row_t, 1)
            v.tensor_copy(cols[:, :, :].rearrange("p a n -> p (a n)"), bank[5][:, 0:SEQ]).then_inc(col_e, 1)
            v.tensor_copy(colm[:, :, :].rearrange("p a n -> p (a n)"), bank[5][:, SEQ:SEQ + TT * MH]).then_inc(col_e, 1)
            beside(14)
            dve.wait_ge(col_a, 1)
            dve.wait_ge(col_e, 2)
            tt(beg, eg[:, GH:2 * GH], cols[:, 1, 0:GH], ALU.mult).then_inc(col_e, 1)
            tap_of(0, 3)
            beside(15)
            for d in range(GDN_TAPS):
                tap_of(1, d)
                beside(16 + d)
            for d in range(GDN_TAPS):
                tap_of(2, d)
                beside(20 + d)
            c_.settle()

            def tm_odd(g):
                dve.wait_ge(tm_t, g + 1)
                v.tensor_copy(tm[:, :, 2 * g:2 * g + 2, :].rearrange("p a c d -> p c a d"),
                              mb6(g)[:, :].rearrange("p (c a d) -> p c a d", c=2, a=TT)).then_inc(tm_ed, 1)

            m = first_half("GA")
            tm_odd(1)
            beside(m)
            tm_odd(3)
            tm_odd(5)
            beside(m + 1)
            tm_odd(7)
            dve.wait_ge(tm_ea, 3)
            dve.wait_ge(tm_ed, 3)
            l2 = Count(dve, l2_v)
            dve.wait_ge(gw_l, 1)
            sq = slabf[:, 12 * P:36 * P].rearrange("p (a c d) -> p a c d", a=TT, d=P)
            ssv = ss.rearrange("p (a c) -> p a c", a=TT)
            l2(tt(sq, tm[:, :, 0:12, :], tm[:, :, 0:12, :], ALU.mult))
            l2.settle()
            l2(v.tensor_reduce(ssv, sq, AX.X, ALU.add))
            l2.settle()
            l2(v.tensor_scalar(ss, ss, EPS, None, ALU.add))
            beside(m + 2)
            for j in range(3):
                dve.wait_ge(dec_t, j + 1)
                for x in range(2):
                    for a in range(TT):
                        h = 2 * j + x
                        v.tensor_scalar(S_L[:, a * GH + h, :], mb6(j + 3)[:, x * SEQ + a * P:x * SEQ + a * P + P],
                                        cols[:, a, 32 + h:33 + h], 0.0, ALU.subtract, ALU.max).then_inc(dec_v, 1)
            dve.wait_ge(l2_a, 1)
            l2(v.reciprocal(ss, ss))
            l2.settle()
            l2(v.tensor_scalar(ssv[:, :, 0:GH], ssv[:, :, 0:GH], DK ** -0.5, None, ALU.mult))
            l2.settle()
            l2(tt(tm[:, :, 0:12, :], tm[:, :, 0:12, :], bc(ssv.unsqueeze(3), [P, TT, 12, P]), ALU.mult))
            bshape = [P, 12, P]
            cc = Count(dve, c_v)
            beside(m + 3)
            cc(v.tensor_copy(S_T, bc(ident[:, :].unsqueeze(1), bshape)))
            cc(v.tensor_copy(S_U, bc(ident[:, :].unsqueeze(1), bshape)))
            beside(m + 4)
            dve.wait_ge(dec_a, 1)
            for n in range(12):
                a, h = n // GH, n % GH
                dve.wait_ge(kk_t, n // 4 + 1)
                v.scalar_tensor_tensor(S_L[:, n, :], bank[2 + n // 4][:, n % 4 * P:n % 4 * P + P], cols[:, a, h:h + 1], S_L[:, n, :],
                                       ALU.mult, ALU.mult).then_inc(l_v, 1)
            beside(m + 5)
            dve.wait_ge(lev_in, 16)
            dve.wait_ge(l_v, 12)
            cc(tt(S_C, S_L, bc(lev[:, 0, :].unsqueeze(1), bshape), ALU.mult))
            beside(m + 6)
            m += 7
            kv = Count(dve, kv_v)
            hs = [P, GH, P]
            for l in range(7):
                if l == 0:
                    dve.wait_ge(qk_t, 6)
                    dve.wait_ge(tm_ea, 5)
                    dve.wait_ge(tm_ed, 4)
                    kv(tt(tm[:, :, 12:18, :], tm[:, :, 12:18, :], bc(cols[:, :, 0:GH].unsqueeze(3), [P, TT, GH, P]), ALU.mult))
                elif l == 1:
                    kv(tt(tm[:, 0, 6:12, :], tm[:, 0, 6:12, :], bc(tail[:, 0:GH].unsqueeze(2), hs), ALU.mult))
                    dve.wait_ge(col_e, 3)
                    kv(tt(tm[:, 1, 6:12, :], tm[:, 1, 6:12, :], bc(beg.unsqueeze(2), hs), ALU.mult))
                elif l == 2:
                    kv(tt(tm[:, 1, 0:6, :], tm[:, 1, 0:6, :], bc(eg[:, GH:2 * GH].unsqueeze(2), hs), ALU.mult))
                if l < 6:
                    dve.wait_ge(z_t, 3 * l + 3)
                    cc(tt(S_C, S_L, bc(lev[:, l + 1, :].unsqueeze(1), bshape), ALU.mult))
                beside(m)
                for g in range(3):
                    dve.wait_ge(d_t, 6 * l + 2 * g + 2)
                    for x, S_X in enumerate((S_T, S_U)):
                        t = S_X[:, 4 * g:4 * g + 4, :].rearrange("p c s -> p (c s)")
                        v.scalar_tensor_tensor(t, bank[2 + 2 * g + x][:, :], -1.0, t, ALU.mult, ALU.add).then_inc(d_e, 1)
                beside(m + 1)
                m += 2
            for g, k in ((0, 4), (1, 2)):
                dve.wait_ge(u_t, g + 1)
                v.tensor_copy(S_C[:, 4 * g:4 * g + k, :].rearrange("p c s -> p (c s)"), bank[2 + g][:, 0:k * P]).then_inc(u_e, 1)
            beside(m)
            beside(m + 1)
            av = Count(dve, a_v)
            cc.settle()
            for j in range(3):
                dve.wait_ge(a_t, j + 1)
                for x in range(2):
                    for a in range(TT):
                        h = 2 * j + x
                        av(v.tensor_scalar(S_L[:, a * GH + h, :], bank[4 + j][:, x * SEQ + a * P:x * SEQ + a * P + P],
                                           cols[:, a, 32 + h:33 + h], 0.0, ALU.subtract, ALU.min))
            beside(m + 2)
            for g, k in ((0, 4), (1, 2)):
                dve.wait_ge(vn_t, g + 1)
                v.tensor_copy(S_C[:, 6 + 4 * g:6 + 4 * g + k, :].rearrange("p c s -> p (c s)"),
                              bank[4 + g][:, 0:k * P]).then_inc(vn_e, 1)
            dve.wait_ge(a_a, 1)
            av(tt(S_L, S_L, bc(upper[:, :].unsqueeze(1), bshape), ALU.mult))
            av.settle()
            for g in range(3):
                dve.wait_ge(a_t, 4 + g)
                t = S_L[:, 4 * g:4 * g + 4, :].rearrange("p c s -> p (c s)")
                av(tt(t, bank[(7, 2, 3)[g]][:, :], t, ALU.mult))
            beside(m + 3)
            dve.wait_ge(o_e, 3)
            yn = Count(dve, yn_v)
            yn(tt(S_L, S_T, S_T, ALU.mult))
            yn.settle()
            yn(v.tensor_reduce(ss[:, 0:12], S_L, AX.X, ALU.add))
            yn.settle()
            yn(v.tensor_scalar(ss[:, 0:12], ss[:, 0:12], 1.0 / DK, EPS, ALU.mult, ALU.add))
            beside(m + 4)
            dve.wait_ge(yn_a, 1)
            yn(v.reciprocal(ss[:, 0:12], ss[:, 0:12]))
            yn.settle()
            yn(tt(S_T, S_T, bc(ss[:, 0:12].unsqueeze(2), bshape), ALU.mult))
            beside(m + 5)
            dve.wait_ge(spill, 16)
            dve.wait_ge(act_evac, evacuated("Z", 2)[1])
            for j in range(3):
                dve.wait_ge(y_t, j + 1)
                v.scalar_tensor_tensor(yT[:, 2 * j:2 * j + 2, :].rearrange("p c s -> p (c s)"), bank[3 + j][:, :], g_gdn,
                                       zs[:, 2 * j:2 * j + 2, :].rearrange("p c s -> p (c s)"), ALU.mult, ALU.mult).then_inc(y_e, 1)
            v.memset(v_b[:, :, :, DK:DK + 1], 1.0).then_inc(set_up, 1)

            beside(m + 6)

            beside(first_half("BQK"))
            rest("BQK")
            first("BV")
            rest("BV")
            first("BO")
            rest("BO")

            def ml_weights(h):
                b = bank[4 + 2 * ML_PAIR[h]], bank[5 + 2 * ML_PAIR[h]]
                dve.wait_ge(ml_s, h + 1)
                v.scalar_tensor_tensor(ml_x[:, h, 0:SEQ], b[0][:, 0:SEQ], cols[:, 0, 96 + h:97 + h], pos_mask[:, 0:SEQ],
                                       ALU.subtract, ALU.add).then_inc(ml_v, 1)
                v.scalar_tensor_tensor(ml_x[:, h, SEQ:384], b[0][:, P:SEQ], cols[:, 1, 96 + h:97 + h], pos_mask[:, SEQ:384],
                                       ALU.subtract, ALU.add).then_inc(ml_v, 1)
                dve.wait_ge(ml_a, h + 1)
                v.scalar_tensor_tensor(ml_x[:, h, :], b[1][:, 0:384], DK ** -0.5, ml_x[:, h, :], ALU.mult, ALU.mult).then_inc(ml_w, 1)

            m = first_half("CQK")
            lo_half(*half_of(m))
            dve.wait_ge(mask_in, 32)
            beside(m)
            ml_weights(0)
            ml_weights(1)
            beside(m + 1)
            beside(m + 2)
            ml_weights(2)
            beside(m + 3)
            beside(m + 4)
            ml_weights(3)
            beside(m + 5)
            dve.wait_ge(ml_ne, MH)
            mh = Count(dve, ml_h)
            den3 = den.rearrange("p (a h) -> p a h", a=TT)
            mh(v.scalar_tensor_tensor(den3, num[:, :, :, DK], -1.0, num[:, :, :, DK], ALU.mult, ALU.max))
            mh.settle()
            mh(tt(den, den, emn, ALU.max))
            mh.settle()
            mh(v.reciprocal(den, den))
            mh.settle()
            hv = num[:, :, :, 0:DK]
            nshape = [P, TT, MH, DK]
            mh(tt(hv, hv, bc(den3.unsqueeze(3), nshape), ALU.mult))
            beside(m + 6)
            mh.settle()
            sq = slabf[:, 0:8 * DK].rearrange("p (a h d) -> p a h d", a=TT, h=MH)
            mh(tt(sq, hv, hv, ALU.mult))
            mh.settle()
            s3 = ss[:, 0:8].rearrange("p (a h) -> p a h", a=TT)
            mh(v.tensor_reduce(s3, sq, AX.X, ALU.add))
            mh.settle()
            mh(v.tensor_scalar(ss[:, 0:8], ss[:, 0:8], 1.0 / DK, EPS, ALU.mult, ALU.add))
            beside(m + 7)
            dve.wait_ge(ml_ha, 1)
            mh(v.reciprocal(ss[:, 0:8], ss[:, 0:8]))
            mh.settle()
            mh(tt(hv, hv, bc(s3.unsqueeze(3), nshape), ALU.mult))
            beside(m + 8)
            for j in range(2):
                dve.wait_ge(ml_t, j + 1)
                v.scalar_tensor_tensor(yT[:, GH + 2 * j:GH + 2 * j + 2, :].rearrange("p c s -> p (c s)"), bank[4 + j][:, :], g_ml,
                                       o_b[:, 2 * j:2 * j + 2, :].rearrange("p c s -> p (c s)"), ALU.mult, ALU.mult).then_inc(ml_y, 1)

            for j in range(9, 13):
                beside(m + j)
            rest("CV")

            m = first_half("GB")
            lo_half(*half_of(m))
            for h in range(SH):
                dve.wait_ge(sb_t, h + 1)
                v.scalar_tensor_tensor(sb_z[:, h, :], mb6(h + 2)[:, 0:384], DK ** -0.5, neg_mask, ALU.mult, ALU.add).then_inc(sb_zv, 1)
            for j in range(3):
                beside(m + j)
                for h in (2 * j, 2 * j + 1):
                    dve.wait_ge(sb_a, 3 * h + 3)
                    v.scalar_tensor_tensor(sb_s[:, h, :], sb_z[:, h, :], 0.0, sb_s[:, h, :], ALU.max, ALU.add).then_inc(sb_sp, 1)
            for h in range(SH):
                dve.wait_ge(sb_r, h + 1)
                tt(sb_z[:, h, :], sb_z[:, h, :], mb6(h + 2)[:, 0:384], ALU.subtract).then_inc(sb_x, 1)
            for j in range(3, 7):
                beside(m + j)

            rest("GC")
            lo_half(*half_of(first_half("BR")))
            for c in range(4):
                dve.wait_ge(y_hi, c + 1)
                tt(x_hl[:, 1, 4 * c:4 * c + 4, :], yT[:, 4 * c:4 * c + 4, :], x_hl[:, 0, 4 * c:4 * c + 4, :].bitcast(f32),
                   ALU.subtract).then_inc(y_lo, 1)
            beside(first_half("BR"))
            dve.wait_ge(act_evac, evacuated("GC", COUNT["GC"] - 1)[1])
            dve.wait_ge(g_back, 16)

            def merge(i, par, hp):
                dve.wait_ge(half_used, hp * 4 + (2 * par + 2))
                if not isinstance(i, int) or i >= 2:
                    dve.wait_ge(m_lo, i - 1)
                m0, m1 = tmp[:, par, 0:512], tmp[:, par, 512:1024]
                gate = lambda j: gates[:, bass.ds(i * 2 + j * KC, 2), :].rearrange("p c s -> p (c s)")
                tt(m0, bank[par][:, :], gate(0), ALU.mult)
                tt(m1, bank[2 + par][:, :], gate(1), ALU.mult).then_inc(br_c, 1)
                dve.wait_ge(br_c, i * 2 + 1)
                tt(m0, m0, m1, ALU.add).then_inc(br_c, 1)
                dve.wait_ge(br_c, i * 2 + 2)
                tt(m1, bank[4 + par][:, :], gate(2), ALU.mult).then_inc(dve_evac, 1)
                dve.wait_ge(dve_evac, i + 1)
                tt(m0, m0, m1, ALU.add).then_inc(br_m, 1)

            def merged_lo(i, par):
                dve.wait_ge(m_hi, i + 1)
                two = lambda j: m_hl[:, j, bass.ds(i * 2, 2), :].rearrange("p c s -> p (c s)")
                tt(two(1), tmp[:, par, 0:512], two(0).bitcast(f32), ALU.subtract).then_inc(m_lo, 1)

            def br_unit(i, par, hp):
                lo("BR", i, par, hp)
                if not isinstance(i, int) or i >= 2:
                    merged_lo(i - 2, par)
                merge(i - 1, 1 - par, hp if par else hp - 1)
            each_unit(dve, "BR", br_unit, 1, 2)
            each_unit(dve, "BR", br_unit, 2)
            first("WO")
            u = last_unit("BR")
            merged_lo(COUNT["BR"] - 2, 1 - u % 2)
            merge(COUNT["BR"] - 1, u % 2, u // 2)
            merged_lo(COUNT["BR"] - 1, u % 2)
            dve.wait_ge(back, 16)
            rest("WO", 1, 4)
            m = first_half("WO", 4)
            lo_half(*half_of(m))
            beside(m)
            beside(m + 1)
            norm_beside(1, m + 2, memT, g_mem, mem_hl)
            beside(m + 7)
            m = first_half("K")
            beside(m)
            norm_beside(2, m + 1, xT, g_xa, x_hl)
            beside(m + 6)
            rest("K", 4)
            m = first_half("Q")
            lo_half(*half_of(m))
            tt(gqk, gq, gk, ALU.mult).then_inc(set_up, 1)
            dve.wait_ge(set_up, 4)

            def scale_keys(h):
                dve.wait_ge(xk_a, h + 1)
                v.reciprocal(rstd[:, :], rstd[:, :]).then_inc(xk_v, 1)
                dve.wait_ge(xk_v, 3 * h + 2)
                for c in range(XC):
                    last = v.scalar_tensor_tensor(kT[:, 4 * h + c, :], kT[:, 4 * h + c, :], gqk[:, c:c + 1], rstd[:, :], ALU.mult, ALU.mult)
                last.then_inc(xk_v, 1)

            for j in range(XH + 2):
                if j >= 2:
                    scale_keys(j - 2)
                if 1 <= j <= XH:
                    dve.wait_ge(xk_t, j)
                    if j >= 2:
                        dve.wait_ge(xk_v, 3 * (j - 1))
                    v.tensor_scalar(rstd[:, :], bank[6 + (j - 1) % 2][:, 0:SEQ], 1.0 / XD, EPS, ALU.mult, ALU.add).then_inc(xk_v, 1)
                beside(m + j)
            beside(m + 6)
            rest("Q", 4)
            def scale_prob(j):
                h, a = j // 2, j % 2
                dve.wait_ge(xl_a, j + 1)
                v.reciprocal(xsum[:, j:j + 1], xsum[:, j:j + 1]).then_inc(xp_v, 1)
                dve.wait_ge(xp_v, 2 * j + 1)
                v.tensor_scalar(prob[:, a, h, :], prob[:, a, h, :], xsum[:, j:j + 1], None, ALU.mult).then_inc(xp_v, 1)

            def output_lo(c):
                dve.wait_ge(xo_h, c + 1)
                tt(x_hl[:, 1, 2 * c:2 * c + 2, :].rearrange("p c s -> p (c s)"), mb(c)[:, :],
                   x_hl[:, 0, 2 * c:2 * c + 2, :].rearrange("p c s -> p (c s)").bitcast(f32), ALU.subtract).then_inc(xo_l, 1)

            m = first_half("V")
            lo_half(*half_of(m))
            beside(m)
            beside(m + 1)
            dve.wait_ge(xq_t, XH)
            v.tensor_scalar(xss, bank[6][:, 0:8], 1.0 / XD, EPS, ALU.mult, ALU.add).then_inc(xq_v, 1)
            beside(m + 2)
            dve.wait_ge(xq_a, 1)
            v.reciprocal(xss, xss).then_inc(xq_v, 1)
            dve.wait_ge(xq_v, 2)
            v.tensor_scalar(xss, xss, XD ** -0.5, None, ALU.mult).then_inc(xq_v, 1)
            dve.wait_ge(xq_v, 3)
            for p in range(XH):
                for j in (2 * p, 2 * p + 1):
                    dve.wait_ge(xl_t, j + 1)
                    v.reduce_max(xmx[:, j:j + 1], mb(j)[:, 0:SEQ], AX.X).then_inc(xl_v, 1)
                    dve.wait_ge(xl_v, 2 * j + 1)
                    v.scalar_tensor_tensor(xmx[:, j:j + 1], xmx[:, j:j + 1], -1.0, xss[:, j:j + 1], ALU.mult, ALU.mult).then_inc(xl_v, 1)
                beside(m + 3 + p)
                scale_prob(2 * p)
                scale_prob(2 * p + 1)
            beside(m + 7)
            beside(m + 8)
            for j, cs_ in ((9, (0, 1)), (10, (2, 3)), (11, (4,)), (12, ()), (13, (5,)), (14, ()), (15, (6,)), (16, (7,))):
                for c in cs_:
                    output_lo(c)
                beside(m + j)
            rest("XO")
            lo_half(*half_of(first_half("UP")))
            u = last_unit("XO")
            add_residual("XO", 7, u % 2, u // 2)
            norm(3, xT, g_ffn, x_hl)
            lo_half(*half_of(first_half("UP") + 1))

            def taps(j, up, done):
                par, h0 = slot_of("UP", up)
                dve.wait_ge(half_used, j * 4 + (4 * h0 + 2 * par + 2))
                if not isinstance(j, int) or j:
                    dve.wait_ge(f_p, j)
                n = 0
                for d in range(FFN_TAPS):
                    for x in range(2):
                        o = tmp[:, 0, (2 * up + x) * SEQ + d:(2 * up + x + 1) * SEQ]
                        b = bank[par][:, x * SEQ:(x + 1) * SEQ - d]
                        w = vec3[:, FFN_TAPS - 1 - d, bass.ds(j * 2 + (up * FC + x), 1)]
                        if d:
                            dve.wait_ge(done, j * 5 + (n - 1))
                            ins = v.scalar_tensor_tensor(o, b, w, o, ALU.mult, ALU.add)
                        else:
                            ins = v.tensor_scalar(o, b, w, None, ALU.mult)
                        n += 1
                        ins.then_inc(done if n < 6 else dve_evac, 1)

            def product(j):
                dve.wait_ge(f_s, j + 1)
                if not isinstance(j, int) or j:
                    dve.wait_ge(f_l, j)
                dve.wait_ge(dve_evac, j * 2 + (evacuated("UP", 1)[1]))
                tt(tmp[:, 1, 512:1024], tmp[:, 0, 0:512], tmp[:, 0, 512:1024], ALU.mult).then_inc(f_p, 1)

            def product_lo(j):
                dve.wait_ge(f_h, j + 1)
                two = lambda k: act_hl[:, k, bass.ds(j * 2, 2), :].rearrange("p c s -> p (c s)")
                tt(two(1), tmp[:, 1, 512:1024], two(0).bitcast(f32), ALU.subtract).then_inc(f_l, 1)

            (p0, h0), (p1, h1) = slot_of("UP", 0), slot_of("UP", 1)
            lo("UP", 1, p1, h1)
            taps(0, 0, f_c)
            with dve.Fori(1, FC // 2) as j:
                lo("UP", 2 * j, p0, j + h0)
                taps(j - 1, 1, f_g)
                product(j - 1)
                lo("UP", 2 * j + 1, p1, j + h1)
                taps(j, 0, f_c)
                product_lo(j - 1)
            first("DN")
            taps(FC // 2 - 1, 1, f_g)
            product(FC // 2 - 1)
            product_lo(FC // 2 - 1)

            for g in range(1, NDG):
                lo("DN", g, *slot_of("DN", g))
            dve.wait_ge(back, 32)
            dve.wait_ge(f_l, FC // 2)

            def finish(c, par):
                dve.wait_ge(half_used, c * (2 * NDG) + (2 * FIRST["DN"] + 2 * NDG))
                if not isinstance(c, int) or c >= 2:
                    dve.wait_ge(ot_t, c - 1)
                for x in range(2):
                    last = tt(tmp[:, par, x * SEQ:(x + 1) * SEQ], bank[par + 2 * x][:, 0:SEQ],
                              x_back[:, bass.ds(c * 2 + x, 1), :].rearrange("p c s -> p (c s)"), ALU.add)
                last.then_inc(dve_evac, 1)

            def down_pair(c, par):
                for g in range(NDG):
                    p, h0 = slot_of("DN", g)
                    lo("DN", g, p, c * (NDG // 2) + h0)
                    if g == 0:
                        finish(c - 1, 1 - par)

            down_pair(1, 1)
            down_pair(2, 0)
            down_pair(3, 1)
            with dve.Fori(2, 4) as r:
                down_pair(r * 2, 0)
                down_pair(r * 2 + 1, 1)
            finish(7, 1)

        @block.tensor
        def _(pe):
            mm = nc.tensor.matmul

            def three(o, w, x, start, stop):
                mm(o, w[0], x[0], start=start, stop=False)
                mm(o, w[0], x[1], start=False, stop=False)
                return mm(o, w[1], x[0], start=False, stop=stop)

            def wait_bank(name, i):
                if isinstance(i, int) and i < 2:
                    u = FIRST[name] + i - 2
                    if u < 0:
                        return
                    before = phase_of(u)
                    e, n = evacuated(before, u - FIRST[before])
                    pe.wait_ge(evac[e], n)
                else:
                    e, n = evacuated(name, 0)
                    pe.wait_ge(evac[e], i + (n - 2))

            def half_unit(name, i, par, hp, half, acts, ready=None):
                kind = kind_of[name]
                pe.wait_ge(lo_ready, hp * 4 + (2 * par + half + 1))
                if kind == TM_:
                    for k in range(KC // 2):
                        kk = half * (KC // 2) + k
                        w = [t[:, half, k * CW:(k + 1) * CW] for t in (w_hi, w_lo)]
                        for a in range(TT):
                            x = [acts[:, j, kk, a * P:(a + 1) * P] for j in range(2)]
                            last = three(bank[par + 2 * a][:, 0:CW], x, w, kk == 0, kk == KC - 1)
                else:
                    cuts = (0, GH, GH + MH, KC) if kind == BR else (0, KC)
                    for k in range(KC):
                        if ready and k % ready[2] == 0:
                            pe.wait_ge(ready[0], ready[1] + k // ready[2] + 1)
                        g = sum(k >= c for c in cuts) - 1
                        w = [t[:, half, k * P:(k + 1) * P] for t in (w_hi, w_lo)]
                        last = three(bank[par + 2 * g][:, half * SEQ:(half + 1) * SEQ], w, [acts[:, j, k, :] for j in range(2)],
                                     k == cuts[g], k + 1 == cuts[g + 1])
                last.then_inc(half_used, 1)

            def product_half(m, acts=x_hl, ready=None):
                name, i, par, hp, half = half_of(m)
                if half == 0:
                    wait_bank(name, i)
                half_unit(name, i, par, hp, half, acts, ready)

            def project(name, acts, start=0, stop=None, after=None):
                def unit(i, par, hp):
                    wait_bank(name, i)
                    for half in range(2):
                        half_unit(name, i, par, hp, half, acts)
                    if after:
                        after(i, par)
                stop = COUNT[name] if stop is None else stop
                if start < 2:
                    each_unit(pe, name, unit, start, min(2, stop))
                each_unit(pe, name, unit, max(2, start), stop)

            def transposes(k, src, gs):
                for g in gs:
                    if g >= 4:
                        pe.wait_ge(tin_e, 8 * k + g - 3)
                    for c in range(4):
                        cc = 4 * (g % 4) + c
                        last = nc.tensor.transpose(mb(g)[:, c * P:(c + 1) * P], src[:, g // 4, cc * P:(cc + 1) * P], ident[:, :])
                    last.then_inc(tin_t, 1)

            def sum_squares(k, cs_=range(4)):
                for c in cs_:
                    pe.wait_ge(n_sq, 4 * k + c + 1)
                    for j in range(4):
                        last = mm(bank[7][:, 0:SEQ], ones[:, :], tmp[:, c % 2, j * SEQ:(j + 1) * SEQ], start=c + j == 0, stop=c + j == 6)
                    last.then_inc(n_ss, 1)

            def norm_beside(k, m, acts):
                product_half(m, acts)
                sum_squares(k, (0, 1))
                product_half(m + 1, acts)
                sum_squares(k, (2, 3))
                for j in range(2, 5):
                    product_half(m + j, acts)

            pe.wait_ge(x_in, 16)
            pe.wait_ge(const_in, 48)
            transposes(0, x_tm, range(8))
            pe.wait_ge(vec_in, 16 * 14)
            pe.wait_ge(tin_e, 8)
            at = 0
            for i, k in ((0, 74), (1, 72), (2, 88), (3, 88), (4, 88)):
                last = nc.tensor.transpose(bank[4][:, at:at + k], vecs[0:k, i, :], ident[0:k, 0:k])
                at += k
            last.then_inc(vec_t, 1)
            pe.wait_ge(set_up, 1)
            sum_squares(0)
            product_half(0, x_hl, (n_lo, 0, 4))
            product_half(1)
            product_half(2)
            pe.wait_ge(gw_l, 1)
            pe.wait_ge(set_up, 2)
            for k in range(KC):
                last = three(bank[4][:, 0:SEQ], [t[:, k, :] for t in (gw_hi, gw_lo)], [x_hl[:, j, k, :] for j in range(2)],
                             k == 0, k == KC - 1)
            last.then_inc(row_mm, 1)
            for m in range(3, 14):
                product_half(m)
            pe.wait_ge(row_v, ROW_V)
            for a in range(TT):
                nc.tensor.transpose(bank[5][:, a * P:(a + 1) * P], rt[:, a * P:(a + 1) * P], ident[:, :])
                last = nc.tensor.transpose(bank[5][:, SEQ + a * MH:SEQ + (a + 1) * MH], rt2[:, a * P:(a + 1) * P], ident[0:MH, 0:MH])
            last.then_inc(row_t, 1)
            for m in range(14, first_half("GA")):
                product_half(m)

            def tm_transposes(gs):
                for g in gs:
                    pe.wait_ge(cs, (2 * g + 1) // 6 + 1)
                    if g >= 6:
                        pe.wait_ge(tm_ed if g % 2 else tm_ea, (g - 6) // 2 + 1)
                    for c in range(2):
                        for a in range(TT):
                            last = nc.tensor.transpose(mb6(g)[:, (2 * c + a) * P:(2 * c + a + 1) * P],
                                                       conv[:, 2 * g + c, a * P:(a + 1) * P], ident[:, :])
                    last.then_inc(tm_t, 1)

            def spread(b, h, row):
                n = row.shape[0]
                return mm(b, ident[0:n, h:h + 1].to_broadcast([n, P]), row, start=True, stop=True)

            def chunk_pairs(sem_, banks, rhs):
                for g in range(3):
                    for n in range(4 * g, 4 * g + 4):
                        a, h = n // GH, n % GH
                        last = mm(banks[g][:, n % 4 * P:n % 4 * P + P], conv[:, GH + h, a * P:(a + 1) * P],
                                  conv[:, rhs + h, a * P:(a + 1) * P], start=True, stop=True)
                    last.then_inc(sem_, 1)

            def group(o, lhs, rhs, ns):
                for i, n in enumerate(ns):
                    last = mm(o[:, i * P:(i + 1) * P], lhs(n), rhs(n), start=True, stop=True)
                return last

            m = first_half("GA")
            pe.wait_ge(col_e, 2)
            tm_transposes(range(3))
            product_half(m)
            tm_transposes(range(3, 6))
            product_half(m + 1)
            tm_transposes(range(6, 9))
            pe.wait_ge(tm_ed, 3)
            pe.wait_ge(tm_ea, 3)
            for j in range(3):
                for x in range(2):
                    last = spread(mb6(j + 3)[:, x * SEQ:(x + 1) * SEQ], 2 * j + x, g_row[:, :])
                last.then_inc(dec_t, 1)
            product_half(m + 2)
            product_half(m + 3)
            pe.wait_ge(l2_v, 6)
            pe.wait_ge(tm_ea, 5)
            pe.wait_ge(tm_ed, 4)
            pe.wait_ge(dec_v, 12)
            for g in range(6):
                for c in range(2):
                    for a in range(TT):
                        last = nc.tensor.transpose(mb6(g)[:, (2 * c + a) * P:(2 * c + a + 1) * P], tm[:, a, 2 * g + c, :], ident[:, :])
                last.then_inc(qk_t, 1)
            product_half(m + 4)
            pe.wait_ge(qk_e, 6)
            chunk_pairs(kk_t, bank[2:5], GH)
            product_half(m + 5)
            product_half(m + 6)
            m += 7
            for l in range(7):
                pe.wait_ge(c_v, 3 + l)
                pe.wait_ge(l_v, 12)
                if l:
                    pe.wait_ge(d_e, 6 * l)
                for g in range(3):
                    group(bank[5 + g], lambda n: S_C[:, n, :], lambda n: S_U[:, n, :], range(4 * g, 4 * g + 4)).then_inc(z_t, 1)
                product_half(m)
                for g in range(3):
                    pe.wait_ge(z_e, 3 * l + (g + 1 if g < 2 else 3))
                    ns = range(4 * g, 4 * g + 4)
                    group(bank[2 + 2 * g], lambda n: S_Z[:, n, :], lambda n: S_T[:, n, :], ns).then_inc(d_t, 1)
                    group(bank[3 + 2 * g], lambda n: S_T[:, n, :], lambda n: S_Z[:, n, :], ns).then_inc(d_t, 1)
                product_half(m + 1)
                m += 2

            two_groups = ((0, range(0, 4)), (1, range(4, 6)))
            pe.wait_ge(d_e, 42)
            pe.wait_ge(kv_v, 4)
            for g, hs in two_groups:
                group(bank[2 + g], lambda h: S_U[:, h, :], lambda h: tm[:, 0, 12 + h, :], hs).then_inc(u_t, 1)
            for g, hs in two_groups:
                group(bank[4 + g], lambda h: tm[:, 1, 6 + h, :], lambda h: S_U[:, 6 + h, :], hs).then_inc(w_t, 1)
            product_half(m)
            pe.wait_ge(u_e, 2)
            for g, hs in two_groups:
                group(bank[6 + g], lambda h: tm[:, 0, 6 + h, :], lambda h: S_C[:, h, :], hs).then_inc(s_t, 1)
            for g, hs in two_groups:
                for i, h in enumerate(hs):
                    last = nc.tensor.transpose(bank[2 + g][:, i * P:(i + 1) * P], tm[:, 1, h, :], ident[:, :])
                last.then_inc(qd_t, 1)
            product_half(m + 1)
            pe.wait_ge(w_e, 2)
            pe.wait_ge(s_e, 2)
            pe.wait_ge(qd_e, 2)
            for j in range(3):
                for x in range(2):
                    last = spread(bank[4 + j][:, x * SEQ:(x + 1) * SEQ], 2 * j + x, g_row[:, :])
                last.then_inc(a_t, 1)
            chunk_pairs(a_t, (bank[7], bank[2], bank[3]), 0)
            product_half(m + 2)
            pe.wait_ge(a_v, 8)
            for g, hs in two_groups:
                for i, h in enumerate(hs):
                    o = bank[4 + g][:, i * P:(i + 1) * P]
                    mm(o, S_U[:, 6 + h, :], tm[:, 1, 12 + h, :], start=True, stop=False)
                    last = mm(o, S_Z[:, h, :], S_Z[:, 6 + h, :], start=False, stop=True)
                last.then_inc(vn_t, 1)
            product_half(m + 3)
            pe.wait_ge(a_v, 16)
            pe.wait_ge(vn_e, 2)
            for g in range(3):
                for n in range(4 * g, 4 * g + 4):
                    o = bank[(6, 7, 2)[g]][:, n % 4 * P:n % 4 * P + P]
                    if n >= GH:
                        mm(o, tm[:, 0, n - GH, :], S_Z[:, n, :], start=True, stop=False)
                    last = mm(o, S_L[:, n, :], S_C[:, n, :], start=n < GH, stop=True)
                last.then_inc(o_t, 1)
            product_half(m + 4)
            product_half(m + 5)

            def to_features(b, j, src, sem_):
                for x in range(2):
                    for a in range(TT):
                        last = nc.tensor.transpose(b[:, x * SEQ + a * P:x * SEQ + (a + 1) * P], src(2 * j + x, a), ident[:, :])
                last.then_inc(sem_, 1)

            pe.wait_ge(yn_v, 5)
            for j in range(3):
                to_features(bank[3 + j], j, lambda h, a: S_T[:, a * GH + h, :], y_t)
            product_half(m + 6)

            for name in ("BQK", "BV", "BO"):
                project(name, x_hl)

            def scores(b, k, q):
                mm(b[:, 0:SEQ], k[:, 0:P], q, start=True, stop=True)
                return mm(b[:, SEQ:384], k[:, P:SEQ], q[:, P:SEQ], start=True, stop=True)

            def ml_scores(h):
                spread(bank[4 + 2 * ML_PAIR[h]][:, 0:SEQ], h, m_row[:, :])
                scores(bank[5 + 2 * ML_PAIR[h]], qk_b[:, MH + h, :], qk_b[:, h, :]).then_inc(ml_s, 1)

            def ml_numerator(h):
                b = bank[4 + h]
                mm(b[:, 0:129], ml_x[:, h, 0:P], v_b[:, 0, h, :], start=True, stop=True)
                mm(b[:, 129:258], ml_x[:, h, P:SEQ], v_b[:, 0, h, :], start=True, stop=False)
                mm(b[:, 129:258], ml_x[:, h, SEQ:384], v_b[:, 1, h, :], start=False, stop=True).then_inc(ml_n, 1)

            m = first_half("CQK")
            pe.wait_ge(act_evac, evacuated("BV", 1)[1])
            pe.wait_ge(set_up, 3)
            pe.wait_ge(y_e, 3)
            product_half(m)
            ml_scores(0)
            ml_scores(1)
            product_half(m + 1)
            product_half(m + 2)
            pe.wait_ge(ml_w, 2)
            ml_numerator(0)
            ml_numerator(1)
            ml_scores(2)
            product_half(m + 3)
            product_half(m + 4)
            pe.wait_ge(ml_ne, 2)
            ml_scores(3)
            product_half(m + 5)
            pe.wait_ge(ml_w, 4)
            ml_numerator(2)
            ml_numerator(3)
            for j in (6, 7, 8):
                product_half(m + j)
            pe.wait_ge(ml_h, 9)
            for j in range(2):
                to_features(bank[4 + j], j, lambda h, a: num[:, a, h, 0:DK], ml_t)
            for j in (9, 10, 11):
                product_half(m + j)
            project("CV", x_hl)

            m = first_half("GB")
            pe.wait_ge(ml_y, 2)
            pe.wait_ge(act_evac, evacuated("CV", 2)[1])
            for h in range(SH):
                scores(mb6(h + 2), qk_c[:, SH + h, :], qk_c[:, h, :]).then_inc(sb_t, 1)
            for j in range(3):
                product_half(m + j)
            for h in range(SH):
                pe.wait_ge(sb_sp, h + 1)
                b = mb6(h + 2)
                mm(b[:, 0:SEQ], later[:, :], sb_s[:, h, 0:SEQ], start=True, stop=False)
                mm(b[:, P:SEQ], ones[:, :], sb_s[:, h, SEQ:384], start=False, stop=True)
                mm(b[:, SEQ:384], later[:, :], sb_s[:, h, SEQ:384], start=True, stop=True).then_inc(sb_r, 1)
            product_half(m + 3)
            product_half(m + 4)
            for h in range(SH):
                pe.wait_ge(sb_e, h + 1)
                b = mb6(h + 2)
                mm(b[:, 0:SEQ], v_c[:, 0, h * DK:(h + 1) * DK], sb_z[:, h, 0:SEQ], start=True, stop=False)
                mm(b[:, P:SEQ], v_c[:, 1, h * DK:(h + 1) * DK], sb_z[:, h, SEQ:384], start=False, stop=True).then_inc(sb_o, 1)
            product_half(m + 5)

            project("GC", x_hl)
            m = first_half("BR")
            pe.wait_ge(sb_y, SH)
            product_half(m, x_hl, (y_lo, 0, 4))
            product_half(m + 1)
            project("BR", x_hl, 1)
            pe.wait_ge(m_lo, COUNT["BR"])
            project("WO", m_hl, 0, 4)
            m = first_half("WO", 4)
            pe.wait_ge(mem_in, 16)
            transposes(1, mem_tm, range(4))
            product_half(m, m_hl)
            transposes(1, mem_tm, range(4, 8))
            product_half(m + 1, m_hl)
            pe.wait_ge(tin_e, 16)
            norm_beside(1, m + 2, m_hl)
            product_half(m + 7, m_hl)
            m = first_half("K")
            pe.wait_ge(n_lo, 8)
            product_half(m, mem_hl)
            norm_beside(2, m + 1, mem_hl)
            project("K", mem_hl, 3)
            m = first_half("Q")
            pe.wait_ge(n_lo, 12)
            product_half(m)
            for h in range(XH):
                pe.wait_ge(xk_s, h + 1)
                if h >= 2:
                    pe.wait_ge(xk_v, 3 * (h - 2) + 1)
                for c in range(XC):
                    last = mm(bank[6 + h % 2][:, 0:SEQ], ones[:, :], tmp[:, h % 2, c * SEQ:(c + 1) * SEQ], start=c == 0, stop=c == XC - 1)
                last.then_inc(xk_t, 1)
                product_half(m + h + 1)
            product_half(m + 5)
            project("Q", x_hl, 3)
            def query_sums(h):
                pe.wait_ge(xq_s, h + 1)
                for a in range(TT):
                    for c in range(XC):
                        last = mm(bank[6][:, 2 * h + a:2 * h + a + 1], tmp[:, h % 2, c * SEQ + a * P:c * SEQ + (a + 1) * P],
                                  ones[:, 0:1], start=c == 0, stop=c == XC - 1)
                last.then_inc(xq_t, 1)

            def logits(j):
                h, a = j // 2, j % 2
                for c in range(XC):
                    last = mm(mb(j)[:, 0:SEQ], qT[:, 4 * h + c, a * P:(a + 1) * P], kT[:, 4 * h + c, :], start=c == 0, stop=c == XC - 1)
                last.then_inc(xl_t, 1)

            def prob_transposes(h):
                pe.wait_ge(xp_v, 4 * h + 4)
                for mk in range(TT):
                    for a in range(TT):
                        last = nc.tensor.transpose(mb(h)[:, mk * SEQ + a * P:mk * SEQ + (a + 1) * P],
                                                   prob[:, a, h, mk * P:(mk + 1) * P], ident[:, :])
                last.then_inc(xp_t, 1)

            def output(c):
                h = c // 2
                pe.wait_ge(act_evac, evacuated("V", c)[1])
                if c >= 4:
                    pe.wait_ge(xo_l, c - 3)
                for x in range(2):
                    f = 2 * c + x
                    for mk in range(TT):
                        last = mm(mb(c)[:, x * SEQ:(x + 1) * SEQ], v_tm[:, mk, f * P:(f + 1) * P], probT[:, mk, h, :],
                                  start=mk == 0, stop=mk == TT - 1)
                last.then_inc(xo_t, 1)

            m = first_half("V")
            pe.wait_ge(xk_v, 3 * XH)
            product_half(m, mem_hl)
            query_sums(0)
            query_sums(1)
            product_half(m + 1, mem_hl)
            query_sums(2)
            query_sums(3)
            product_half(m + 2, mem_hl)
            for p in range(XH):
                if p == 1:
                    pe.wait_ge(xq_v, 1)
                elif p > 1:
                    pe.wait_ge(xl_a, 2 * p - 2)
                logits(2 * p)
                logits(2 * p + 1)
                product_half(m + 3 + p, mem_hl)
            for p in range(2):
                pe.wait_ge(xl_a, 6 + 2 * p)
                prob_transposes(2 * p)
                prob_transposes(2 * p + 1)
                product_half(m + 7 + p, mem_hl)
            pe.wait_ge(xp_e, 2)
            output(0)
            output(1)
            product_half(m + 9, mem_hl)
            pe.wait_ge(xp_e, 4)
            output(2)
            output(3)
            product_half(m + 10, mem_hl)
            output(4)
            product_half(m + 11, mem_hl)
            product_half(m + 12, mem_hl)
            output(5)
            product_half(m + 13, mem_hl)
            product_half(m + 14, mem_hl)
            output(6)
            product_half(m + 15, mem_hl)
            output(7)
            m = first_half("XO")
            product_half(m, x_hl, (xo_l, 0, 2))
            product_half(m + 1)

            def residual_sums(i, par):
                pe.wait_ge(x_sq, i + 1)
                first_, last_ = isinstance(i, int) and i == 0, isinstance(i, int) and i == COUNT["XO"] - 1
                mm(bank[7][:, 0:SEQ], ones[:, :], tmp[:, par, 0:SEQ], start=first_, stop=False)
                mm(bank[7][:, 0:SEQ], ones[:, :], tmp[:, par, SEQ:2 * SEQ], start=False, stop=last_).then_inc(x_ss, 1)

            project("XO", x_hl, 1, after=lambda i, par: residual_sums(i - 1, 1 - par))
            residual_sums(COUNT["XO"] - 1, last_unit("XO") % 2)
            m = first_half("UP")
            product_half(m, x_hl, (n_lo, 12, 4))
            product_half(m + 1)
            project("UP", x_hl, 1)
            pe.wait_ge(f_l, FC // 2)
            def down_pair(c, par):
                if isinstance(c, int) and c < 2:
                    pe.wait_ge(dve_evac, evacuated("UP", COUNT["UP"] - 1)[1])
                else:
                    pe.wait_ge(dve_evac, c + (evacuated("DN", 0)[1] - 2))
                for g in range(NDG):
                    for half in range(2):
                        pe.wait_ge(lo_ready, c * (2 * NDG) + (2 * FIRST["DN"] + 2 * g + half + 1))
                        for k in range(DG):
                            w = [t[:, half, k * P:(k + 1) * P] for t in (w_hi, w_lo)]
                            x = [act_hl[:, j, g * DG + k, :] for j in range(2)]
                            last = three(bank[par + 2 * half][:, 0:SEQ], w, x, g + k == 0, g * DG + k == FC - 1)
                        last.then_inc(half_used, 1)
                    if g == 1 and not (isinstance(c, int) and c == 0):
                        finished(c - 1, 1 - par)

            def finished(c, par):
                pe.wait_ge(dve_evac, c + evacuated("DN", 0)[1])
                if not isinstance(c, int) or c >= 1:
                    pe.wait_ge(ot_e, c)
                for a in range(TT):
                    for x in range(2):
                        last = nc.tensor.transpose(bank[6][:, (2 * a + x) * P:(2 * a + x + 1) * P],
                                                   tmp[:, par, x * SEQ + a * P:x * SEQ + (a + 1) * P], ident[:, :])
                last.then_inc(ot_t, 1)

            down_pair(0, 0)
            down_pair(1, 1)
            with pe.Fori(1, 4) as r:
                down_pair(r * 2, 0)
                down_pair(r * 2 + 1, 1)
            finished(7, 1)


ROW_V = 20
ML_PAIR = (0, 1, 1, 0)

INPUTS = ['x', 'mem', 'norm_mix', 'w_in', 'gdn_conv', 'gdn_a_log', 'gdn_dt_bias', 'gdn_norm', 'ml_gate_bias', 'ml_norm', 'w_br',
          'w_out', 'norm_xa', 'norm_mem', 'xa_wq', 'xa_wkv', 'xa_wo', 'xa_qnorm', 'xa_knorm', 'norm_ffn', 'ffn_up', 'ffn_conv',
          'ffn_down']


def kernel(**inputs):
    import concourse.bacc as bacc
    from concourse.bass_utils import run_bass_kernel_spmd

    nc = bacc.Bacc("TRN2", target_bir_lowering=False, num_devices=1)
    arrays = {f"in_{n}": np.ascontiguousarray(inputs[n]) for n in INPUTS}
    arrays["in_shape_masks"] = shape_masks()
    T = {n[3:]: nc.dram_tensor(n, a.shape, mybir.dt.from_np(a.dtype), kind="ExternalInput").ap() for n, a in arrays.items()}
    out = nc.dram_tensor("out", (1, SEQ, D), mybir.dt.float32, kind="ExternalOutput").ap()
    build_program(nc, T, out)
    result = run_bass_kernel_spmd(nc, [arrays], core_ids=[0])
    return result.results[0]["out"]
```

```python
import math
from contextlib import ExitStack

import numpy as np
import concourse.bass as bass
from concourse import mybir

P = 128
SEQ, D = 256, 2048
TT = SEQ // P
KC = D // P
GH, MH, SH = 6, 4, 6
DK = 128
XH = 4
XD = D // XH
XC = XD // P
FF = 5632
FC = FF // P
CW = 256
GDN_TAPS, FFN_TAPS = 4, 3
EPS = 1e-6
BIG = 1e30

C_A = 0
C_AB = C_A + 3 * GH * DK
C_Z = C_AB + 2 * GH
C_QKB = C_Z + GH * DK
C_VB = C_QKB + 2 * MH * DK
C_IF = C_VB + MH * DK
C_O = C_IF + 2 * MH
C_QKC = C_O + MH * DK
C_VC = C_QKC + 2 * SH * DK
C_G = C_VC + SH * DK

FM, TM_, BR, DOWN = "feature-major", "token-major", "branches", "down"
DG = 11
NDG = FC // DG
G_PIECES = 4
GA_UNITS, GB_UNITS = 14, 4
STREAM = [
    ("A", "w_in", C_A, 9, FM), ("Z", "w_in", C_Z, 3, FM), ("GA", "w_in", C_G, GA_UNITS, FM),
    ("BQK", "w_in", C_QKB, 4, FM), ("BV", "w_in", C_VB, 2, TM_), ("BO", "w_in", C_O, 2, FM),
    ("CQK", "w_in", C_QKC, 6, FM), ("CV", "w_in", C_VC, 3, TM_), 
    ("GB", "w_in", C_G + GA_UNITS * CW, GB_UNITS, FM),
    ("GC", "w_in", C_G + (GA_UNITS + GB_UNITS) * CW, 3 * D // CW - GA_UNITS - GB_UNITS, FM),
    ("BR", "w_br", 0, 8, BR), ("WO", "w_out", 0, 8, FM),
    ("K", "xa_wkv", 0, 8, FM), ("Q", "xa_wq", 0, 8, FM), ("V", "xa_wkv", D, 8, TM_),
    ("XO", "xa_wo", 0, 8, FM), ("UP", "ffn_up", 0, 2 * FC // 2, FM), ("DN", "ffn_down", 0, 8 * NDG, DOWN),
]
FIRST, COUNT = {}, {}
_u = 0
for _n, _w, _c, _k, _kind in STREAM:
    FIRST[_n], COUNT[_n] = _u, _k
    _u += _k
UNITS = _u
EVAC = {n: "act" for n in ("A", "Z", "BQK", "BV", "BO", "CQK", "CV", "GA", "GB", "GC", "K", "V", "Q")}
EVAC.update({n: "dve" for n in ("BR", "WO", "XO", "UP", "DN")})


def slot_of(name, k):
    return (FIRST[name] + k) % 2, (FIRST[name] + k) // 2


def last_unit(name):
    return FIRST[name] + COUNT[name] - 1


def evacuated(name, i):
    engine, n = EVAC[name], 0
    for m, _, _, k, kind in STREAM:
        per = NDG if kind == DOWN else 1
        if m == name:
            return engine, n + i // per + 1
        if EVAC[m] == engine:
            n += k // per
    raise ValueError(name)


def half_of(m):
    u, half = divmod(m, 2)
    name = phase_of(u)
    return name, u - FIRST[name], u % 2, u // 2, half


def first_half(name, i=0):
    return 2 * (FIRST[name] + i)


def phase_of(u):
    for n, _, _, k, _ in STREAM:
        if FIRST[n] <= u < FIRST[n] + k:
            return n
    raise ValueError(u)


def shape_masks():
    r, c = np.arange(P)[:, None], np.arange(P)[None, :]
    ident = (r == c)
    levels = [((r >> (l + 1)) == (c >> (l + 1))) & ((r >> l) % 2 == 1) & ((c >> l) % 2 == 0) for l in range(7)]
    upper = r <= c
    later = r >= c
    t = np.arange(SEQ)[None, :]
    strict = np.concatenate([r < t, r < c], 1)
    incl = np.concatenate([r <= t, r <= c], 1)
    return np.concatenate([ident, upper, later] + levels + [np.where(strict, 0, -BIG), np.where(incl, 0, BIG)],
                          1).astype(np.float32)


def build_program(nc, T, out):
    f32, f32r = mybir.dt.float32, mybir.dt.float32r
    ALU, ACT, AX = mybir.AluOpType, mybir.ActivationFunctionType, mybir.AxisListType
    ctx = ExitStack()
    with ctx:
        def sb(name, shape, dt=f32, stack=ctx):
            return stack.enter_context(nc.sbuf_tensor(name, shape, dt))

        def sem(name):
            return ctx.enter_context(nc.semaphore(name))

        raw = sb("raw", [P, 2, KC * CW])
        w_hi = sb("w_hi", [P, 2, KC * P], f32r)
        w_lo = sb("w_lo", [P, 2, KC * P], f32r)
        e_scope = ExitStack()
        x_back = sb("x_back", [P, KC, SEQ], f32, e_scope)
        o_tm = sb("o_tm", [P, TT, D], f32, e_scope)
        e_scope.close()
        p_scope = ExitStack()
        prob = sb("prob", [P, TT, XH, SEQ], f32, p_scope)
        p_scope.close()
        x_hl = sb("x_hl", [P, 2, KC, SEQ], f32r)
        tmp = sb("tmp", [P, 2, 1024])
        ident = sb("ident", [P, P])
        upper = sb("upper", [P, P])
        later = sb("later", [P, P])
        ones = sb("ones", [P, P])
        rstd = sb("rstd", [P, SEQ])
        vec1 = sb("vec1", [P, 74])
        vec2 = sb("vec2", [P, GDN_TAPS, 18])
        vec3 = sb("vec3", [P, FFN_TAPS, 2 * FC])
        cols = sb("cols", [P, TT, P])
        colm = sb("colm", [P, TT, MH])
        small = sb("small", [P, 128])
        r_scope = ExitStack()
        xT = sb("xT", [P, KC, SEQ], f32, r_scope)
        yT = xT

        a_scope = ExitStack()
        A = lambda name, shape, dt=f32: sb(name, shape, dt, a_scope)
        proj = A("proj", [P, 24, SEQ])
        conv = A("conv", [P, 18, SEQ])
        lev = A("lev", [P, 7, P])
        rt = A("rt", [P, SEQ])
        rt2 = A("rt2", [MH, SEQ])
        g_row = A("g_row", [GH, SEQ])
        m_row = A("m_row", [MH, SEQ])
        s_scope = ExitStack()
        slab = sb("slab", [P, 5, 12, P], f32, s_scope)
        s_scope.close()
        w_scope = ExitStack()
        gw = sb("gw", [P, KC, P], f32, w_scope)
        gw_hi = sb("gw_hi", [P, KC, P], f32r, w_scope)
        gw_lo = sb("gw_lo", [P, KC, P], f32r, w_scope)
        vecs = sb("vecs", [P, 5, P], f32, w_scope)
        w_scope.close()
        a_scope.close()
        b_scope = ExitStack()
        gates = sb("gates", [P, 3 * KC, SEQ], f32, b_scope)
        y_hl = sb("y_hl", [P, 2, KC, SEQ], f32r, b_scope)
        b_scope.close()
        c_scope = ExitStack()
        mem_hl = sb("mem_hl", [P, 2, KC, SEQ], f32r, c_scope)
        kT = sb("kT", [P, KC, SEQ], f32, c_scope)
        v_tm = sb("v_tm", [P, TT, D], f32, c_scope)
        qT = sb("qT", [P, KC, SEQ], f32, c_scope)
        c_scope.close()
        r_scope.close()
        d_scope = ExitStack()
        act_hl = sb("act_hl", [P, 2, FC, SEQ], f32r, d_scope)
        d_scope.close()

        bank = [ctx.enter_context(nc.psum_tensor(f"bank{i}", [P, 512], f32)) for i in range(8)]

        x_tm = proj[:, 0:16, :].rearrange("p (a c) s -> p a (c s)", a=TT)
        mem_tm = gates[:, 16:32, :].rearrange("p (a c) s -> p a (c s)", a=TT)
        memT = gates[:, 32:48, :]
        tm = proj[:, 0:18, :].rearrange("p (a s) (b d) -> p a (s b) d", a=TT, d=P)
        zs = proj[:, 18:24, :]
        qk_b, o_b, qk_c = proj[:, 0:8, :], proj[:, 8:12, :], proj[:, 12:24, :]
        convf = conv[:, :, :].rearrange("p a b -> p (a b)")
        v_b = convf[:, 0:TT * MH * 129].rearrange("p (a h d) -> p a h d", a=TT, h=MH)
        num = convf[:, 1032:2064].rearrange("p (a h d) -> p a h d", a=TT, h=MH)
        v_c = convf[:, 2064:3600].rearrange("p (a n) -> p a n", a=TT)
        slabf = slab[:, :, :, :].rearrange("p a b c -> p (a b c)")
        S_L, S_C, S_Z, S_T, S_U = (slab[:, i, :, :] for i in range(5))
        ml_x = slabf[:, 0:1536].rearrange("p (h n) -> p h n", h=MH)
        sb_z = slabf[:, 1536:3840].rearrange("p (h n) -> p h n", h=SH)
        sb_s = slabf[:, 3840:6144].rearrange("p (h n) -> p h n", h=SH)
        neg_mask, pos_mask = slabf[:, 6144:6528], slabf[:, 6528:6912]
        probT = kT[:, :, :].rearrange("p (h m) s -> p m h s", h=XH)
        xg = qT
        sq_sum = kT[:, 0:2, :].rearrange("p c s -> p (c s)")
        x_spill = nc.dram_tensor("x_spill", [P, KC * SEQ], f32).ap()
        g_spill = nc.dram_tensor("g_spill", [P, (GA_UNITS + GB_UNITS) * 2 * SEQ], f32).ap()

        ss = small[:, 0:24]
        eg, tail, beg = small[:, 24:36], small[:, 36:48], small[:, 48:54]
        nalog, dtb = small[0:GH, 54:55], small[0:GH, 55:56]
        ib, fb = small[0:MH, 56:57], small[0:MH, 57:58]
        den, emn = small[:, 60:68], small[:, 68:76]
        xss, xmx, xsum = small[:, 76:84], small[:, 84:92], small[:, 92:100]
        gqk = small[:, 100:104]

        g_mix, g_xa, g_mem, g_ffn = (vec1[:, 16 * i:16 * i + 16] for i in range(4))
        gq, gk = vec1[:, 64:68], vec1[:, 68:72]
        g_gdn, g_ml = vec1[:, 72:73], vec1[:, 73:74]

        raw_full = [sem("raw_full0"), sem("raw_full1")]
        hi_ready = sem("hi_ready")
        lo_ready = sem("lo_ready")
        half_used = sem("half_used")
        act_evac, dve_evac = sem("act_evac"), sem("dve_evac")
        evac = {"act": act_evac, "dve": dve_evac}
        x_in = [sem("x_in0"), sem("x_in1")]
        causal_in = sem("causal_in")
        mem_in, const_in, lev_in, mask_in = (sem(n) for n in ("mem_in", "const_in", "lev_in", "mask_in"))
        vec_in, gw_zero, gw_in, spill, back, stored = (sem(n) for n in ("vec_in", "gw_zero", "gw_in", "spill", "back", "stored"))
        g_out = [sem("g_out0"), sem("g_out1")]
        g_back = sem("g_back")
        tin_t, tin_e, tin_d = sem("tin_t"), sem("tin_e"), sem("tin_d")
        vec_t = sem("vec_t")
        n_add = sem("norm_add")
        n_sq, n_ss, n_stat, n_rt, n_n, n_hi, n_lo = (sem("norm_" + n) for n in ("sq", "ss", "stat", "rt", "n", "hi", "lo"))
        x_sq, x_add, x_ss, x_g = (sem("residual_" + n) for n in ("sq", "add", "ss", "g"))
        set_up = sem("set_up")
        gw_h, gw_l, row_mm, row_v, row_a, row_t, col_e, col_a = (sem(n) for n in (
            "gw_h", "gw_l", "row_mm", "row_v", "row_a", "row_t", "col_e", "col_a"))
        cv, cs, tm_t, tm_ea, tm_ed, l2_v, l2_a, qk_t, qk_e, kv_v, qd_t, qd_e = (sem(n) for n in (
            "conv_v", "conv_silu", "tm_t", "tm_ea", "tm_ed", "l2_v", "l2_a", "qk_t", "qk_e", "kv_v", "qd_t", "qd_e"))
        dec_t, dec_v, dec_a, kk_t, l_v, z_t, z_e, d_t, d_e, c_v = (sem("gdn_" + n) for n in (
            "dec_t", "dec_v", "dec_a", "kk_t", "l_v", "z_t", "z_e", "d_t", "d_e", "c_v"))
        u_t, u_e, w_t, w_e, s_t, s_e, a_t, a_v, a_a, vn_t, vn_e, o_t, o_e, yn_v, yn_a, y_t, y_e = (sem("gdn_" + n) for n in (
            "u_t", "u_e", "w_t", "w_e", "st_t", "st_e", "at_t", "at_v", "at_a", "vn_t", "vn_e", "o_t", "o_e", "yn_v", "yn_a",
            "y_t", "y_e"))
        ml_s, ml_v, ml_a, ml_n, ml_ne, ml_h, ml_ha, ml_t, ml_y = (sem("ml_" + n) for n in (
            "s", "v", "a", "n", "ne", "h", "ha", "t", "y"))
        ml_w = sem("ml_w")
        sb_t, sb_zv, sb_a, sb_sp, sb_r, sb_x, sb_e, sb_o, sb_y = (sem("sb_" + n) for n in (
            "t", "zv", "a", "sp", "r", "x", "e", "o", "y"))
        y_hi, y_lo, br_c, br_m, m_hi, m_lo = (sem(n) for n in ("y_hi", "y_lo", "br_c", "br_m", "m_hi", "m_lo"))
        xk_s, xk_t, xk_v, xk_a, xq_s, xq_t, xq_v, xq_a = (sem(n) for n in (
            "xk_s", "xk_t", "xk_v", "xk_a", "xq_s", "xq_t", "xq_v", "xq_a"))
        xk_r, xq_r = sem("xk_r"), sem("xq_r")
        xl_t, xl_v, xl_a, xp_v, xp_t, xp_e, xo_t, xo_h, xo_l = (sem(n) for n in (
            "xl_t", "xl_v", "xl_a", "xp_v", "xp_t", "xp_e", "xo_t", "xo_h", "xo_l"))
        f_c, f_g, f_s, f_p, f_h, f_l = (sem("ffn_" + n) for n in ("c", "g", "s", "p", "h", "l"))
        ot_t, ot_e = sem("ot_t"), sem("ot_e")

        block = ctx.enter_context(nc.Block())

        @block.sync
        def _(sp):
            W = {n: T[n][0].rearrange("(k p) n -> p k n", p=P) for n in ("w_in", "w_br", "w_out", "xa_wq", "xa_wkv", "xa_wo", "ffn_up")}
            down = T["ffn_down"][0].rearrange("(g k p) n -> g p k n", p=P, k=DG)

            def load(par, half, src, kc, first=False):
                if not first:
                    sp.wait_ge(lo_ready, half * 4 + (2 * par - 2))
                sp.dma_start(raw[:, par, 0:kc * CW].rearrange("p (k n) -> p k n", n=CW), src).then_inc(raw_full[par], 16)

            def stream(name):
                u0, n = FIRST[name], COUNT[name]
                _, w, c0, _, kind = next(s for s in STREAM if s[0] == name)
                if name == "UP":
                    with sp.Fori(0, n // 2) as i:
                        for j in range(2):
                            par, h0 = slot_of(name, j)
                            load(par, i + h0, W[w][:, :, bass.ds(i * CW + j * FF, CW)], KC)
                    return
                if name == "DN":
                    with sp.Fori(0, n // NDG) as i:
                        for g in range(NDG):
                            par, h0 = slot_of(name, g)
                            load(par, i * (NDG // 2) + h0, down[g][:, :, bass.ds(i * CW, CW)], DG)
                    return
                i = 2 if name == "A" else 0
                while i < n:
                    u = u0 + i
                    pairs = (n - i) // 2
                    if u % 2 == 0 and u >= 2 and pairs > 1:
                        with sp.Fori(0, pairs) as r:
                            for j in range(2):
                                load(j, r + u // 2, W[w][:, :, bass.ds(r * (2 * CW) + (c0 + (i + j) * CW), CW)], KC)
                        i += 2 * pairs
                    else:
                        load(u % 2, u // 2, W[w][:, :, c0 + i * CW:c0 + (i + 1) * CW], KC)
                        i += 1

            c = T["shape_masks"]
            sp.dma_start(ident[:, :], c[:, 0:P]).then_inc(const_in, 16)
            x_cols = T["x"][0].rearrange("(a p) d -> p a d", p=P)
            for j in range(2):
                sp.dma_start(x_tm[:, :, j * (D // 2):(j + 1) * (D // 2)], x_cols[:, :, j * (D // 2):(j + 1) * (D // 2)]).then_inc(x_in[j], 16)
            sp.dma_start(upper[:, :], c[:, P:2 * P]).then_inc(causal_in, 16)
            sp.dma_start(later[:, :], c[:, 2 * P:3 * P]).then_inc(causal_in, 16)
            row = 0
            for name, k in (("norm_mix", 16), ("norm_xa", 16), ("norm_mem", 16), ("norm_ffn", 16), ("xa_qnorm", 4),
                            ("xa_knorm", 4), ("gdn_norm", 1), ("ml_norm", 1)):
                sp.dma_start(vecs[row:row + k, 0, :], T[name].rearrange("o (c p) -> (o c) p", p=P)).then_inc(vec_in, 16)
                row += k
            sp.dma_start(vecs[0:72, 1, :], T["gdn_conv"][0].rearrange("t (c p) -> (t c) p", p=P)).then_inc(vec_in, 16)
            sp.dma_start(vecs[0:2 * FC, 2:5, :], T["ffn_conv"][0].rearrange("t (c p) -> c t p", p=P)).then_inc(vec_in, 16)
            sp.dma_start(nalog, T["gdn_a_log"].rearrange("o h -> h o")).then_inc(vec_in, 16)
            sp.dma_start(dtb, T["gdn_dt_bias"].rearrange("o h -> h o")).then_inc(vec_in, 16)
            sp.dma_start(ib, T["ml_gate_bias"][0, 0:1, :].rearrange("o h -> h o")).then_inc(vec_in, 16)
            sp.dma_start(fb, T["ml_gate_bias"][0, 1:2, :].rearrange("o h -> h o")).then_inc(vec_in, 16)
            load(0, 0, W["w_in"][:, :, C_A:C_A + CW], KC, first=True)
            load(1, 0, W["w_in"][:, :, C_A + CW:C_A + 2 * CW], KC, first=True)
            sp.wait_ge(gw_zero, 1)
            for at, c0, k in ((0, C_AB, GH), (32, C_AB + GH, GH), (64, C_IF, MH), (96, C_IF + MH, MH)):
                sp.dma_start(gw[:, :, at:at + k], W["w_in"][:, :, c0:c0 + k]).then_inc(gw_in, 16)
            sp.dma_start(lev[:, :, :], c[:, 3 * P:10 * P].rearrange("p (l n) -> p l n", l=7)).then_inc(lev_in, 16)
            for name, _, _, _, _ in STREAM:
                stream(name)

        def halves(tile, kind, half, slot):
            if kind == TM_:
                return tile[:, slot, half * (KC // 2) * CW:(half + 1) * (KC // 2) * CW]
            k = DG if kind == DOWN else KC
            return tile[:, slot, 0:k * CW].rearrange("p (k n) -> p k n", n=CW)[:, :, half * P:(half + 1) * P]

        def split_out(tile, kind, half):
            if kind == TM_:
                return tile[:, half, :]
            k = DG if kind == DOWN else KC
            return tile[:, half, 0:k * P].rearrange("p (k n) -> p k n", n=P)

        @block.gpsimd
        def _(pool):
            pool.memset(gw[:, :, :], 0.0).then_inc(gw_zero, 1)
            for m in range(2):
                name, _, par, _, half = half_of(m)
                pool.wait_ge(hi_ready, m + 1)
                pool.tensor_tensor(split_out(w_lo, FM, half), halves(raw, FM, half, par),
                                   split_out(w_hi, FM, half).bitcast(f32), ALU.subtract).then_inc(lo_ready, 1)
            pool.wait_ge(tin_e, 4)
            pool.wait_ge(tin_d, 4)
            pool.dma_start(x_spill, xT[:, :, :].rearrange("p c s -> p (c s)")).then_inc(spill, 16)

            def store_gates(i):
                name, k = ("GA", i) if i < GA_UNITS else ("GB", i - GA_UNITS)
                pool.wait_ge(act_evac, evacuated(name, k)[1])
                pool.dma_start(g_spill[:, i * 2 * SEQ:(i + 1) * 2 * SEQ], tmp[:, i % 2, 0:512]).then_inc(g_out[i % 2], 16)

            for i in range(GA_UNITS - 1):
                store_gates(i)
            pool.wait_ge(y_t, 3)
            c = T["shape_masks"]
            pool.dma_start(neg_mask, c[:, 10 * P:10 * P + 384]).then_inc(mask_in, 16)
            pool.dma_start(pos_mask, c[:, 10 * P + 384:10 * P + 768]).then_inc(mask_in, 16)
            for i in range(GA_UNITS - 1, GA_UNITS + GB_UNITS):
                store_gates(i)
            for par in range(2):
                pool.wait_ge(g_out[par], 16 * ((GA_UNITS + GB_UNITS + 1 - par) // 2))
            pool.wait_ge(ml_y, 2)
            pool.wait_ge(sb_y, SH)
            n = 2 * (GA_UNITS + GB_UNITS) // G_PIECES
            for i in range(G_PIECES):
                pool.wait_ge(half_used, first_half("GC", i))
                pool.dma_start(gates[:, i * n:(i + 1) * n, :].rearrange("p c s -> p (c s)"),
                               g_spill[:, i * n * SEQ:(i + 1) * n * SEQ]).then_inc(g_back, 16)
            pool.wait_ge(y_lo, 4)
            pool.wait_ge(spill, 16)
            pool.dma_start(xT[:, :, :].rearrange("p c s -> p (c s)"), x_spill).then_inc(back, 16)
            pool.wait_ge(dve_evac, evacuated("BR", 7)[1])
            pool.dma_start(mem_tm, T["mem"][0].rearrange("(a p) d -> p a d", p=P)).then_inc(mem_in, 16)
            pool.wait_ge(dve_evac, evacuated("XO", 7)[1])
            pool.wait_ge(back, 16)
            pool.dma_start(x_spill, xT[:, :, :].rearrange("p c s -> p (c s)")).then_inc(spill, 16)
            pool.wait_ge(half_used, 2 * last_unit("UP") + 2)
            pool.wait_ge(spill, 32)
            pool.dma_start(x_back[:, :, :].rearrange("p c s -> p (c s)"), x_spill).then_inc(back, 16)
            for c in range(D // CW):
                pool.wait_ge(ot_e, c + 1)
                pool.dma_start(out[0].rearrange("(a p) d -> p a d", p=P)[:, :, c * CW:(c + 1) * CW],
                               o_tm[:, :, c * CW:(c + 1) * CW]).then_inc(stored, 16)
            pool.wait_ge(stored, 16 * (D // CW))

        def each_unit(eng, name, fn, start=0, stop=None):
            u0, n = FIRST[name], COUNT[name] if stop is None else stop
            i = start
            while i < n:
                u, pairs = u0 + i, (n - i) // 2
                if u % 2 == 0 and pairs > 1:
                    with eng.Fori(0, pairs) as r:
                        for j in range(2):
                            fn(r * 2 + (i + j), j, r + u // 2)
                    i += 2 * pairs
                else:
                    fn(i, u % 2, u // 2)
                    i += 1

        def level_columns(t, l, bit):
            return t.rearrange("p n (b x w) -> p n b x w", x=2, w=1 << l)[:, :, :, bit, :]

        kind_of = {n: k for n, _, _, _, k in STREAM}

        def mb(i):
            return bank[4 + i % 4]

        def mb6(i):
            return bank[2 + i % 6]

        @block.scalar
        def _(act):
            def copy(out_, in_, func=ACT.Copy, **kw):
                return nc.scalar.activation(out_, in_, func, **kw)

            def hi_half(name, i, par, hp, half):
                act.wait_ge(raw_full[par], hp * 16 + 16)
                if not (isinstance(hp, int) and 2 * hp + par == 0):
                    act.wait_ge(half_used, hp * 4 + (2 * par + half - 1))
                copy(split_out(w_hi, kind_of[name], half), halves(raw, kind_of[name], half, par)).then_inc(hi_ready, 1)

            def hi(name, i, par, hp):
                for half in range(2):
                    hi_half(name, i, par, hp, half)

            def first(name):
                hi(name, 0, FIRST[name] % 2, FIRST[name] // 2)

            def beside(m):
                hi_half(*half_of(m + 1))
                name, i, par, hp, _ = half_of(m - 2 if m >= 2 else 0)
                if m >= 2 and m % 2 == 0 and EVAC[name] == "act":
                    evac_unit(name, i, par, hp)

            def evac_unit(name, i, par, hp):
                act.wait_ge(half_used, hp * 4 + (2 * par + 2))
                b = bank[par]
                strips = lambda t: t[:, bass.ds(i * 2, 2), :].rearrange("p c s -> p (c s)")
                if name == "BV":
                    for a in range(TT):
                        last = copy(v_b[:, a, 2 * i:2 * i + 2, 0:DK],
                                    bank[par + 2 * a][:, :].rearrange("p (x h d) -> p x h d", x=2, h=2)[:, 0])
                elif name == "CV":
                    for a in range(TT):
                        last = copy(v_c[:, a, i * CW:(i + 1) * CW], bank[par + 2 * a][:, 0:CW])
                elif name == "V":
                    for a in range(TT):
                        last = copy(v_tm[:, a, bass.ds(i * CW, CW)], bank[par + 2 * a][:, 0:CW])
                elif name in ("GA", "GB"):
                    k = i + (GA_UNITS if name == "GB" else 0)
                    if k < 2:
                        act.wait_ge(row_v, ROW_V)
                    else:
                        act.wait_ge(g_out[k % 2], 16 * (k // 2))
                    last = copy(tmp[:, k % 2, 0:512], b[:, :], ACT.Sigmoid)
                elif name == "GC":
                    last = copy(gates[:, bass.ds(i * 2 + 2 * (GA_UNITS + GB_UNITS), 2), :].rearrange("p c s -> p (c s)"), b[:, :], ACT.Sigmoid)
                else:
                    to, func = {"A": (proj[:, 0:18, :], ACT.Copy), "Z": (zs, ACT.Silu), "BQK": (qk_b, ACT.Copy),
                                "BO": (o_b, ACT.Sigmoid), "CQK": (qk_c, ACT.Copy),
                                "K": (kT, ACT.Copy), "Q": (qT, ACT.Copy)}[name]
                    last = copy(strips(to), b[:, :], func)
                last.then_inc(act_evac, 1)

            def evac_last(name):
                u = last_unit(name)
                evac_unit(name, COUNT[name] - 1, u % 2, u // 2)

            def rest(name, start=1, stop=None):
                def unit(i, par, hp):
                    hi(name, i, par, hp)
                    if EVAC[name] == "act":
                        evac_unit(name, i - 1, 1 - par, hp if par else hp - 1)
                each_unit(act, name, unit, start, stop)

            def transposed(k, to, c):
                act.wait_ge(tin_t, 8 * k + 2 * c + 1)
                copy(to[:, 4 * c:4 * c + 4, 0:P], mb(2 * c)[:, :].rearrange("p (c s) -> p c s", c=4)).then_inc(tin_e, 1)

            def squares(k, src, c):
                if k < 2:
                    act.wait_ge(tin_e, 4 * k + c + 1)
                    act.wait_ge(tin_d, 4 * k + c + 1)
                if c >= 2:
                    act.wait_ge(*((n_ss, c - 1) if k == 0 else (n_add, 3 * (k - 1) + c - 1)))
                copy(tmp[:, 1 if c and k else c % 2, :], src[:, 4 * c:4 * c + 4, :].rearrange("p c s -> p (c s)"), ACT.Square).then_inc(n_sq, 1)

            def root(k):
                act.wait_ge(n_stat, 2 * k + 1)
                copy(rstd[:, :], rstd[:, :], ACT.Sqrt).then_inc(n_rt, 1)

            def upper_part(k, gain, dst, c):
                act.wait_ge(n_n, 4 * k + c + 1)
                for j in range(4):
                    last = copy(dst[:, 0, 4 * c + j, :], tmp[:, c % 2, j * SEQ:(j + 1) * SEQ], scale=gain[:, 4 * c + j:4 * c + j + 1])
                last.then_inc(n_hi, 1)

            def norm_beside(k, m, src, gain, dst):
                beside(m)
                if k == 1:
                    act.wait_ge(m_lo, COUNT["BR"])
                else:
                    act.wait_ge(n_lo, 4 * k)
                    act.wait_ge(dve_evac, evacuated("WO", 7)[1])
                squares(k, src, 0)
                squares(k, src, 1)
                beside(m + 1)
                squares(k, src, 2)
                beside(m + 2)
                squares(k, src, 3)
                beside(m + 3)
                beside(m + 4)
                root(k)
                beside(m + 5)
                upper_part(k, gain, dst, 0)
                beside(m + 6)
                upper_part(k, gain, dst, 1)
                upper_part(k, gain, dst, 2)
                beside(m + 7)
                upper_part(k, gain, dst, 3)

            for c in range(4):
                transposed(0, xT, c)
                if c:
                    squares(0, xT, c - 1)
            squares(0, xT, 3)
            root(0)
            hi_half(*half_of(0))
            act.wait_ge(set_up, 2)
            for c in range(4):
                upper_part(0, g_mix, x_hl, c)
                if c == 1:
                    hi_half(*half_of(1))
            beside(1)
            act.wait_ge(gw_in, 64)
            copy(gw_hi[:, :, :], gw[:, :, :]).then_inc(gw_h, 1)
            for m in range(2, 7):
                beside(m)

            ra, rb, ri, rf, t0, t1 = (tmp[0:GH if j < 2 or j == 4 else MH, j // 4, (j % 4) * SEQ:(j % 4 + 1) * SEQ] for j in range(6))
            act.wait_ge(row_v, 4)
            copy(rb, rb, ACT.Sigmoid).then_inc(row_a, 1)
            nc.scalar.preload_act_table_set("natural_log_exp_and_others")
            copy(t0, ra, ACT.Abs).then_inc(row_a, 1)
            copy(t1, rf, ACT.Abs).then_inc(row_a, 1)
            act.wait_ge(row_a, 3)
            copy(t0, t0, ACT.Exp, scale=-1.0).then_inc(row_a, 1)
            copy(t1, t1, ACT.Exp, scale=-1.0).then_inc(row_a, 1)
            copy(nalog, nalog, ACT.Exp).then_inc(row_a, 1)
            beside(7)
            act.wait_ge(row_a, 6)
            copy(t0, t0, ACT.Ln, bias=1.0).then_inc(row_a, 1)
            copy(t1, t1, ACT.Ln, bias=1.0).then_inc(row_a, 1)
            for m in range(8, 15):
                beside(m)

            def conv_silu(j):
                act.wait_ge(cv, 24 * (j + 1))
                copy(conv[:, 6 * j:6 * j + 6, :], conv[:, 6 * j:6 * j + 6, :], ACT.Silu).then_inc(cs, 1)

            act.wait_ge(col_e, 2)
            copy(eg.rearrange("p (a h) -> p a h", a=TT), cols[:, :, 32:32 + GH], ACT.Exp).then_inc(col_a, 1)
            copy(tail.rearrange("p (a h) -> p a h", a=TT), cols[:, :, 64:64 + GH], ACT.Exp).then_inc(col_a, 1)
            copy(emn.rearrange("p (a h) -> p a h", a=TT), colm[:, :, :], ACT.Exp, scale=-1.0).then_inc(col_a, 1)
            nc.scalar.preload_act_table_set("silu_and_others")
            for m in (15, 16, 17):
                beside(m)
            conv_silu(0)
            for m in (18, 19, 20):
                beside(m)
            conv_silu(1)
            for m in (21, 22, 23):
                beside(m)
            conv_silu(2)

            def tm_even(g):
                act.wait_ge(tm_t, g + 1)
                copy(tm[:, :, 2 * g:2 * g + 2, :].rearrange("p a c d -> p c a d"),
                     mb6(g)[:, :].rearrange("p (c a d) -> p c a d", c=2, a=TT)).then_inc(tm_ea, 1)

            m = first_half("GA")
            beside(m)
            tm_even(0)
            tm_even(2)
            beside(m + 1)
            tm_even(4)
            beside(m + 2)
            tm_even(6)
            tm_even(8)
            act.wait_ge(l2_v, 5)
            copy(ss, ss, ACT.Sqrt).then_inc(l2_a, 1)
            beside(m + 3)
            beside(m + 4)
            for g in range(6):
                act.wait_ge(qk_t, g + 1)
                copy(conv[:, 2 * g:2 * g + 2, :].rearrange("p c s -> p (c s)"), mb6(g)[:, :]).then_inc(qk_e, 1)
            act.wait_ge(dec_v, 12)
            copy(S_L, S_L, ACT.Exp, scale=-1.0).then_inc(dec_a, 1)
            beside(m + 5)
            beside(m + 6)
            m += 7
            for l in range(7):
                beside(m)
                for g in range(3 if l else 0):
                    act.wait_ge(z_t, 3 * l + g + 1)
                    if l > 1 and g == 0:
                        act.wait_ge(d_t, 6 * (l - 1))
                    copy(S_Z[:, 4 * g:4 * g + 4, :].rearrange("p c s -> p (c s)"), bank[5 + g][:, :]).then_inc(z_e, 1)
                if l:
                    beside(m + 1)
                m += 2 if l else 1
            beside(m)
            for g, k in ((0, 4), (1, 2)):
                act.wait_ge(w_t, g + 1)
                nc.scalar.mul(S_Z[:, 4 * g:4 * g + k, :].rearrange("p c s -> p (c s)"), bank[4 + g][:, 0:k * P], -1.0).then_inc(w_e, 1)
            beside(m + 1)
            for g, k in ((0, 4), (1, 2)):
                act.wait_ge(s_t, g + 1)
                copy(S_Z[:, 6 + 4 * g:6 + 4 * g + k, :].rearrange("p c s -> p (c s)"), bank[6 + g][:, 0:k * P]).then_inc(s_e, 1)
            for g, k in ((0, 4), (1, 2)):
                act.wait_ge(qd_t, g + 1)
                copy(tm[:, 0, 4 * g:4 * g + k, :], bank[2 + g][:, 0:k * P].rearrange("p (c d) -> p c d", d=P)).then_inc(qd_e, 1)
            beside(m + 2)
            beside(m + 3)
            act.wait_ge(a_v, 12)
            copy(S_L, S_L, ACT.Exp).then_inc(a_a, 1)
            beside(m + 4)
            m += 1
            beside(m + 4)
            for g in range(3):
                act.wait_ge(o_t, g + 1)
                copy(S_T[:, 4 * g:4 * g + 4, :].rearrange("p c s -> p (c s)"), bank[(6, 7, 2)[g]][:, :]).then_inc(o_e, 1)
            beside(m + 5)
            act.wait_ge(yn_v, 3)
            copy(ss[:, 0:12], ss[:, 0:12], ACT.Sqrt).then_inc(yn_a, 1)
            beside(m + 6)
            assert m + 7 == first_half("BQK")

            beside(first_half("BQK"))
            rest("BQK")
            first("BV")
            evac_last("BQK")
            rest("BV")
            first("BO")
            evac_last("BV")
            rest("BO")

            def ml_exp(h):
                act.wait_ge(ml_v, 2 * h + 2)
                copy(ml_x[:, h, :], ml_x[:, h, :], ACT.Exp, scale=-1.0).then_inc(ml_a, 1)

            def ml_num(h):
                act.wait_ge(ml_n, h + 1)
                copy(num[:, :, h, :], bank[(4, 5, 6, 7)[h]][:, 0:258].rearrange("p (a d) -> p a d", a=TT)).then_inc(ml_ne, 1)

            m = first_half("CQK")
            hi_half(*half_of(m))
            beside(m)
            ml_exp(0)
            ml_exp(1)
            act.wait_ge(y_e, 3)
            beside(m + 1)
            beside(m + 2)
            ml_num(0)
            ml_num(1)
            ml_exp(2)
            beside(m + 3)
            beside(m + 4)
            ml_exp(3)
            beside(m + 5)
            ml_num(2)
            ml_num(3)
            beside(m + 6)
            act.wait_ge(ml_h, 7)
            copy(ss[:, 0:8], ss[:, 0:8], ACT.Sqrt).then_inc(ml_ha, 1)
            for j in range(7, 13):
                beside(m + j)
            rest("CV")

            def sb_soft(h):
                act.wait_ge(sb_zv, h + 1)
                copy(sb_s[:, h, :], sb_z[:, h, :], ACT.Abs).then_inc(sb_a, 1)
                act.wait_ge(sb_a, 3 * h + 1)
                copy(sb_s[:, h, :], sb_s[:, h, :], ACT.Exp, scale=-1.0).then_inc(sb_a, 1)
                act.wait_ge(sb_a, 3 * h + 2)
                copy(sb_s[:, h, :], sb_s[:, h, :], ACT.Ln, bias=1.0).then_inc(sb_a, 1)

            m = first_half("GB")
            hi_half(*half_of(m))
            for j in range(3):
                beside(m + j)
                nc.scalar.preload_act_table_set("natural_log_exp_and_others")
                sb_soft(2 * j)
                sb_soft(2 * j + 1)
            beside(m + 3)
            beside(m + 4)
            for h in range(SH):
                act.wait_ge(sb_x, h + 1)
                copy(sb_z[:, h, :], sb_z[:, h, :], ACT.Exp).then_inc(sb_e, 1)
            beside(m + 5)
            beside(m + 6)
            for h in range(SH):
                act.wait_ge(sb_o, h + 1)
                copy(yT[:, GH + MH + h, :], mb6(h + 2)[:, 0:SEQ]).then_inc(sb_y, 1)
            beside(m + 7)
            beside(m + 8)

            act.wait_ge(ml_y, 2)
            act.wait_ge(sb_y, SH)
            for c in range(4):
                beside(first_half("GC") + 1 + c)
                copy(y_hl[:, 0, 4 * c:4 * c + 4, :], yT[:, 4 * c:4 * c + 4, :]).then_inc(y_hi, 1)
            rest("GC", 3)
            first("BR")
            evac_last("GC")

            def merged_hi(i, par):
                act.wait_ge(br_m, i + 1)
                copy(x_hl[:, 0, bass.ds(i * 2, 2), :].rearrange("p c s -> p (c s)"), tmp[:, par, 0:512]).then_inc(m_hi, 1)

            def br_unit(i, par, hp):
                hi_half("BR", i, par, hp, 0)
                if not isinstance(i, int) or i >= 2:
                    merged_hi(i - 2, par)
                hi_half("BR", i, par, hp, 1)
            each_unit(act, "BR", br_unit, 1, 2)
            each_unit(act, "BR", br_unit, 2)
            hi_half(*half_of(first_half("WO")))
            merged_hi(COUNT["BR"] - 2, 1 - last_unit("BR") % 2)
            hi_half(*half_of(first_half("WO") + 1))
            merged_hi(COUNT["BR"] - 1, last_unit("BR") % 2)
            rest("WO", 1, 3)
            m = first_half("WO", 3)
            hi_half(*half_of(m))
            beside(m)
            transposed(1, memT, 0)
            transposed(1, memT, 1)
            beside(m + 1)
            transposed(1, memT, 2)
            transposed(1, memT, 3)
            norm_beside(1, m + 2, memT, g_mem, mem_hl)
            m = first_half("K")
            beside(m)
            norm_beside(2, m + 1, xT, g_xa, x_hl)
            rest("K", 5)
            m = first_half("Q")
            hi_half(*half_of(m))
            for j in range(XH + 2):
                beside(m + 2 * j)
                if j == 0:
                    act.wait_ge(n_lo, 12)
                    act.wait_ge(act_evac, evacuated("K", 7)[1])
                if j < XH:
                    if j >= 2:
                        act.wait_ge(xk_t, j - 1)
                    copy(tmp[:, j % 2, :], kT[:, 4 * j:4 * j + 4, :].rearrange("p c s -> p (c s)"), ACT.Square).then_inc(xk_s, 1)
                if 1 <= j <= XH:
                    act.wait_ge(xk_v, 3 * j - 2)
                    copy(rstd[:, :], rstd[:, :], ACT.Sqrt).then_inc(xk_a, 1)
                beside(m + 2 * j + 1)
            beside(m + 12)
            rest("Q", 7)
            def query_squares(h):
                if h >= 2:
                    act.wait_ge(xq_t, h - 1)
                copy(tmp[:, h % 2, :], qT[:, 4 * h:4 * h + 4, :].rearrange("p c s -> p (c s)"), ACT.Square).then_inc(xq_s, 1)

            def output_hi(c):
                act.wait_ge(xo_t, c + 1)
                copy(x_hl[:, 0, 2 * c:2 * c + 2, :].rearrange("p c s -> p (c s)"), mb(c)[:, :]).then_inc(xo_h, 1)

            m = first_half("V")
            hi_half(*half_of(m))
            beside(m)
            act.wait_ge(act_evac, evacuated("Q", 7)[1])
            act.wait_ge(xk_t, XH)
            query_squares(0)
            query_squares(1)
            beside(m + 1)
            query_squares(2)
            query_squares(3)
            beside(m + 2)
            act.wait_ge(xq_v, 1)
            copy(xss, xss, ACT.Sqrt).then_inc(xq_a, 1)
            nc.scalar.preload_act_table_set("natural_log_exp_and_others")
            for p in range(XH):
                beside(m + 3 + p)
                for a in range(TT):
                    j = 2 * p + a
                    act.wait_ge(xl_v, 2 * j + 2)
                    copy(prob[:, a, p, :], mb(j)[:, 0:SEQ], ACT.Exp, bias=xmx[:, j:j + 1], scale=xss[:, j:j + 1],
                         accum_out=xsum[:, j:j + 1]).then_inc(xl_a, 1)
            for p in range(2):
                beside(m + 7 + p)
                for h in (2 * p, 2 * p + 1):
                    act.wait_ge(xp_t, h + 1)
                    copy(probT[:, 0:TT, h, :], mb(h)[:, :].rearrange("p (m s) -> p m s", m=TT)).then_inc(xp_e, 1)
            for j, cs_ in ((9, (0, 1)), (10, (2, 3)), (11, (4,)), (12, ()), (13, (5,)), (14, ()), (15, (6,)), (16, (7,))):
                if j < 16:
                    beside(m + j)
                else:
                    evac_last("V")
                    hi_half(*half_of(m + 17))
                for c in cs_:
                    output_hi(c)

            def new_residual(i, par):
                act.wait_ge(dve_evac, i + evacuated("XO", 0)[1])
                if not isinstance(i, int) or i >= 2:
                    act.wait_ge(x_add, i - 1)
                copy(tmp[:, par, 0:512], xT[:, bass.ds(i * 2, 2), :].rearrange("p c s -> p (c s)"), ACT.Square).then_inc(x_sq, 1)
                for x in range(2):
                    last = copy(xg[:, bass.ds(i * 2 + x, 1), :].rearrange("p c s -> p (c s)"),
                                xT[:, bass.ds(i * 2 + x, 1), :].rearrange("p c s -> p (c s)"), scale=g_ffn[:, bass.ds(i * 2 + x, 1)])
                last.then_inc(x_g, 1)

            def upper_residual(c):
                act.wait_ge(x_g, c + 1)
                copy(x_hl[:, 0, 2 * c:2 * c + 2, :], xg[:, 2 * c:2 * c + 2, :]).then_inc(n_hi, 1)

            def xo_unit(i, par, hp):
                hi("XO", i, par, hp)
                new_residual(i - 1, 1 - par)
            each_unit(act, "XO", xo_unit, 1, 3)
            each_unit(act, "XO", xo_unit, 3)
            m = first_half("UP")
            hi_half(*half_of(m))
            act.wait_ge(half_used, m)
            upper_residual(0)
            upper_residual(1)
            new_residual(COUNT["XO"] - 1, last_unit("XO") % 2)
            for c in range(2, 8):
                upper_residual(c)
            hi_half(*half_of(m + 1))
            root(3)
            nc.scalar.preload_act_table_set("silu_and_others")

            def silu_gate(j):
                act.wait_ge(f_c, j * 6 + 6)
                copy(tmp[:, 0, 0:512], tmp[:, 0, 0:512], ACT.Silu).then_inc(f_s, 1)

            def product_hi(j):
                act.wait_ge(f_p, j + 1)
                copy(act_hl[:, 0, bass.ds(j * 2, 2), :].rearrange("p c s -> p (c s)"), tmp[:, 1, 512:1024]).then_inc(f_h, 1)

            (p0, h0), (p1, h1) = slot_of("UP", 0), slot_of("UP", 1)
            hi("UP", 1, p1, h1)
            act.wait_ge(spill, 32)
            with act.Fori(1, FC // 2) as j:
                hi_half("UP", 2 * j, p0, j + h0, 0)
                silu_gate(j - 1)
                hi_half("UP", 2 * j, p0, j + h0, 1)
                hi_half("UP", 2 * j + 1, p1, j + h1, 0)
                product_hi(j - 1)
                hi_half("UP", 2 * j + 1, p1, j + h1, 1)
            hi_half(*half_of(first_half("DN")))
            silu_gate(FC // 2 - 1)
            hi_half(*half_of(first_half("DN") + 1))
            product_hi(FC // 2 - 1)

            for g in range(1, NDG):
                hi("DN", g, *slot_of("DN", g))
            with act.Fori(1, D // CW) as c:
                for g in range(NDG):
                    par, h0 = slot_of("DN", g)
                    hi("DN", g, par, c * (NDG // 2) + h0)
                act.wait_ge(ot_t, c)
                copy(o_tm[:, :, bass.ds((c - 1) * CW, CW)].rearrange("p a (x d) -> p a x d", x=2),
                     bank[6][:, :].rearrange("p (a x d) -> p a x d", a=TT, x=2)).then_inc(ot_e, 1)
            act.wait_ge(ot_t, D // CW)
            copy(o_tm[:, :, D - CW:D].rearrange("p a (x d) -> p a x d", x=2),
                 bank[6][:, :].rearrange("p (a x d) -> p a x d", a=TT, x=2)).then_inc(ot_e, 1)

        class Count:

            def __init__(self, eng, sem_):
                self.eng, self.sem, self.n = eng, sem_, 0

            def __call__(self, ins):
                ins.then_inc(self.sem, 1)
                self.n += 1

            def settle(self, back=0):
                self.eng.wait_ge(self.sem, self.n - back)

        @block.vector
        def _(dve):
            v = nc.vector
            tt = v.tensor_tensor
            bc = lambda t, shape: t.to_broadcast(shape)

            def lo_half(name, i, par, hp, half):
                dve.wait_ge(hi_ready, hp * 4 + (2 * par + half + 1))
                kind = kind_of[name]
                tt(split_out(w_lo, kind, half), halves(raw, kind, half, par),
                   split_out(w_hi, kind, half).bitcast(f32), ALU.subtract).then_inc(lo_ready, 1)

            def lo(name, i, par, hp):
                for half in range(2):
                    lo_half(name, i, par, hp, half)

            def first(name):
                lo(name, 0, FIRST[name] % 2, FIRST[name] // 2)

            def add_residual(name, i, par, hp):
                dve.wait_ge(half_used, hp * 4 + (2 * par + 2))
                x2 = xT[:, bass.ds(i * 2, 2), :].rearrange("p c s -> p (c s)")
                tt(x2, bank[par][:, :], x2, ALU.add).then_inc(dve_evac, 1)

            def beside(m):
                lo_half(*half_of(m + 1))
                name, i, par, hp, _ = half_of(m - 2 if m >= 2 else 0)
                if m >= 2 and m % 2 == 0 and name in ("WO", "XO"):
                    add_residual(name, i, par, hp)

            def rest(name, start=1, stop=None):
                def unit(i, par, hp):
                    lo_half(name, i, par, hp, 0)
                    if name in ("WO", "XO"):
                        add_residual(name, i - 1, 1 - par, hp if par else hp - 1)
                    lo_half(name, i, par, hp, 1)
                each_unit(dve, name, unit, start, stop)

            def mean(k):
                dve.wait_ge(*((n_ss, k + 4) if k < 3 else (x_ss, 1)))
                v.tensor_scalar(rstd[:, :], bank[3][:, 0:SEQ], 1.0 / D, EPS, ALU.mult, ALU.add).then_inc(n_stat, 1)

            def inverse(k):
                dve.wait_ge(n_rt, k + 1)
                v.reciprocal(rstd[:, :], rstd[:, :]).then_inc(n_stat, 1)
                dve.wait_ge(n_stat, 2 * k + 2)

            def normed(k, src, c):
                if c >= 2:
                    dve.wait_ge(n_lo, 4 * k + c - 1)
                tt(tmp[:, c % 2, :].rearrange("p (c s) -> p c s", c=4), src[:, 4 * c:4 * c + 4, :],
                   bc(rstd[:, :].unsqueeze(1), [P, 4, SEQ]), ALU.mult).then_inc(n_n, 1)

            def lower_part(k, gain, dst, c):
                dve.wait_ge(n_hi, 4 * k + c + 1)
                for j in range(4):
                    last = v.scalar_tensor_tensor(dst[:, 1, 4 * c + j, :], tmp[:, c % 2, j * SEQ:(j + 1) * SEQ],
                                                  gain[:, 4 * c + j:4 * c + j + 1], dst[:, 0, 4 * c + j, :].bitcast(f32),
                                                  ALU.mult, ALU.subtract)
                last.then_inc(n_lo, 1)

            def add_squares(k, c):
                dve.wait_ge(n_sq, 4 * k + c + 1)
                if c > 1:
                    dve.wait_ge(n_add, 3 * (k - 1) + c - 1)
                tt(tmp[:, 0, :], tmp[:, 0, :], tmp[:, 1, :], ALU.add).then_inc(n_add, 1)

            def transposed(k, to, c):
                dve.wait_ge(tin_t, 8 * k + 2 * c + 2)
                v.tensor_copy(to[:, 4 * c:4 * c + 4, P:SEQ], mb(2 * c + 1)[:, :].rearrange("p (c s) -> p c s", c=4)).then_inc(tin_d, 1)

            def norm_beside(k, m, src, gain, dst):
                beside(m)
                add_squares(k, 1)
                beside(m + 1)
                add_squares(k, 2)
                beside(m + 2)
                add_squares(k, 3)
                beside(m + 3)
                mean(k)
                beside(m + 4)
                inverse(k)
                normed(k, src, 0)
                normed(k, src, 1)
                beside(m + 5)
                lower_part(k, gain, dst, 0)
                normed(k, src, 2)
                beside(m + 6)
                lower_part(k, gain, dst, 1)
                normed(k, src, 3)
                beside(m + 7)
                lower_part(k, gain, dst, 2)
                lower_part(k, gain, dst, 3)

            v.memset(ones[:, :], 1.0).then_inc(set_up, 1)
            for c in range(4):
                transposed(0, xT, c)
            dve.wait_ge(vec_t, 1)
            v.tensor_copy(vec1[:, :], bank[4][:, 0:74])
            v.tensor_copy(vec2[:, :, :].rearrange("p t c -> p (t c)"), bank[4][:, 74:146])
            v.tensor_copy(vec3[:, :, :].rearrange("p t c -> p (t c)"), bank[4][:, 146:410]).then_inc(set_up, 1)
            mean(0)
            inverse(0)
            normed(0, xT, 0)
            dve.wait_ge(set_up, 2)
            normed(0, xT, 1)
            lower_part(0, g_mix, x_hl, 0)
            normed(0, xT, 2)
            lower_part(0, g_mix, x_hl, 1)
            normed(0, xT, 3)
            lower_part(0, g_mix, x_hl, 2)
            lower_part(0, g_mix, x_hl, 3)
            dve.wait_ge(lo_ready, 2)
            beside(1)
            dve.wait_ge(gw_h, 1)
            tt(gw_lo[:, :, :], gw[:, :, :], gw_hi[:, :, :].bitcast(f32), ALU.subtract).then_inc(gw_l, 1)
            for m in range(2, 6):
                beside(m)

            ra, rb, ri, rf, t0, t1, rg, rl = (tmp[0:GH if j in (0, 1, 4, 6) else MH, j // 4, (j % 4) * SEQ:(j % 4 + 1) * SEQ]
                                              for j in range(8))
            rv = Count(dve, row_v)
            dve.wait_ge(row_mm, 1)
            dve.wait_ge(n_lo, 4)
            rv(v.tensor_scalar(ra, bank[4][0:GH, 0:SEQ], dtb, None, ALU.add))
            rv(v.tensor_copy(rb, bank[4][32:32 + GH, 0:SEQ]))
            rv(v.tensor_scalar(ri, bank[4][64:64 + MH, 0:SEQ], ib, None, ALU.add))
            rv(v.tensor_scalar(rf, bank[4][96:96 + MH, 0:SEQ], fb, None, ALU.add))
            rv(v.memset(rt[:, :], 0.0))
            for m in range(6, 9):
                beside(m)
            dve.wait_ge(row_a, 8)
            rv.settle()
            rv(v.scalar_tensor_tensor(rg, ra, 0.0, t0, ALU.max, ALU.add))
            rv(v.scalar_tensor_tensor(rl, rf, 0.0, t1, ALU.min, ALU.subtract))
            rv.settle()
            rv(v.tensor_scalar(rg, rg, nalog, -1.0, ALU.mult, ALU.mult))
            rv.settle()
            for a in range(TT):
                sl = slice(a * P, a * P + P)
                rv(v.tensor_tensor_scan(g_row[:, sl], ones[0:GH, :], rg[:, sl], 0.0, ALU.mult, ALU.add))
            rv(v.tensor_tensor_scan(t1[:, 0:P], ones[0:MH, :], rl[:, 0:P], 0.0, ALU.mult, ALU.add))
            rv.settle()
            rv(v.tensor_tensor_scan(t1[:, P:SEQ], ones[0:MH, :], rl[:, P:SEQ], t1[:, P - 1:P], ALU.mult, ALU.add))
            rv.settle()
            beside(9)
            rv(tt(ri, ri, t1, ALU.subtract))
            rv.settle()
            rv(v.tensor_tensor_scan(m_row[:, :], ri, ri, 0.0, ALU.max, ALU.max))
            rv.settle()
            rv(tt(rt2[:, :], t1, m_row[:, :], ALU.add))
            rv(v.tensor_copy(rt[0:GH, :], rb))
            rv(v.tensor_copy(rt[32:32 + GH, :], g_row[:, :]))
            for a in range(TT):
                sl = slice(a * P, a * P + P)
                rv(v.tensor_scalar(rt[64:64 + GH, sl], g_row[:, sl], g_row[:, a * P + P - 1:a * P + P], -1.0, ALU.subtract, ALU.mult))
            rv(v.tensor_copy(rt[96:96 + MH, :], ri))
            assert rv.n == ROW_V
            beside(10)

            c_ = Count(dve, cv)

            def tap_of(j, d):
                tap = GDN_TAPS - 1 - d
                if d == 0:
                    dve.wait_ge(act_evac, evacuated("A", 3 * j + 2)[1])
                for c in range(6 * j, 6 * j + 6):
                    if d:
                        c_.settle(5)
                        c_(v.scalar_tensor_tensor(conv[:, c, d:], proj[:, c, 0:SEQ - d], vec2[:, tap, c:c + 1], conv[:, c, d:],
                                                  ALU.mult, ALU.add))
                    else:
                        c_(v.tensor_scalar(conv[:, c, :], proj[:, c, :], vec2[:, tap, c:c + 1], None, ALU.mult))

            for d in range(3):
                tap_of(0, d)
                beside(11 + d)
            dve.wait_ge(row_t, 1)
            v.tensor_copy(cols[:, :, :].rearrange("p a n -> p (a n)"), bank[5][:, 0:SEQ]).then_inc(col_e, 1)
            v.tensor_copy(colm[:, :, :].rearrange("p a n -> p (a n)"), bank[5][:, SEQ:SEQ + TT * MH]).then_inc(col_e, 1)
            beside(14)
            dve.wait_ge(col_a, 1)
            dve.wait_ge(col_e, 2)
            tt(beg, eg[:, GH:2 * GH], cols[:, 1, 0:GH], ALU.mult).then_inc(col_e, 1)
            tap_of(0, 3)
            beside(15)
            for d in range(GDN_TAPS):
                tap_of(1, d)
                beside(16 + d)
            for d in range(GDN_TAPS):
                tap_of(2, d)
                beside(20 + d)
            c_.settle()

            def tm_odd(g):
                dve.wait_ge(tm_t, g + 1)
                v.tensor_copy(tm[:, :, 2 * g:2 * g + 2, :].rearrange("p a c d -> p c a d"),
                              mb6(g)[:, :].rearrange("p (c a d) -> p c a d", c=2, a=TT)).then_inc(tm_ed, 1)

            m = first_half("GA")
            tm_odd(1)
            beside(m)
            l2 = Count(dve, l2_v)
            sq = slabf[:, 12 * P:36 * P].rearrange("p (a c d) -> p a c d", a=TT, d=P)
            ssv = ss.rearrange("p (a c) -> p a c", a=TT)

            def head_squares(part):
                c = slice(GH * part, GH * part + GH)
                l2(tt(sq[:, :, c, :], tm[:, :, c, :], tm[:, :, c, :], ALU.mult))

            def head_sums(part):
                c = slice(GH * part, GH * part + GH)
                l2.settle()
                l2(v.tensor_reduce(ssv[:, :, c], sq[:, :, c, :], AX.X, ALU.add))

            dve.wait_ge(gw_l, 1)
            dve.wait_ge(tm_ea, 2)
            dve.wait_ge(tm_ed, 1)
            head_squares(0)
            tm_odd(3)
            tm_odd(5)
            beside(m + 1)
            head_sums(0)
            tm_odd(7)
            dve.wait_ge(tm_ea, 3)
            dve.wait_ge(tm_ed, 3)
            head_squares(1)
            beside(m + 2)
            head_sums(1)
            l2.settle()
            l2(v.tensor_scalar(ss, ss, EPS, None, ALU.add))
            dve.wait_ge(l2_a, 1)
            l2(v.reciprocal(ss, ss))
            l2.settle()
            l2(v.tensor_scalar(ssv[:, :, 0:GH], ssv[:, :, 0:GH], DK ** -0.5, None, ALU.mult))
            l2.settle()
            l2(tt(tm[:, :, 0:12, :], tm[:, :, 0:12, :], bc(ssv.unsqueeze(3), [P, TT, 12, P]), ALU.mult))
            for j in range(3):
                dve.wait_ge(dec_t, j + 1)
                for x in range(2):
                    for a in range(TT):
                        h = 2 * j + x
                        v.tensor_scalar(S_L[:, a * GH + h, :], mb6(j + 3)[:, x * SEQ + a * P:x * SEQ + a * P + P],
                                        cols[:, a, 32 + h:33 + h], 0.0, ALU.subtract, ALU.max).then_inc(dec_v, 1)
            bshape = [P, 12, P]
            cc = Count(dve, c_v)
            beside(m + 3)
            beside(m + 4)
            dve.wait_ge(dec_a, 1)
            for n in range(12):
                a, h = n // GH, n % GH
                dve.wait_ge(kk_t, n // 4 + 1)
                v.scalar_tensor_tensor(S_L[:, n, :], bank[2 + n // 4][:, n % 4 * P:n % 4 * P + P], cols[:, a, h:h + 1], S_L[:, n, :],
                                       ALU.mult, ALU.mult).then_inc(l_v, 1)
            beside(m + 5)
            dve.wait_ge(lev_in, 16)
            dve.wait_ge(causal_in, 32)
            dve.wait_ge(l_v, 12)
            cc(tt(S_C, S_L, bc(lev[:, 0, :].unsqueeze(1), bshape), ALU.mult))
            cc.settle()
            cc(tt(S_T, bc(ident[:, :].unsqueeze(1), bshape), S_C, ALU.subtract))
            beside(m + 6)
            m += 7
            kv = Count(dve, kv_v)
            hs = [P, GH, P]
            for l in range(7):
                if l == 0:
                    dve.wait_ge(qk_t, 6)
                    dve.wait_ge(tm_ea, 5)
                    dve.wait_ge(tm_ed, 4)
                    kv(tt(tm[:, :, 12:18, :], tm[:, :, 12:18, :], bc(cols[:, :, 0:GH].unsqueeze(3), [P, TT, GH, P]), ALU.mult))
                elif l == 1:
                    kv(tt(tm[:, 0, 6:12, :], tm[:, 0, 6:12, :], bc(tail[:, 0:GH].unsqueeze(2), hs), ALU.mult))
                    dve.wait_ge(col_e, 3)
                    kv(tt(tm[:, 1, 6:12, :], tm[:, 1, 6:12, :], bc(beg.unsqueeze(2), hs), ALU.mult))
                elif l == 2:
                    kv(tt(tm[:, 1, 0:6, :], tm[:, 1, 0:6, :], bc(eg[:, GH:2 * GH].unsqueeze(2), hs), ALU.mult))
                if l < 6:
                    dve.wait_ge(z_t, 3 * l + 3)
                    cc.settle()
                    cc(tt(S_C, S_L, bc(lev[:, l + 1, :].unsqueeze(1), bshape), ALU.mult))
                beside(m)
                for g in range(3):
                    if l == 0:
                        tt(S_U[:, 4 * g:4 * g + 4, :], bc(ident[:, :].unsqueeze(1), [P, 4, P]),
                           bank[5 + g][:, :].rearrange("p (n s) -> p n s", n=4), ALU.subtract).then_inc(d_e, 1)
                        continue
                    dve.wait_ge(d_t, 6 * (l - 1) + (2 * g + 2 if l < 6 else g + 1))
                    for x, S_X in ((0, S_T), (1, S_U))[l // 6:]:
                        t = level_columns(S_X[:, 4 * g:4 * g + 4, :], l, x)
                        o = bank[2 + 2 * g + x][:, 0:4 * P // 2].rearrange("p (n b w) -> p n b w", n=4, w=1 << l)
                        v.scalar_tensor_tensor(t, o, -1.0, t, ALU.mult, ALU.add).then_inc(d_e, 1)
                if l:
                    beside(m + 1)
                m += 2 if l else 1
            for g, k in ((0, 4), (1, 2)):
                dve.wait_ge(u_t, g + 1)
                v.tensor_copy(S_C[:, 4 * g:4 * g + k, :].rearrange("p c s -> p (c s)"), bank[2 + g][:, 0:k * P]).then_inc(u_e, 1)
            beside(m)
            beside(m + 1)
            av = Count(dve, a_v)
            cc.settle()
            for j in range(3):
                dve.wait_ge(a_t, j + 1)
                for x in range(2):
                    for a in range(TT):
                        h = 2 * j + x
                        av(v.tensor_scalar(S_L[:, a * GH + h, :], bank[4 + j][:, x * SEQ + a * P:x * SEQ + a * P + P],
                                           cols[:, a, 32 + h:33 + h], 0.0, ALU.subtract, ALU.min))
            beside(m + 2)
            for g, k in ((0, 4), (1, 2)):
                dve.wait_ge(vn_t, g + 1)
                v.tensor_copy(S_C[:, 6 + 4 * g:6 + 4 * g + k, :].rearrange("p c s -> p (c s)"),
                              bank[4 + g][:, 0:k * P]).then_inc(vn_e, 1)
            beside(m + 3)
            dve.wait_ge(a_a, 1)
            av(tt(S_L, S_L, bc(upper[:, :].unsqueeze(1), bshape), ALU.mult))
            av.settle()
            for g in range(3):
                dve.wait_ge(a_t, 4 + g)
                t = S_L[:, 4 * g:4 * g + 4, :].rearrange("p c s -> p (c s)")
                av(tt(t, bank[(7, 2, 3)[g]][:, :], t, ALU.mult))
            m += 1
            beside(m + 3)
            dve.wait_ge(o_e, 3)
            yn = Count(dve, yn_v)
            yn(tt(S_L, S_T, S_T, ALU.mult))
            beside(m + 4)
            yn.settle()
            yn(v.tensor_reduce(ss[:, 0:12], S_L, AX.X, ALU.add))
            yn.settle()
            yn(v.tensor_scalar(ss[:, 0:12], ss[:, 0:12], 1.0 / DK, EPS, ALU.mult, ALU.add))
            dve.wait_ge(yn_a, 1)
            yn(v.reciprocal(ss[:, 0:12], ss[:, 0:12]))
            yn.settle()
            yn(tt(S_T, S_T, bc(ss[:, 0:12].unsqueeze(2), bshape), ALU.mult))
            beside(m + 5)
            dve.wait_ge(spill, 16)
            dve.wait_ge(act_evac, evacuated("Z", 2)[1])
            for j in range(3):
                dve.wait_ge(y_t, j + 1)
                v.scalar_tensor_tensor(yT[:, 2 * j:2 * j + 2, :].rearrange("p c s -> p (c s)"), bank[3 + j][:, :], g_gdn,
                                       zs[:, 2 * j:2 * j + 2, :].rearrange("p c s -> p (c s)"), ALU.mult, ALU.mult).then_inc(y_e, 1)
            v.memset(v_b[:, :, :, DK:DK + 1], 1.0).then_inc(set_up, 1)

            beside(m + 6)

            beside(first_half("BQK"))
            rest("BQK")
            first("BV")
            rest("BV")
            first("BO")
            rest("BO")

            def ml_weights(h):
                b = bank[4 + 2 * ML_PAIR[h]], bank[5 + 2 * ML_PAIR[h]]
                dve.wait_ge(ml_s, h + 1)
                v.scalar_tensor_tensor(ml_x[:, h, 0:SEQ], b[0][:, 0:SEQ], cols[:, 0, 96 + h:97 + h], pos_mask[:, 0:SEQ],
                                       ALU.subtract, ALU.add).then_inc(ml_v, 1)
                v.scalar_tensor_tensor(ml_x[:, h, SEQ:384], b[0][:, P:SEQ], cols[:, 1, 96 + h:97 + h], pos_mask[:, SEQ:384],
                                       ALU.subtract, ALU.add).then_inc(ml_v, 1)
                dve.wait_ge(ml_a, h + 1)
                v.scalar_tensor_tensor(ml_x[:, h, :], b[1][:, 0:384], DK ** -0.5, ml_x[:, h, :], ALU.mult, ALU.mult).then_inc(ml_w, 1)

            m = first_half("CQK")
            lo_half(*half_of(m))
            dve.wait_ge(mask_in, 32)
            beside(m)
            ml_weights(0)
            ml_weights(1)
            beside(m + 1)
            beside(m + 2)
            ml_weights(2)
            beside(m + 3)
            beside(m + 4)
            ml_weights(3)
            beside(m + 5)
            dve.wait_ge(ml_ne, MH)
            mh = Count(dve, ml_h)
            den3 = den.rearrange("p (a h) -> p a h", a=TT)
            mh(v.scalar_tensor_tensor(den3, num[:, :, :, DK], -1.0, num[:, :, :, DK], ALU.mult, ALU.max))
            mh.settle()
            mh(tt(den, den, emn, ALU.max))
            mh.settle()
            mh(v.reciprocal(den, den))
            mh.settle()
            hv = num[:, :, :, 0:DK]
            nshape = [P, TT, MH, DK]
            mh(tt(hv, hv, bc(den3.unsqueeze(3), nshape), ALU.mult))
            beside(m + 6)
            mh.settle()
            sq = slabf[:, 0:8 * DK].rearrange("p (a h d) -> p a h d", a=TT, h=MH)
            mh(tt(sq, hv, hv, ALU.mult))
            mh.settle()
            s3 = ss[:, 0:8].rearrange("p (a h) -> p a h", a=TT)
            mh(v.tensor_reduce(s3, sq, AX.X, ALU.add))
            mh.settle()
            mh(v.tensor_scalar(ss[:, 0:8], ss[:, 0:8], 1.0 / DK, EPS, ALU.mult, ALU.add))
            beside(m + 7)
            dve.wait_ge(ml_ha, 1)
            mh(v.reciprocal(ss[:, 0:8], ss[:, 0:8]))
            mh.settle()
            mh(tt(hv, hv, bc(s3.unsqueeze(3), nshape), ALU.mult))
            beside(m + 8)
            for j in range(2):
                dve.wait_ge(ml_t, j + 1)
                v.scalar_tensor_tensor(yT[:, GH + 2 * j:GH + 2 * j + 2, :].rearrange("p c s -> p (c s)"), bank[4 + j][:, :], g_ml,
                                       o_b[:, 2 * j:2 * j + 2, :].rearrange("p c s -> p (c s)"), ALU.mult, ALU.mult).then_inc(ml_y, 1)

            for j in range(9, 13):
                beside(m + j)
            rest("CV")

            m = first_half("GB")
            lo_half(*half_of(m))
            for h in range(SH):
                dve.wait_ge(sb_t, h + 1)
                v.scalar_tensor_tensor(sb_z[:, h, :], mb6(h + 2)[:, 0:384], DK ** -0.5, neg_mask, ALU.mult, ALU.add).then_inc(sb_zv, 1)
            for j in range(3):
                beside(m + j)
                for h in (2 * j, 2 * j + 1):
                    dve.wait_ge(sb_a, 3 * h + 3)
                    v.scalar_tensor_tensor(sb_s[:, h, :], sb_z[:, h, :], 0.0, sb_s[:, h, :], ALU.max, ALU.add).then_inc(sb_sp, 1)
            beside(m + 3)
            for h in range(SH):
                dve.wait_ge(sb_r, h + 1)
                tt(sb_z[:, h, :], sb_z[:, h, :], mb6(h + 2)[:, 0:384], ALU.subtract).then_inc(sb_x, 1)
            for j in range(4, 9):
                beside(m + j)

            for c in range(4):
                beside(first_half("GC") + 1 + c)
                dve.wait_ge(y_hi, c + 1)
                tt(y_hl[:, 1, 4 * c:4 * c + 4, :], yT[:, 4 * c:4 * c + 4, :], y_hl[:, 0, 4 * c:4 * c + 4, :].bitcast(f32),
                   ALU.subtract).then_inc(y_lo, 1)
            rest("GC", 3)
            first("BR")
            dve.wait_ge(act_evac, evacuated("GC", COUNT["GC"] - 1)[1])
            dve.wait_ge(g_back, 16 * G_PIECES)

            def merge(i, par, hp):
                dve.wait_ge(half_used, hp * 4 + (2 * par + 2))
                if not isinstance(i, int) or i >= 2:
                    dve.wait_ge(m_lo, i - 1)
                m0, m1 = tmp[:, par, 0:512], tmp[:, par, 512:1024]
                gate = lambda j: gates[:, bass.ds(i * 2 + j * KC, 2), :].rearrange("p c s -> p (c s)")
                tt(m0, bank[par][:, :], gate(0), ALU.mult)
                tt(m1, bank[2 + par][:, :], gate(1), ALU.mult).then_inc(br_c, 1)
                dve.wait_ge(br_c, i * 2 + 1)
                tt(m0, m0, m1, ALU.add).then_inc(br_c, 1)
                dve.wait_ge(br_c, i * 2 + 2)
                tt(m1, bank[4 + par][:, :], gate(2), ALU.mult).then_inc(dve_evac, 1)
                dve.wait_ge(dve_evac, i + 1)
                tt(m0, m0, m1, ALU.add).then_inc(br_m, 1)

            def merged_lo(i, par):
                dve.wait_ge(m_hi, i + 1)
                two = lambda j: x_hl[:, j, bass.ds(i * 2, 2), :].rearrange("p c s -> p (c s)")
                tt(two(1), tmp[:, par, 0:512], two(0).bitcast(f32), ALU.subtract).then_inc(m_lo, 1)

            def br_unit(i, par, hp):
                lo_half("BR", i, par, hp, 0)
                if not isinstance(i, int) or i >= 2:
                    merged_lo(i - 2, par)
                lo_half("BR", i, par, hp, 1)
                merge(i - 1, 1 - par, hp if par else hp - 1)
            each_unit(dve, "BR", br_unit, 1, 2)
            each_unit(dve, "BR", br_unit, 2)
            lo_half(*half_of(first_half("WO")))
            u = last_unit("BR")
            merged_lo(COUNT["BR"] - 2, 1 - u % 2)
            merge(COUNT["BR"] - 1, u % 2, u // 2)
            lo_half(*half_of(first_half("WO") + 1))
            merged_lo(COUNT["BR"] - 1, u % 2)
            dve.wait_ge(back, 16)
            rest("WO", 1, 3)
            m = first_half("WO", 3)
            lo_half(*half_of(m))
            add_residual("WO", 2, *((m - 2) // 2 % 2, (m - 2) // 4))
            transposed(1, memT, 0)
            transposed(1, memT, 1)
            lo_half(*half_of(m + 1))
            transposed(1, memT, 2)
            transposed(1, memT, 3)
            beside(m + 1)
            norm_beside(1, m + 2, memT, g_mem, mem_hl)
            m = first_half("K")
            beside(m)
            norm_beside(2, m + 1, xT, g_xa, x_hl)
            rest("K", 5)
            m = first_half("Q")
            lo_half(*half_of(m))
            tt(gqk, gq, gk, ALU.mult).then_inc(set_up, 1)
            dve.wait_ge(set_up, 4)

            def add_head_squares(h, made, added):
                sq = tmp[:, h % 2, :]
                dve.wait_ge(made, h + 1)
                tt(sq[:, 0:512], sq[:, 0:512], sq[:, 512:1024], ALU.add).then_inc(added, 1)
                dve.wait_ge(added, 2 * h + 1)
                tt(sq[:, 0:SEQ], sq[:, 0:SEQ], sq[:, SEQ:512], ALU.add).then_inc(added, 1)

            def scale_keys(h):
                dve.wait_ge(xk_a, h + 1)
                v.reciprocal(rstd[:, :], rstd[:, :]).then_inc(xk_v, 1)
                dve.wait_ge(xk_v, 3 * h + 2)
                for c in range(XC):
                    last = v.scalar_tensor_tensor(kT[:, 4 * h + c, :], kT[:, 4 * h + c, :], gqk[:, c:c + 1], rstd[:, :], ALU.mult, ALU.mult)
                last.then_inc(xk_v, 1)

            for j in range(XH + 2):
                if j >= 2:
                    scale_keys(j - 2)
                if 1 <= j <= XH:
                    dve.wait_ge(xk_t, j)
                    if j >= 2:
                        dve.wait_ge(xk_v, 3 * (j - 1))
                    v.tensor_scalar(rstd[:, :], bank[6 + (j - 1) % 2][:, 0:SEQ], 1.0 / XD, EPS, ALU.mult, ALU.add).then_inc(xk_v, 1)
                beside(m + 2 * j)
                if j < XH:
                    add_head_squares(j, xk_s, xk_r)
                beside(m + 2 * j + 1)
            beside(m + 12)
            rest("Q", 7)
            def scale_prob(j):
                h, a = j // 2, j % 2
                dve.wait_ge(xl_a, j + 1)
                v.reciprocal(xsum[:, j:j + 1], xsum[:, j:j + 1]).then_inc(xp_v, 1)
                dve.wait_ge(xp_v, 2 * j + 1)
                v.tensor_scalar(prob[:, a, h, :], prob[:, a, h, :], xsum[:, j:j + 1], None, ALU.mult).then_inc(xp_v, 1)

            def output_lo(c):
                dve.wait_ge(xo_h, c + 1)
                tt(x_hl[:, 1, 2 * c:2 * c + 2, :].rearrange("p c s -> p (c s)"), mb(c)[:, :],
                   x_hl[:, 0, 2 * c:2 * c + 2, :].rearrange("p c s -> p (c s)").bitcast(f32), ALU.subtract).then_inc(xo_l, 1)

            m = first_half("V")
            lo_half(*half_of(m))
            beside(m)
            add_head_squares(0, xq_s, xq_r)
            add_head_squares(1, xq_s, xq_r)
            beside(m + 1)
            add_head_squares(2, xq_s, xq_r)
            add_head_squares(3, xq_s, xq_r)
            beside(m + 2)
            dve.wait_ge(xq_t, XH)
            v.tensor_scalar(xss, bank[6][:, 0:8], 1.0 / XD, EPS, ALU.mult, ALU.add).then_inc(xq_v, 1)
            dve.wait_ge(xq_a, 1)
            v.reciprocal(xss, xss).then_inc(xq_v, 1)
            dve.wait_ge(xq_v, 2)
            v.tensor_scalar(xss, xss, XD ** -0.5, None, ALU.mult).then_inc(xq_v, 1)
            dve.wait_ge(xq_v, 3)
            for p in range(XH):
                for j in (2 * p, 2 * p + 1):
                    dve.wait_ge(xl_t, j + 1)
                    v.reduce_max(xmx[:, j:j + 1], mb(j)[:, 0:SEQ], AX.X).then_inc(xl_v, 1)
                    dve.wait_ge(xl_v, 2 * j + 1)
                    v.scalar_tensor_tensor(xmx[:, j:j + 1], xmx[:, j:j + 1], -1.0, xss[:, j:j + 1], ALU.mult, ALU.mult).then_inc(xl_v, 1)
                beside(m + 3 + p)
                scale_prob(2 * p)
                scale_prob(2 * p + 1)
            beside(m + 7)
            beside(m + 8)
            for j, cs_ in ((9, (0, 1)), (10, (2, 3)), (11, (4,)), (12, ()), (13, (5,)), (14, ()), (15, (6,)), (16, (7,))):
                for c in cs_:
                    output_lo(c)
                beside(m + j)

            def sum_residual_squares(i, par):
                dve.wait_ge(x_sq, i + 1)
                if isinstance(i, int) and i == 0:
                    v.tensor_copy(sq_sum, tmp[:, par, 0:512]).then_inc(x_add, 1)
                else:
                    dve.wait_ge(x_add, i)
                    tt(sq_sum, sq_sum, tmp[:, par, 0:512], ALU.add).then_inc(x_add, 1)

            def xo_unit(i, par, hp):
                lo_half("XO", i, par, hp, 0)
                add_residual("XO", i - 1, 1 - par, hp if par else hp - 1)
                lo_half("XO", i, par, hp, 1)
                sum_residual_squares(i - 1, 1 - par)
            each_unit(dve, "XO", xo_unit, 1, 2)
            each_unit(dve, "XO", xo_unit, 2)
            m = first_half("UP")
            lo_half(*half_of(m))
            u = last_unit("XO")
            add_residual("XO", 7, u % 2, u // 2)
            for c in range(8):
                dve.wait_ge(n_hi, 13 + c)
                tt(x_hl[:, 1, 2 * c:2 * c + 2, :], xg[:, 2 * c:2 * c + 2, :], x_hl[:, 0, 2 * c:2 * c + 2, :].bitcast(f32),
                   ALU.subtract).then_inc(n_lo, 1)
            sum_residual_squares(7, u % 2)
            lo_half(*half_of(m + 1))
            mean(3)
            inverse(3)

            scaled = tmp[:, 1, 0:512]

            def scale_tokens(j, up):
                par, h0 = slot_of("UP", up)
                dve.wait_ge(half_used, j * 4 + (4 * h0 + 2 * par + 2))
                if up:
                    dve.wait_ge(f_c, j * 6 + 6)
                elif not isinstance(j, int) or j:
                    dve.wait_ge(f_g, j * 6)
                tt(scaled.rearrange("p (c s) -> p c s", c=2), bank[par][:, :].rearrange("p (c s) -> p c s", c=2),
                   bc(rstd[:, :].unsqueeze(1), [P, 2, SEQ]), ALU.mult).then_inc(dve_evac, 1)

            def taps(j, up):
                done = f_g if up else f_c
                dve.wait_ge(dve_evac, j * 2 + evacuated("UP", up)[1])
                if not up and (not isinstance(j, int) or j):
                    dve.wait_ge(f_p, j)
                n = 0
                for d in range(FFN_TAPS):
                    for x in range(2):
                        o = tmp[:, 0, (2 * up + x) * SEQ + d:(2 * up + x + 1) * SEQ]
                        b = scaled[:, x * SEQ:(x + 1) * SEQ - d]
                        w = vec3[:, FFN_TAPS - 1 - d, bass.ds(j * 2 + (up * FC + x), 1)]
                        if d:
                            dve.wait_ge(done, j * 6 + (n - 1))
                            ins = v.scalar_tensor_tensor(o, b, w, o, ALU.mult, ALU.add)
                        else:
                            ins = v.tensor_scalar(o, b, w, None, ALU.mult)
                        n += 1
                        ins.then_inc(done, 1)

            def product(j):
                dve.wait_ge(f_s, j + 1)
                if not isinstance(j, int) or j:
                    dve.wait_ge(f_l, j)
                dve.wait_ge(f_g, j * 6 + 6)
                tt(tmp[:, 1, 512:1024], tmp[:, 0, 0:512], tmp[:, 0, 512:1024], ALU.mult).then_inc(f_p, 1)

            def product_lo(j):
                dve.wait_ge(f_h, j + 1)
                two = lambda k: act_hl[:, k, bass.ds(j * 2, 2), :].rearrange("p c s -> p (c s)")
                tt(two(1), tmp[:, 1, 512:1024], two(0).bitcast(f32), ALU.subtract).then_inc(f_l, 1)

            (p0, h0), (p1, h1) = slot_of("UP", 0), slot_of("UP", 1)
            lo_half("UP", 1, p1, h1, 0)
            scale_tokens(0, 0)
            lo_half("UP", 1, p1, h1, 1)
            taps(0, 0)
            with dve.Fori(1, FC // 2) as j:
                lo_half("UP", 2 * j, p0, j + h0, 0)
                scale_tokens(j - 1, 1)
                lo_half("UP", 2 * j, p0, j + h0, 1)
                taps(j - 1, 1)
                product(j - 1)
                lo_half("UP", 2 * j + 1, p1, j + h1, 0)
                scale_tokens(j, 0)
                lo_half("UP", 2 * j + 1, p1, j + h1, 1)
                product_lo(j - 1)
                taps(j, 0)
            m = first_half("DN")
            lo_half(*half_of(m))
            scale_tokens(FC // 2 - 1, 1)
            taps(FC // 2 - 1, 1)
            product(FC // 2 - 1)
            lo_half(*half_of(m + 1))
            product_lo(FC // 2 - 1)

            for g in range(1, NDG):
                lo("DN", g, *slot_of("DN", g))
            dve.wait_ge(back, 32)
            dve.wait_ge(f_l, FC // 2)

            def finish(c, par):
                dve.wait_ge(half_used, c * (2 * NDG) + (2 * FIRST["DN"] + 2 * NDG))
                if not isinstance(c, int) or c >= 2:
                    dve.wait_ge(ot_t, c - 1)
                for x in range(2):
                    last = tt(tmp[:, par, x * SEQ:(x + 1) * SEQ], bank[par + 2 * x][:, 0:SEQ],
                              x_back[:, bass.ds(c * 2 + x, 1), :].rearrange("p c s -> p (c s)"), ALU.add)
                last.then_inc(dve_evac, 1)

            def down_pair(c, par):
                for g in range(NDG):
                    p, h0 = slot_of("DN", g)
                    lo("DN", g, p, c * (NDG // 2) + h0)
                    if g == 0:
                        finish(c - 1, 1 - par)

            down_pair(1, 1)
            down_pair(2, 0)
            down_pair(3, 1)
            with dve.Fori(2, 4) as r:
                down_pair(r * 2, 0)
                down_pair(r * 2 + 1, 1)
            finish(7, 1)

        @block.tensor
        def _(pe):
            mm = nc.tensor.matmul

            def three(o, w, x, start, stop):
                mm(o, w[0], x[0], start=start, stop=False)
                mm(o, w[0], x[1], start=False, stop=False)
                return mm(o, w[1], x[0], start=False, stop=stop)

            def wait_bank(name, i):
                if isinstance(i, int) and i < 2:
                    u = FIRST[name] + i - 2
                    if u < 0:
                        return
                    before = phase_of(u)
                    e, n = evacuated(before, u - FIRST[before])
                    pe.wait_ge(evac[e], n)
                else:
                    e, n = evacuated(name, 0)
                    pe.wait_ge(evac[e], i + (n - 2))

            def half_unit(name, i, par, hp, half, acts, ready=None):
                kind = kind_of[name]
                pe.wait_ge(lo_ready, hp * 4 + (2 * par + half + 1))
                if kind == TM_:
                    for k in range(KC // 2):
                        kk = half * (KC // 2) + k
                        w = [t[:, half, k * CW:(k + 1) * CW] for t in (w_hi, w_lo)]
                        for a in range(TT):
                            x = [acts[:, j, kk, a * P:(a + 1) * P] for j in range(2)]
                            last = three(bank[par + 2 * a][:, 0:CW], x, w, kk == 0, kk == KC - 1)
                else:
                    cuts = (0, GH, GH + MH, KC) if kind == BR else (0, KC)
                    for k in range(KC):
                        if ready and k % ready[2] == 0:
                            pe.wait_ge(ready[0], ready[1] + k // ready[2] + 1)
                        g = sum(k >= c for c in cuts) - 1
                        w = [t[:, half, k * P:(k + 1) * P] for t in (w_hi, w_lo)]
                        last = three(bank[par + 2 * g][:, half * SEQ:(half + 1) * SEQ], w, [acts[:, j, k, :] for j in range(2)],
                                     k == cuts[g], k + 1 == cuts[g + 1])
                last.then_inc(half_used, 1)

            def product_half(m, acts=x_hl, ready=None):
                name, i, par, hp, half = half_of(m)
                if half == 0:
                    wait_bank(name, i)
                half_unit(name, i, par, hp, half, acts, ready)

            def project(name, acts, start=0, stop=None):
                def unit(i, par, hp):
                    wait_bank(name, i)
                    for half in range(2):
                        half_unit(name, i, par, hp, half, acts)
                stop = COUNT[name] if stop is None else stop
                if start < 2:
                    each_unit(pe, name, unit, start, min(2, stop))
                each_unit(pe, name, unit, max(2, start), stop)

            def transposes(k, src, gs):
                for g in gs:
                    if g >= 4:
                        pe.wait_ge(tin_d if g % 2 else tin_e, 4 * k + g // 2 - 1)
                    for c in range(4):
                        cc = 4 * (g // 2) + c
                        last = nc.tensor.transpose(mb(g)[:, c * P:(c + 1) * P], src[:, g % 2, cc * P:(cc + 1) * P], ident[:, :])
                    last.then_inc(tin_t, 1)

            def first_squares(c):
                pe.wait_ge(n_sq, c + 1)
                for j in range(4):
                    last = mm(bank[3][:, 0:SEQ], ones[:, :], tmp[:, c % 2, j * SEQ:(j + 1) * SEQ], start=c + j == 0, stop=c + j == 6)
                last.then_inc(n_ss, 1)

            def norm_beside(k, m, acts):
                product_half(m, acts)
                product_half(m + 1, acts)
                product_half(m + 2, acts)
                pe.wait_ge(n_add, 3 * k)
                for j in range(4):
                    last = mm(bank[3][:, 0:SEQ], ones[:, :], tmp[:, 0, j * SEQ:(j + 1) * SEQ], start=j == 0, stop=j == 3)
                last.then_inc(n_ss, 1)
                for j in range(3, 8):
                    product_half(m + j, acts)

            pe.wait_ge(const_in, 16)
            pe.wait_ge(x_in[0], 16)
            transposes(0, x_tm, range(4))
            pe.wait_ge(x_in[1], 16)
            pe.wait_ge(set_up, 1)
            transposes(0, x_tm, (4, 5))
            first_squares(0)
            transposes(0, x_tm, (6, 7))
            first_squares(1)
            first_squares(2)
            pe.wait_ge(vec_in, 16 * 14)
            pe.wait_ge(tin_e, 3)
            at = 0
            for i, k in ((0, 74), (1, 72), (2, 88), (3, 88), (4, 88)):
                last = nc.tensor.transpose(bank[4][:, at:at + k], vecs[0:k, i, :], ident[0:k, 0:k])
                at += k
            last.then_inc(vec_t, 1)
            first_squares(3)
            product_half(0, x_hl, (n_lo, 0, 4))
            product_half(1)
            product_half(2)
            pe.wait_ge(gw_l, 1)
            pe.wait_ge(set_up, 2)
            for k in range(KC):
                last = three(bank[4][:, 0:SEQ], [t[:, k, :] for t in (gw_hi, gw_lo)], [x_hl[:, j, k, :] for j in range(2)],
                             k == 0, k == KC - 1)
            last.then_inc(row_mm, 1)
            for m in range(3, 14):
                product_half(m)
            pe.wait_ge(row_v, ROW_V)
            for a in range(TT):
                nc.tensor.transpose(bank[5][:, a * P:(a + 1) * P], rt[:, a * P:(a + 1) * P], ident[:, :])
                last = nc.tensor.transpose(bank[5][:, SEQ + a * MH:SEQ + (a + 1) * MH], rt2[:, a * P:(a + 1) * P], ident[0:MH, 0:MH])
            last.then_inc(row_t, 1)
            for m in range(14, first_half("GA")):
                product_half(m)

            def tm_transposes(gs):
                for g in gs:
                    pe.wait_ge(cs, (2 * g + 1) // 6 + 1)
                    if g >= 6:
                        pe.wait_ge(tm_ed if g % 2 else tm_ea, (g - 6) // 2 + 1)
                    for c in range(2):
                        for a in range(TT):
                            last = nc.tensor.transpose(mb6(g)[:, (2 * c + a) * P:(2 * c + a + 1) * P],
                                                       conv[:, 2 * g + c, a * P:(a + 1) * P], ident[:, :])
                    last.then_inc(tm_t, 1)

            def spread(b, h, row):
                n = row.shape[0]
                return mm(b, ident[0:n, h:h + 1].to_broadcast([n, P]), row, start=True, stop=True)

            def chunk_pairs(sem_, banks, rhs):
                for g in range(3):
                    for n in range(4 * g, 4 * g + 4):
                        a, h = n // GH, n % GH
                        last = mm(banks[g][:, n % 4 * P:n % 4 * P + P], conv[:, GH + h, a * P:(a + 1) * P],
                                  conv[:, rhs + h, a * P:(a + 1) * P], start=True, stop=True)
                    last.then_inc(sem_, 1)

            def group(o, lhs, rhs, ns):
                for i, n in enumerate(ns):
                    last = mm(o[:, i * P:(i + 1) * P], lhs(n), rhs(n), start=True, stop=True)
                return last

            m = first_half("GA")
            pe.wait_ge(col_e, 2)
            tm_transposes(range(3))
            product_half(m)
            tm_transposes(range(3, 6))
            product_half(m + 1)
            tm_transposes(range(6, 9))
            pe.wait_ge(tm_ed, 3)
            pe.wait_ge(tm_ea, 3)
            for j in range(3):
                for x in range(2):
                    last = spread(mb6(j + 3)[:, x * SEQ:(x + 1) * SEQ], 2 * j + x, g_row[:, :])
                last.then_inc(dec_t, 1)
            product_half(m + 2)
            product_half(m + 3)
            pe.wait_ge(l2_v, 8)
            pe.wait_ge(tm_ea, 5)
            pe.wait_ge(tm_ed, 4)
            for g in range(6):
                if g == 3:
                    pe.wait_ge(dec_v, 12)
                for c in range(2):
                    for a in range(TT):
                        last = nc.tensor.transpose(mb6(g)[:, (2 * c + a) * P:(2 * c + a + 1) * P], tm[:, a, 2 * g + c, :], ident[:, :])
                last.then_inc(qk_t, 1)
            product_half(m + 4)
            pe.wait_ge(qk_e, 6)
            chunk_pairs(kk_t, bank[2:5], GH)
            product_half(m + 5)
            product_half(m + 6)
            m += 7
            for l in range(7):
                pe.wait_ge(c_v, 2 + l if l else 1)
                pe.wait_ge(l_v, 12)
                if l:
                    pe.wait_ge(d_e, 6 * l - 3)
                for g in range(3):
                    ns = range(4 * g, 4 * g + 4)
                    if l:
                        last = group(bank[5 + g], lambda n: S_C[:, n, :], lambda n: S_U[:, n, :], ns)
                    else:
                        for n in ns:
                            last = nc.tensor.transpose(bank[5 + g][:, n % 4 * P:n % 4 * P + P], S_C[:, n, :], ident[:, :])
                    last.then_inc(z_t, 1)
                product_half(m)
                for g in range(3 if l else 0):
                    pe.wait_ge(z_e, 3 * l - 3 + (1, 2, 3)[g])
                    for x, (lhs, rhs) in ((0, (S_Z, S_T)), (1, (S_T, S_Z)))[l // 6:]:
                        for n in range(4 * g, 4 * g + 4):
                            last = mm(bank[2 + 2 * g + x][:, n % 4 * 64:n % 4 * 64 + 64].rearrange("p (b w) -> p b w", w=1 << l),
                                      lhs[:, n, :], level_columns(rhs[:, n:n + 1, :], l, x)[:, 0], start=True, stop=True)
                        last.then_inc(d_t, 1)
                if l:
                    product_half(m + 1)
                m += 2 if l else 1

            two_groups = ((0, range(0, 4)), (1, range(4, 6)))
            pe.wait_ge(d_e, 36)
            pe.wait_ge(kv_v, 4)
            for g, hs in two_groups:
                group(bank[2 + g], lambda h: S_U[:, h, :], lambda h: tm[:, 0, 12 + h, :], hs).then_inc(u_t, 1)
            for g, hs in two_groups:
                group(bank[4 + g], lambda h: tm[:, 1, 6 + h, :], lambda h: S_U[:, 6 + h, :], hs).then_inc(w_t, 1)
            product_half(m)
            pe.wait_ge(u_e, 2)
            for g, hs in two_groups:
                group(bank[6 + g], lambda h: tm[:, 0, 6 + h, :], lambda h: S_C[:, h, :], hs).then_inc(s_t, 1)
            for g, hs in two_groups:
                for i, h in enumerate(hs):
                    last = nc.tensor.transpose(bank[2 + g][:, i * P:(i + 1) * P], tm[:, 1, h, :], ident[:, :])
                last.then_inc(qd_t, 1)
            product_half(m + 1)
            pe.wait_ge(w_e, 2)
            pe.wait_ge(s_e, 2)
            pe.wait_ge(qd_e, 2)
            for j in range(3):
                for x in range(2):
                    last = spread(bank[4 + j][:, x * SEQ:(x + 1) * SEQ], 2 * j + x, g_row[:, :])
                last.then_inc(a_t, 1)
            chunk_pairs(a_t, (bank[7], bank[2], bank[3]), 0)
            product_half(m + 2)
            pe.wait_ge(a_v, 8)
            for g, hs in two_groups:
                for i, h in enumerate(hs):
                    o = bank[4 + g][:, i * P:(i + 1) * P]
                    mm(o, S_U[:, 6 + h, :], tm[:, 1, 12 + h, :], start=True, stop=False)
                    last = mm(o, S_Z[:, h, :], S_Z[:, 6 + h, :], start=False, stop=True)
                last.then_inc(vn_t, 1)
            product_half(m + 3)
            m += 1
            product_half(m + 3)
            pe.wait_ge(a_v, 16)
            pe.wait_ge(vn_e, 2)
            for g in range(3):
                for n in range(4 * g, 4 * g + 4):
                    o = bank[(6, 7, 2)[g]][:, n % 4 * P:n % 4 * P + P]
                    if n >= GH:
                        mm(o, tm[:, 0, n - GH, :], S_Z[:, n, :], start=True, stop=False)
                    last = mm(o, S_L[:, n, :], S_C[:, n, :], start=n < GH, stop=True)
                last.then_inc(o_t, 1)
            product_half(m + 4)
            product_half(m + 5)

            def to_features(b, j, src, sem_):
                for x in range(2):
                    for a in range(TT):
                        last = nc.tensor.transpose(b[:, x * SEQ + a * P:x * SEQ + (a + 1) * P], src(2 * j + x, a), ident[:, :])
                last.then_inc(sem_, 1)

            pe.wait_ge(yn_v, 5)
            for j in range(3):
                to_features(bank[3 + j], j, lambda h, a: S_T[:, a * GH + h, :], y_t)
            product_half(m + 6)

            for name in ("BQK", "BV", "BO"):
                project(name, x_hl)

            def scores(b, k, q):
                mm(b[:, 0:SEQ], k[:, 0:P], q, start=True, stop=True)
                return mm(b[:, SEQ:384], k[:, P:SEQ], q[:, P:SEQ], start=True, stop=True)

            def ml_scores(h):
                spread(bank[4 + 2 * ML_PAIR[h]][:, 0:SEQ], h, m_row[:, :])
                scores(bank[5 + 2 * ML_PAIR[h]], qk_b[:, MH + h, :], qk_b[:, h, :]).then_inc(ml_s, 1)

            def ml_numerator(h):
                b = bank[4 + h]
                mm(b[:, 0:129], ml_x[:, h, 0:P], v_b[:, 0, h, :], start=True, stop=True)
                mm(b[:, 129:258], ml_x[:, h, P:SEQ], v_b[:, 0, h, :], start=True, stop=False)
                mm(b[:, 129:258], ml_x[:, h, SEQ:384], v_b[:, 1, h, :], start=False, stop=True).then_inc(ml_n, 1)

            m = first_half("CQK")
            pe.wait_ge(act_evac, evacuated("BV", 1)[1])
            pe.wait_ge(set_up, 3)
            pe.wait_ge(y_e, 3)
            product_half(m)
            ml_scores(0)
            ml_scores(1)
            product_half(m + 1)
            product_half(m + 2)
            pe.wait_ge(ml_w, 2)
            ml_numerator(0)
            ml_numerator(1)
            ml_scores(2)
            product_half(m + 3)
            product_half(m + 4)
            pe.wait_ge(ml_ne, 2)
            ml_scores(3)
            product_half(m + 5)
            pe.wait_ge(ml_w, 4)
            ml_numerator(2)
            ml_numerator(3)
            for j in (6, 7, 8):
                product_half(m + j)
            pe.wait_ge(ml_h, 9)
            for j in range(2):
                to_features(bank[4 + j], j, lambda h, a: num[:, a, h, 0:DK], ml_t)
            for j in (9, 10, 11):
                product_half(m + j)
            project("CV", x_hl)

            m = first_half("GB")
            pe.wait_ge(ml_y, 2)
            for h in range(SH):
                if h == 4:
                    pe.wait_ge(act_evac, evacuated("CV", 2)[1])
                scores(mb6(h + 2), qk_c[:, SH + h, :], qk_c[:, h, :]).then_inc(sb_t, 1)
            for j in range(4):
                product_half(m + j)
            for h in range(SH):
                pe.wait_ge(sb_sp, h + 1)
                b = mb6(h + 2)
                mm(b[:, 0:SEQ], later[:, :], sb_s[:, h, 0:SEQ], start=True, stop=False)
                mm(b[:, P:SEQ], ones[:, :], sb_s[:, h, SEQ:384], start=False, stop=True)
                mm(b[:, SEQ:384], later[:, :], sb_s[:, h, SEQ:384], start=True, stop=True).then_inc(sb_r, 1)
            product_half(m + 4)
            product_half(m + 5)
            for h in range(SH):
                pe.wait_ge(sb_e, h + 1)
                b = mb6(h + 2)
                mm(b[:, 0:SEQ], v_c[:, 0, h * DK:(h + 1) * DK], sb_z[:, h, 0:SEQ], start=True, stop=False)
                mm(b[:, P:SEQ], v_c[:, 1, h * DK:(h + 1) * DK], sb_z[:, h, SEQ:384], start=False, stop=True).then_inc(sb_o, 1)
            product_half(m + 6)
            product_half(m + 7)

            project("GC", x_hl)
            pe.wait_ge(y_lo, 4)
            project("BR", y_hl)
            m = first_half("WO")
            product_half(m, x_hl, (m_lo, 0, 2))
            product_half(m + 1, x_hl)
            project("WO", x_hl, 1, 3)
            m = first_half("WO", 3)
            pe.wait_ge(mem_in, 16)
            transposes(1, mem_tm, range(4))
            product_half(m, x_hl)
            transposes(1, mem_tm, range(4, 8))
            product_half(m + 1, x_hl)
            norm_beside(1, m + 2, x_hl)
            m = first_half("K")
            product_half(m, mem_hl, (n_lo, 4, 4))
            norm_beside(2, m + 1, mem_hl)
            product_half(m + 9, mem_hl)
            project("K", mem_hl, 5)
            m = first_half("Q")
            pe.wait_ge(n_lo, 12)
            for h in range(XH):
                product_half(m + 2 * h)
                product_half(m + 2 * h + 1)
                pe.wait_ge(xk_r, 2 * h + 2)
                if h >= 2:
                    pe.wait_ge(xk_v, 3 * (h - 2) + 1)
                mm(bank[6 + h % 2][:, 0:SEQ], ones[:, :], tmp[:, h % 2, 0:SEQ], start=True, stop=True).then_inc(xk_t, 1)
            project("Q", x_hl, 4)
            def query_sums(h):
                pe.wait_ge(xq_r, 2 * h + 2)
                for a in range(TT):
                    last = mm(bank[6][:, 2 * h + a:2 * h + a + 1], tmp[:, h % 2, a * P:(a + 1) * P], ones[:, 0:1], start=True, stop=True)
                last.then_inc(xq_t, 1)

            def logits(j):
                h, a = j // 2, j % 2
                for c in range(XC):
                    last = mm(mb(j)[:, 0:SEQ], qT[:, 4 * h + c, a * P:(a + 1) * P], kT[:, 4 * h + c, :], start=c == 0, stop=c == XC - 1)
                last.then_inc(xl_t, 1)

            def prob_transposes(h):
                pe.wait_ge(xp_v, 4 * h + 4)
                for mk in range(TT):
                    for a in range(TT):
                        last = nc.tensor.transpose(mb(h)[:, mk * SEQ + a * P:mk * SEQ + (a + 1) * P],
                                                   prob[:, a, h, mk * P:(mk + 1) * P], ident[:, :])
                last.then_inc(xp_t, 1)

            def output(c):
                h = c // 2
                pe.wait_ge(act_evac, evacuated("V", c)[1])
                if c >= 4:
                    pe.wait_ge(xo_l, c - 3)
                for x in range(2):
                    f = 2 * c + x
                    for mk in range(TT):
                        last = mm(mb(c)[:, x * SEQ:(x + 1) * SEQ], v_tm[:, mk, f * P:(f + 1) * P], probT[:, mk, h, :],
                                  start=mk == 0, stop=mk == TT - 1)
                last.then_inc(xo_t, 1)

            m = first_half("V")
            pe.wait_ge(xk_v, 3 * XH)
            product_half(m, mem_hl)
            product_half(m + 1, mem_hl)
            query_sums(0)
            query_sums(1)
            product_half(m + 2, mem_hl)
            query_sums(2)
            query_sums(3)
            for p in range(XH):
                if p == 1:
                    pe.wait_ge(xq_v, 1)
                elif p > 1:
                    pe.wait_ge(xl_a, 2 * p - 2)
                logits(2 * p)
                logits(2 * p + 1)
                product_half(m + 3 + p, mem_hl)
            for p in range(2):
                pe.wait_ge(xl_a, 6 + 2 * p)
                prob_transposes(2 * p)
                prob_transposes(2 * p + 1)
                product_half(m + 7 + p, mem_hl)
            pe.wait_ge(xp_e, 2)
            output(0)
            output(1)
            product_half(m + 9, mem_hl)
            pe.wait_ge(xp_e, 4)
            output(2)
            output(3)
            product_half(m + 10, mem_hl)
            output(4)
            product_half(m + 11, mem_hl)
            product_half(m + 12, mem_hl)
            output(5)
            product_half(m + 13, mem_hl)
            product_half(m + 14, mem_hl)
            output(6)
            product_half(m + 15, mem_hl)
            output(7)
            m = first_half("XO")
            product_half(m, x_hl, (xo_l, 0, 2))
            product_half(m + 1)

            project("XO", x_hl, 1)
            m = first_half("UP")
            product_half(m, x_hl, (n_lo, 12, 2))
            pe.wait_ge(x_add, COUNT["XO"])
            for x in range(2):
                last = mm(bank[3][:, 0:SEQ], ones[:, :], sq_sum[:, x * SEQ:(x + 1) * SEQ], start=x == 0, stop=x == 1)
            last.then_inc(x_ss, 1)
            product_half(m + 1)
            project("UP", x_hl, 1)
            pe.wait_ge(f_l, FC // 2 - 1)

            def down_pair(c, par):
                if isinstance(c, int) and c < 2:
                    pe.wait_ge(dve_evac, evacuated("UP", COUNT["UP"] - 1)[1])
                else:
                    pe.wait_ge(dve_evac, c + (evacuated("DN", 0)[1] - 2))
                for g in range(NDG):
                    for half in range(2):
                        pe.wait_ge(lo_ready, c * (2 * NDG) + (2 * FIRST["DN"] + 2 * g + half + 1))
                        for k in range(DG):
                            if isinstance(c, int) and c == 0 and g * DG + k == FC - 2:
                                pe.wait_ge(f_l, FC // 2)
                            w = [t[:, half, k * P:(k + 1) * P] for t in (w_hi, w_lo)]
                            x = [act_hl[:, j, g * DG + k, :] for j in range(2)]
                            last = three(bank[par + 2 * half][:, 0:SEQ], w, x, g + k == 0, g * DG + k == FC - 1)
                        last.then_inc(half_used, 1)
                    if g == 1 and not (isinstance(c, int) and c == 0):
                        finished(c - 1, 1 - par)

            def finished(c, par):
                pe.wait_ge(dve_evac, c + evacuated("DN", 0)[1])
                if not isinstance(c, int) or c >= 1:
                    pe.wait_ge(ot_e, c)
                for a in range(TT):
                    for x in range(2):
                        last = nc.tensor.transpose(bank[6][:, (2 * a + x) * P:(2 * a + x + 1) * P],
                                                   tmp[:, par, x * SEQ + a * P:x * SEQ + (a + 1) * P], ident[:, :])
                last.then_inc(ot_t, 1)

            down_pair(0, 0)
            down_pair(1, 1)
            with pe.Fori(1, 4) as r:
                down_pair(r * 2, 0)
                down_pair(r * 2 + 1, 1)
            finished(7, 1)


ROW_V = 20
ML_PAIR = (0, 1, 1, 0)

INPUTS = ['x', 'mem', 'norm_mix', 'w_in', 'gdn_conv', 'gdn_a_log', 'gdn_dt_bias', 'gdn_norm', 'ml_gate_bias', 'ml_norm', 'w_br',
          'w_out', 'norm_xa', 'norm_mem', 'xa_wq', 'xa_wkv', 'xa_wo', 'xa_qnorm', 'xa_knorm', 'norm_ffn', 'ffn_up', 'ffn_conv',
          'ffn_down']


def kernel(**inputs):
    import concourse.bacc as bacc
    from concourse.bass_utils import run_bass_kernel_spmd

    nc = bacc.Bacc("TRN2", target_bir_lowering=False, num_devices=1)
    arrays = {f"in_{n}": np.ascontiguousarray(inputs[n]) for n in INPUTS}
    arrays["in_shape_masks"] = shape_masks()
    T = {n[3:]: nc.dram_tensor(n, a.shape, mybir.dt.from_np(a.dtype), kind="ExternalInput").ap() for n, a in arrays.items()}
    out = nc.dram_tensor("out", (1, SEQ, D), mybir.dt.float32, kind="ExternalOutput").ap()
    build_program(nc, T, out)
    result = run_bass_kernel_spmd(nc, [arrays], core_ids=[0])
    return result.results[0]["out"]
```
